# Optimizing a Trainium2 kernel written in Bass

```python
import math
import jax
import jax.numpy as jnp
from jax import lax
import numpy as np

D_MODEL = 2048
BATCH = 1
SEQ = 512
DEPTH = 2

N_MEM = 256
Q_BLOCK = 128
RMS_EPS = 1e-6
NEG_INF = -1e30
MAX_POS_OFFSET = 1024

S5_WIDTH = 1024
S5_GROUP = 16
S5_GROUPS = S5_WIDTH // S5_GROUP
S5_STATE = 64
S5_DT_MIN = 1e-3
S5_DT_MAX = 1e-1

FOX_HEADS = 8
FOX_HEAD_DIM = 128
FOX_WIDTH = FOX_HEADS * FOX_HEAD_DIM
FOX_FORGET_BIAS = 2.0

MEM_HEADS = 4
MEM_HEAD_DIM = 128
MEM_WIDTH = MEM_HEADS * MEM_HEAD_DIM

MLA_HEADS = 8
MLA_Q_RANK = 512
MLA_KV_RANK = 512
MLA_NOPE = 128
MLA_ROPE = 64
MLA_V = 128
MLA_WIDTH = MLA_HEADS * MLA_V
ROPE_THETA = 10000.0

NSA_HEADS = 8
NSA_KV_GROUPS = 2
NSA_HEAD_DIM = 128
NSA_WIDTH = NSA_HEADS * NSA_HEAD_DIM
NSA_KV = NSA_KV_GROUPS * NSA_HEAD_DIM
NSA_CMP_LEN = 32
NSA_CMP_STRIDE = 16
NSA_CMP_HIDDEN = 256
NSA_SLC_BLOCK = 64
NSA_SLC_TOPK = 16
NSA_WINDOW = 512
FORCE_SCORE = 1e6

T5_BUCKETS = 32
T5_MAX_DIST = 1024

N_EVEN = (DEPTH + 1) // 2
N_ODD = DEPTH // 2
EVEN_SPLITS = (S5_WIDTH, S5_WIDTH, FOX_WIDTH, FOX_WIDTH, FOX_WIDTH, FOX_HEADS, FOX_WIDTH, MEM_WIDTH, MEM_WIDTH)
ODD_SPLITS = (MLA_Q_RANK, MLA_KV_RANK, MLA_ROPE, MLA_WIDTH, NSA_WIDTH, NSA_KV, NSA_KV, NSA_KV, NSA_KV, NSA_KV, NSA_KV, 3 * NSA_HEADS, NSA_WIDTH, MEM_WIDTH, MEM_WIDTH)
EVEN_IN = sum(EVEN_SPLITS)
ODD_IN = sum(ODD_SPLITS)
MIX_WIDTH = S5_WIDTH + FOX_WIDTH + MEM_WIDTH

kernel_name = 'hybrid_s5_fox_mla_nsa_trunk'

def rms_norm(x, g):
    xf = x.astype(jnp.float32)
    y = xf * lax.rsqrt(jnp.mean(xf * xf, axis=-1, keepdims=True) + RMS_EPS)
    return (y * g.astype(jnp.float32)).astype(x.dtype)

def split_cols(h, sizes):
    return jnp.split(h, np.cumsum(sizes)[:-1].tolist(), axis=-1)

def rope(x, positions):
    half = x.shape[-1] // 2
    inv_freq = ROPE_THETA ** (-jnp.arange(half, dtype=jnp.float32) / half)
    ang = positions.astype(jnp.float32)[..., None] * inv_freq
    cos = jnp.cos(ang)[:, :, None, :]
    sin = jnp.sin(ang)[:, :, None, :]
    x1 = x[..., :half].astype(jnp.float32)
    x2 = x[..., half:].astype(jnp.float32)
    return jnp.concatenate([x1 * cos - x2 * sin, x1 * sin + x2 * cos], axis=-1).astype(x.dtype)

def t5_bucket(dist):
    n = jnp.maximum(dist, 0)
    max_exact = T5_BUCKETS // 2
    log_ratio = jnp.log(jnp.maximum(n, 1).astype(jnp.float32) / max_exact) / math.log(T5_MAX_DIST / max_exact)
    large = jnp.minimum(max_exact + (log_ratio * (T5_BUCKETS - max_exact)).astype(jnp.int32), T5_BUCKETS - 1)
    return jnp.where(n < max_exact, n, large)

def causal_block_attention(q, k, v, scale, log_decay=None):
    B_, L, H, _ = q.shape
    nblk = L // Q_BLOCK
    k_idx = jnp.arange(L)
    qb = q.reshape(B_, nblk, Q_BLOCK, H, -1).swapaxes(0, 1)
    cb = None if log_decay is None else log_decay.reshape(B_, nblk, Q_BLOCK, H).swapaxes(0, 1)
    ck = None if log_decay is None else log_decay.transpose(0, 2, 1)[:, :, None, :]

    def one_block(args):
        qi, ci, blk = args
        s = jnp.einsum('bqhd,bkhd->bhqk', qi, k, preferred_element_type=jnp.float32) * scale
        if ci is not None:
            s = s + ci.transpose(0, 2, 1)[..., None] - ck
        t = blk * Q_BLOCK + jnp.arange(Q_BLOCK)
        s = jnp.where(k_idx[None, :] <= t[:, None], s, NEG_INF)
        p = jax.nn.softmax(s, axis=-1)
        return jnp.einsum('bhqk,bkhd->bqhd', p.astype(v.dtype), v)

    o = lax.map(one_block, (qb, cb, jnp.arange(nblk)))
    return o.swapaxes(0, 1).reshape(B_, L, H, v.shape[-1])

def memory_attention(q, mem_kv):
    B_, L, _ = q.shape
    M = mem_kv.shape[1]
    qh = q.reshape(B_, L, MEM_HEADS, MEM_HEAD_DIM)
    km, vm = jnp.split(mem_kv, 2, axis=-1)
    km = km.reshape(B_, M, MEM_HEADS, MEM_HEAD_DIM)
    vm = vm.reshape(B_, M, MEM_HEADS, MEM_HEAD_DIM)
    s = jnp.einsum('blhd,bmhd->bhlm', qh, km, preferred_element_type=jnp.float32) * MEM_HEAD_DIM ** -0.5
    p = jax.nn.softmax(s, axis=-1)
    return jnp.einsum('bhlm,bmhd->blhd', p.astype(vm.dtype), vm).reshape(B_, L, MEM_WIDTH)

def s5_mixer(u, lam_re, lam_im, log_dt, b_re, b_im, c_re, c_im, d_skip, w_glu):
    f32 = jnp.float32
    B_, L, _ = u.shape
    uf = u.astype(f32).reshape(B_, L, S5_GROUPS, S5_GROUP)
    dt = jnp.exp(log_dt.astype(f32))[:, None]
    lr = lam_re.astype(f32)
    li = lam_im.astype(f32)
    mag = jnp.exp(lr * dt)
    ab_re = mag * jnp.cos(li * dt)
    ab_im = mag * jnp.sin(li * dt)
    den = lr * lr + li * li
    nr = ab_re - 1.0
    f_re = (nr * lr + ab_im * li) / den
    f_im = (ab_im * lr - nr * li) / den
    br = b_re.astype(f32)
    bim = b_im.astype(f32)
    bb_re = f_re[..., None] * br - f_im[..., None] * bim
    bb_im = f_re[..., None] * bim + f_im[..., None] * br
    bu_re = jnp.einsum('gpc,blgc->blgp', bb_re, uf)
    bu_im = jnp.einsum('gpc,blgc->blgp', bb_im, uf)
    a_re = jnp.broadcast_to(ab_re, bu_re.shape)
    a_im = jnp.broadcast_to(ab_im, bu_im.shape)

    def combine(e1, e2):
        a1r, a1i, b1r, b1i = e1
        a2r, a2i, b2r, b2i = e2
        return (a2r * a1r - a2i * a1i, a2r * a1i + a2i * a1r,
                a2r * b1r - a2i * b1i + b2r, a2r * b1i + a2i * b1r + b2i)

    _, _, xr, xi = lax.associative_scan(combine, (a_re, a_im, bu_re, bu_im), axis=1)
    y = (jnp.einsum('gcp,blgp->blgc', c_re.astype(f32), xr)
         - jnp.einsum('gcp,blgp->blgc', c_im.astype(f32), xi)
         + d_skip.astype(f32) * uf).reshape(B_, L, S5_WIDTH)
    z = jax.nn.gelu(y)
    z = z * jax.nn.sigmoid(z @ w_glu.astype(f32))
    return z.astype(u.dtype)

def mla_attention(c_q, c_kv, k_rope, positions, g_cq, g_ckv, w_uq, w_ukv):
    B_, L, _ = c_q.shape
    q = (rms_norm(c_q, g_cq) @ w_uq).reshape(B_, L, MLA_HEADS, MLA_NOPE + MLA_ROPE)
    q = jnp.concatenate([q[..., :MLA_NOPE], rope(q[..., MLA_NOPE:], positions)], axis=-1)
    kv = (rms_norm(c_kv, g_ckv) @ w_ukv).reshape(B_, L, MLA_HEADS, MLA_NOPE + MLA_V)
    kr = rope(k_rope[:, :, None, :], positions)
    k = jnp.concatenate([kv[..., :MLA_NOPE], jnp.broadcast_to(kr, (B_, L, MLA_HEADS, MLA_ROPE))], axis=-1)
    v = kv[..., MLA_NOPE:]
    o = causal_block_attention(q, k, v, (MLA_NOPE + MLA_ROPE) ** -0.5)
    return o.reshape(B_, L, MLA_WIDTH)

def nsa_attention(q, k_cmp, v_cmp, k_slc, v_slc, k_win, v_win, gate_logits, positions, t5_table, cmp_pe, cmp_w1, cmp_w2):
    f32 = jnp.float32
    B_, L, _ = q.shape
    G = NSA_KV_GROUPS
    R = NSA_HEADS // NSA_KV_GROUPS
    dh = NSA_HEAD_DIM
    scale = dh ** -0.5
    nblk = L // Q_BLOCK
    qh = q.reshape(B_, L, G, R, dh)
    k_cmp, v_cmp, k_slc, v_slc, k_win, v_win = [t.reshape(B_, L, G, dh) for t in (k_cmp, v_cmp, k_slc, v_slc, k_win, v_win)]
    gates = jax.nn.sigmoid(gate_logits.astype(f32)).reshape(B_, L, G, R, 3)

    n_cmp = (L - NSA_CMP_LEN) // NSA_CMP_STRIDE + 1
    cmp_idx = np.arange(n_cmp)[:, None] * NSA_CMP_STRIDE + np.arange(NSA_CMP_LEN)[None, :]

    def compress(t, pe, w1, w2):
        blocks = t[:, cmp_idx] + pe[None, None, :, None, :]
        blocks = blocks.transpose(0, 1, 3, 2, 4).reshape(B_, n_cmp, G, NSA_CMP_LEN * dh)
        return jax.nn.gelu(blocks @ w1) @ w2

    kc = compress(k_cmp, cmp_pe[0], cmp_w1[0], cmp_w2[0])
    vc = compress(v_cmp, cmp_pe[1], cmp_w1[1], cmp_w2[1])
    cmp_end = cmp_idx[:, -1]
    cmp_end_j = jnp.asarray(cmp_end)
    pos_cmp = positions[:, cmp_end]

    n_slc = L // NSA_SLC_BLOCK
    n_top = min(NSA_SLC_TOPK, n_slc)
    cs = np.arange(n_cmp) * NSA_CMP_STRIDE
    ss = np.arange(n_slc) * NSA_SLC_BLOCK
    ov = np.clip(np.minimum(cs[:, None] + NSA_CMP_LEN, ss[None, :] + NSA_SLC_BLOCK) - np.maximum(cs[:, None], ss[None, :]), 0, None) / NSA_CMP_LEN
    overlap = jnp.asarray(ov, jnp.float32)
    k_slc_g = k_slc.transpose(0, 2, 1, 3)
    v_slc_g = v_slc.transpose(0, 2, 1, 3)

    k_win_p = jnp.pad(k_win, ((0, 0), (NSA_WINDOW, 0), (0, 0), (0, 0)))
    v_win_p = jnp.pad(v_win, ((0, 0), (NSA_WINDOW, 0), (0, 0), (0, 0)))
    pos_p = jnp.pad(positions, ((0, 0), (NSA_WINDOW, 0)))

    table_gr = t5_table.reshape(T5_BUCKETS, G, R)
    bi = jnp.arange(B_)[:, None, None, None]
    gi = jnp.arange(G)[None, :, None, None]

    def head_bias(dist):
        return table_gr[t5_bucket(dist)].transpose(0, 3, 4, 1, 2).astype(f32)

    def one_block(args):
        qi, gq, pos_q, blk = args
        t = blk * Q_BLOCK + jnp.arange(Q_BLOCK)
        s = jnp.einsum('bqgrd,bngd->bgrqn', qi, kc, preferred_element_type=f32) * scale
        s = s + head_bias(pos_q[:, :, None] - pos_cmp[:, None, :])
        valid = cmp_end_j[None, :] <= t[:, None]
        p_c = jnp.where(valid, jax.nn.softmax(jnp.where(valid, s, NEG_INF), axis=-1), 0.0)
        o_c = jnp.einsum('bgrqn,bngd->bqgrd', p_c.astype(vc.dtype), vc)
        imp = jnp.einsum('bgrqn,nj->bgqj', p_c, overlap)
        j = jnp.arange(n_slc)
        cur = (t // NSA_SLC_BLOCK)[:, None]
        forced = (j == 0) | (j == cur) | (j == cur - 1)
        score = jnp.where(forced, FORCE_SCORE, jnp.where(j > cur, -1.0, imp))
        _, sel = lax.top_k(score, n_top)
        tok = (sel[..., None] * NSA_SLC_BLOCK + jnp.arange(NSA_SLC_BLOCK)).reshape(B_, G, Q_BLOCK, n_top * NSA_SLC_BLOCK)
        ks = k_slc_g[bi, gi, tok]
        vs = v_slc_g[bi, gi, tok]
        s = jnp.einsum('bqgrd,bgqsd->bgrqs', qi, ks, preferred_element_type=f32) * scale
        dist = pos_q[:, None, :, None] - positions[bi, tok]
        s = s + table_gr[t5_bucket(dist), gi].transpose(0, 1, 4, 2, 3).astype(f32)
        smask = (tok <= t[None, None, :, None])[:, :, None]
        p_s = jax.nn.softmax(jnp.where(smask, s, NEG_INF), axis=-1)
        o_s = jnp.einsum('bgrqs,bgqsd->bqgrd', p_s.astype(vs.dtype), vs)
        kw = lax.dynamic_slice_in_dim(k_win_p, blk * Q_BLOCK, Q_BLOCK + NSA_WINDOW, axis=1)
        vw = lax.dynamic_slice_in_dim(v_win_p, blk * Q_BLOCK, Q_BLOCK + NSA_WINDOW, axis=1)
        pk = lax.dynamic_slice_in_dim(pos_p, blk * Q_BLOCK, Q_BLOCK + NSA_WINDOW, axis=1)
        kidx = blk * Q_BLOCK - NSA_WINDOW + jnp.arange(Q_BLOCK + NSA_WINDOW)
        band = (kidx[None, :] >= 0) & (kidx[None, :] <= t[:, None]) & (t[:, None] - kidx[None, :] < NSA_WINDOW)
        s = jnp.einsum('bqgrd,bkgd->bgrqk', qi, kw, preferred_element_type=f32) * scale
        s = s + head_bias(pos_q[:, :, None] - pk[:, None, :])
        p_w = jax.nn.softmax(jnp.where(band, s, NEG_INF), axis=-1)
        o_w = jnp.einsum('bgrqk,bkgd->bqgrd', p_w.astype(vw.dtype), vw)
        o = gq[..., 0:1] * o_c + gq[..., 1:2] * o_s + gq[..., 2:3] * o_w
        return o.astype(qi.dtype)

    qb = qh.reshape(B_, nblk, Q_BLOCK, G, R, dh).swapaxes(0, 1)
    gb = gates.reshape(B_, nblk, Q_BLOCK, G, R, 3).swapaxes(0, 1)
    pb = positions.reshape(B_, nblk, Q_BLOCK).swapaxes(0, 1)
    o = lax.map(one_block, (qb, gb, pb, jnp.arange(nblk)))
    return o.swapaxes(0, 1).reshape(B_, L, NSA_WIDTH)

def even_layer(xn, mem_kv, w_in, lam_re, lam_im, log_dt, b_re, b_im, c_re, c_im, d_skip, w_glu, b_f):
    B_, L, _ = xn.shape
    u, g_s5, q, k, v, f_logit, g_fox, q_mem, g_mem = split_cols(xn @ w_in, EVEN_SPLITS)
    y_s5 = s5_mixer(u, lam_re, lam_im, log_dt, b_re, b_im, c_re, c_im, d_skip, w_glu) * jax.nn.silu(g_s5)
    log_f = jax.nn.log_sigmoid((f_logit + b_f).astype(jnp.float32))
    cum = jnp.cumsum(log_f, axis=1)
    heads = lambda t: t.reshape(B_, L, FOX_HEADS, FOX_HEAD_DIM)
    y_fox = causal_block_attention(heads(q), heads(k), heads(v), FOX_HEAD_DIM ** -0.5, cum).reshape(B_, L, FOX_WIDTH)
    y_fox = y_fox * jax.nn.silu(g_fox)
    y_mem = memory_attention(q_mem, mem_kv) * jax.nn.silu(g_mem)
    return jnp.concatenate([y_s5, y_fox.astype(y_s5.dtype), y_mem], axis=-1)

def odd_layer(xn, mem_kv, positions, t5_table, w_in, g_cq, g_ckv, w_uq, w_ukv, cmp_pe, cmp_w1, cmp_w2):
    (c_q, c_kv, k_rope, g_mla, q_nsa, k_cmp, v_cmp, k_slc, v_slc, k_win, v_win,
     nsa_gates, g_nsa, q_mem, g_mem) = split_cols(xn @ w_in, ODD_SPLITS)
    y_mla = mla_attention(c_q, c_kv, k_rope, positions, g_cq, g_ckv, w_uq, w_ukv) * jax.nn.silu(g_mla)
    y_nsa = nsa_attention(q_nsa, k_cmp, v_cmp, k_slc, v_slc, k_win, v_win, nsa_gates, positions, t5_table,
                          cmp_pe, cmp_w1, cmp_w2) * jax.nn.silu(g_nsa)
    y_mem = memory_attention(q_mem, mem_kv) * jax.nn.silu(g_mem)
    return jnp.concatenate([y_mla, y_nsa, y_mem], axis=-1)

def setup_inputs(seed: int = 0) -> dict:
    key = jax.random.key(seed)
    ks = jax.random.split(key, 32)
    f32 = jnp.float32

    def nrm(k, shape, scale):
        return scale * jax.random.normal(k, shape, f32)

    x = nrm(ks[0], (BATCH, SEQ, D_MODEL), 1.0)
    mem = nrm(ks[1], (BATCH, N_MEM, D_MODEL), 1.0)
    positions = jax.random.randint(ks[2], (BATCH, 1), 0, MAX_POS_OFFSET, jnp.int32) + jnp.arange(SEQ, dtype=jnp.int32)[None, :]
    norm_g = 1.0 + nrm(ks[3], (DEPTH, D_MODEL), 0.02)
    mem_norm_g = 1.0 + nrm(ks[4], (D_MODEL,), 0.02)
    final_norm_g = 1.0 + nrm(ks[5], (D_MODEL,), 0.02)
    t5_table = nrm(ks[6], (T5_BUCKETS, NSA_HEADS), 0.5)
    w_out = nrm(ks[7], (DEPTH, MIX_WIDTH, D_MODEL), MIX_WIDTH ** -0.5)
    mem_w_kv = nrm(ks[8], (DEPTH, D_MODEL, 2 * MEM_WIDTH), D_MODEL ** -0.5)
    even_w_in = nrm(ks[9], (N_EVEN, D_MODEL, EVEN_IN), D_MODEL ** -0.5)
    s5_lam_re = -0.5 * jnp.exp(nrm(ks[10], (N_EVEN, S5_GROUPS, S5_STATE), 0.05))
    s5_lam_im = math.pi * jnp.arange(S5_STATE, dtype=f32) + nrm(ks[11], (N_EVEN, S5_GROUPS, S5_STATE), 0.05)
    s5_log_dt = jax.random.uniform(ks[12], (N_EVEN, S5_GROUPS), f32, math.log(S5_DT_MIN), math.log(S5_DT_MAX))
    s5_b_re = nrm(ks[13], (N_EVEN, S5_GROUPS, S5_STATE, S5_GROUP), (2 * S5_GROUP) ** -0.5)
    s5_b_im = nrm(ks[14], (N_EVEN, S5_GROUPS, S5_STATE, S5_GROUP), (2 * S5_GROUP) ** -0.5)
    s5_c_re = nrm(ks[15], (N_EVEN, S5_GROUPS, S5_GROUP, S5_STATE), S5_STATE ** -0.5)
    s5_c_im = nrm(ks[16], (N_EVEN, S5_GROUPS, S5_GROUP, S5_STATE), S5_STATE ** -0.5)
    s5_d = nrm(ks[17], (N_EVEN, S5_GROUPS, S5_GROUP), 1.0)
    s5_w_glu = nrm(ks[18], (N_EVEN, S5_WIDTH, S5_WIDTH), S5_WIDTH ** -0.5)
    fox_b_f = FOX_FORGET_BIAS + nrm(ks[19], (N_EVEN, FOX_HEADS), 0.1)
    odd_w_in = nrm(ks[20], (N_ODD, D_MODEL, ODD_IN), D_MODEL ** -0.5)
    mla_g_cq = 1.0 + nrm(ks[21], (N_ODD, MLA_Q_RANK), 0.02)
    mla_g_ckv = 1.0 + nrm(ks[22], (N_ODD, MLA_KV_RANK), 0.02)
    mla_w_uq = nrm(ks[23], (N_ODD, MLA_Q_RANK, MLA_HEADS * (MLA_NOPE + MLA_ROPE)), MLA_Q_RANK ** -0.5)
    mla_w_ukv = nrm(ks[24], (N_ODD, MLA_KV_RANK, MLA_HEADS * (MLA_NOPE + MLA_V)), MLA_KV_RANK ** -0.5)
    nsa_cmp_pe = nrm(ks[25], (N_ODD, 2, NSA_CMP_LEN, NSA_HEAD_DIM), 0.5)
    nsa_cmp_w1 = nrm(ks[26], (N_ODD, 2, NSA_CMP_LEN * NSA_HEAD_DIM, NSA_CMP_HIDDEN), (NSA_CMP_LEN * NSA_HEAD_DIM) ** -0.5)
    nsa_cmp_w2 = nrm(ks[27], (N_ODD, 2, NSA_CMP_HIDDEN, NSA_HEAD_DIM), NSA_CMP_HIDDEN ** -0.5)
    return {'x': x, 'mem': mem, 'positions': positions, 'norm_g': norm_g, 'mem_norm_g': mem_norm_g,
            'final_norm_g': final_norm_g, 't5_table': t5_table, 'w_out': w_out, 'mem_w_kv': mem_w_kv,
            'even_w_in': even_w_in, 's5_lam_re': s5_lam_re, 's5_lam_im': s5_lam_im, 's5_log_dt': s5_log_dt,
            's5_b_re': s5_b_re, 's5_b_im': s5_b_im, 's5_c_re': s5_c_re, 's5_c_im': s5_c_im, 's5_d': s5_d,
            's5_w_glu': s5_w_glu, 'fox_b_f': fox_b_f, 'odd_w_in': odd_w_in, 'mla_g_cq': mla_g_cq,
            'mla_g_ckv': mla_g_ckv, 'mla_w_uq': mla_w_uq, 'mla_w_ukv': mla_w_ukv, 'nsa_cmp_pe': nsa_cmp_pe,
            'nsa_cmp_w1': nsa_cmp_w1, 'nsa_cmp_w2': nsa_cmp_w2}

def reference(x, mem, positions, norm_g, mem_norm_g, final_norm_g, t5_table, w_out, mem_w_kv,
              even_w_in, s5_lam_re, s5_lam_im, s5_log_dt, s5_b_re, s5_b_im, s5_c_re, s5_c_im, s5_d,
              s5_w_glu, fox_b_f, odd_w_in, mla_g_cq, mla_g_ckv, mla_w_uq, mla_w_ukv, nsa_cmp_pe,
              nsa_cmp_w1, nsa_cmp_w2):
    h = x
    mem_n = rms_norm(mem, mem_norm_g)
    for layer in range(DEPTH):
        xn = rms_norm(h, norm_g[layer])
        mem_kv = mem_n @ mem_w_kv[layer]
        i = layer // 2
        if layer % 2 == 0:
            mixed = even_layer(xn, mem_kv, even_w_in[i], s5_lam_re[i], s5_lam_im[i], s5_log_dt[i], s5_b_re[i],
                               s5_b_im[i], s5_c_re[i], s5_c_im[i], s5_d[i], s5_w_glu[i], fox_b_f[i])
        else:
            mixed = odd_layer(xn, mem_kv, positions, t5_table, odd_w_in[i], mla_g_cq[i], mla_g_ckv[i],
                              mla_w_uq[i], mla_w_ukv[i], nsa_cmp_pe[i], nsa_cmp_w1[i], nsa_cmp_w2[i])
        h = h + (mixed @ w_out[layer]).astype(h.dtype)
    return rms_norm(h, final_norm_g)


_drawn_inputs = setup_inputs


def setup_inputs(seed=0):
    import zlib

    import numpy as np

    out = dict(_drawn_inputs(seed))
    spreads = {}
    factors = {'norm_g': 7.353,
     'mem_norm_g': 8.0,
     'final_norm_g': 7.534,
     's5_lam_re': 64.0,
     's5_lam_im': 40.448,
     's5_log_dt': 41.256,
     's5_b_re': 55.024,
     's5_b_im': 56.888,
     's5_c_re': 56.32,
     's5_c_im': 56.816,
     'fox_b_f': 8.0,
     'mla_g_cq': 8.0,
     'mla_g_ckv': 8.0}
    for name, (base, spread) in spreads.items():
        noise = np.random.default_rng([zlib.crc32(name.encode()), seed]).standard_normal(out[name].shape)
        drawn = base * np.exp(spread * noise) if base else spread * noise
        out[name] = jnp.asarray(drawn.astype(out[name].dtype))
    for name, factor in factors.items():
        out[name] = (out[name] * factor).astype(out[name].dtype)
    return out
```

```python
import numpy as np
import math
from contextlib import ExitStack

import concourse.bass as bass
from concourse import mybir

F32 = mybir.dt.float32
F32R = mybir.dt.float32r
I32 = mybir.dt.int32
ACT = mybir.ActivationFunctionType
ALU = mybir.AluOpType
AX = mybir.AxisListType.X
ds = bass.ds

P = 128
D = 2048
T = 512
NMEM = 256
NPAD = 32
LB = 1408
TT = T // P
EVEN_IN = 7176
ODD_IN = 6744
KD = D // P
MIX = 2560
KM = MIX // P
EPS = 1e-6
NEG = -1e30
RAW = 4
COLS = 512


def const_inputs():
    half = 32
    inv_freq = (np.float32(10000.0) ** (-np.arange(half, dtype=np.float32) / np.float32(half))).astype(np.float32)
    inv = np.tile(inv_freq, 4).reshape(P, 1)
    sgn = np.tile(np.repeat(np.array([-1.0, 1.0], np.float32), 32), 2).reshape(P, 1)
    n = np.arange(3000)
    ratio = np.log(np.maximum(n, 1).astype(np.float32) / np.float32(16)) / np.float32(math.log(64))
    large = np.minimum(16 + (ratio * np.float32(16)).astype(np.int32), 31)
    bucket = np.where(n < 16, n, large)
    first = [float(np.argmax(bucket >= b)) for b in range(1, 32)]
    thr = np.tile(np.array(first, np.float32), (P, 1))
    sel = np.zeros((8, P, P), np.float32)
    for h in range(8):
        sel[h, h, :] = 1.0
    return {"c_sel": sel, "c_inv": inv.astype(np.float32), "c_sgn": sgn, "c_thr": thr}


def build(nc, a):
    x, mem = a["x"][0], a["mem"][0]
    out = a["out"][0]
    with ExitStack() as ctx:
        def sb(name, shape, dt=F32):
            return ctx.enter_context(nc.sbuf_tensor(name, shape, dt))

        def sem(name):
            return ctx.enter_context(nc.semaphore(name))

        def dram(name, shape, dt=F32):
            return nc.dram_tensor(name, shape, dt, kind="Internal").ap()

        yE = dram("yE", (EVEN_IN, T))
        yO = dram("yO", (ODD_IN, T))
        kmD = [dram(f"kmD{l}", (512, NMEM)) for l in range(2)]
        vmD = [dram(f"vmD{l}", (NMEM, 512)) for l in range(2)]

        wraw = sb("wraw", [P, RAW, 2, COLS])
        wsp = sb("wsp", [P, RAW, 2, 2, COLS], F32R)
        A = sb("A", [P, 40, T], F32R)
        stage = sb("stage", [P, 4, COLS])
        S = sb("S", [P, 16384])
        ident = sb("ident", [P, P])
        gcol = sb("gcol", [P, 3, KD])
        small = sb("small", [P, 64])
        PS = ctx.enter_context(nc.psum_tensor("PS", [P, 8, 512], F32))

        w_loaded = [sem(f"w_loaded{i}") for i in range(RAW)]
        w_hi = sem("w_hi")
        w_lo = sem("w_lo")
        slot_used = sem("slot_used")
        banks_free = sem("banks_free")
        stored = sem("stored")
        ident_ok = sem("ident_ok")
        gains_in = sem("gains_in")
        rows_in = [sem(f"rows_in{t}") for t in range(4)]
        sq_done = sem("sq_done")
        rms_step = sem("rms_step")
        rms_sqrt = sem("rms_sqrt")
        rows_ok = sem("rows_ok")
        nt_pe = sem("nt_pe")
        nt_hi = sem("nt_hi")
        nt_lo = sem("nt_lo")

        mwk = a["mem_w_kv"]
        plan = []
        count = {"slot": 0, "chunk": 0, "bank": 0, "staged": 0, "stored": 0}

        def job(name, w, k_tiles, chunks, cols=COLS, nf=4, mode="F", n=T, hi=0, lo=16, to_stage=True, c0=0):
            j = dict(name=name, w=w.rearrange("(k p) n -> p k n", p=P), spc=k_tiles // 2, chunks=chunks, cols=cols,
                     nf=nf, mode=mode, n=n, hi=hi, lo=lo, stage=to_stage, c0=c0, **{k + "0": v for k, v in count.items()})
            count["slot"] += k_tiles // 2 * chunks
            count["chunk"] += chunks
            count["bank"] += nf * chunks
            if to_stage:
                count["staged"] += nf * chunks
                count["stored"] += chunks
            plan.append(j)
            return j

        for l in range(2):
            job(f"memk{l}", mwk[l][:, 0:512], KD, 1, mode="F", n=NMEM)
            job(f"memv{l}", mwk[l][:, 512:1024], KD, 1, mode="T", nf=2)
        w_even = a["even_w_in"][0]
        E1 = job("E1", w_even, KD, 14)
        E2 = job("E2", w_even[:, EVEN_IN - P:EVEN_IN], KD, 1, cols=P, nf=1)
        GLU = job("GLU", a["s5_w_glu"][0], 8, 2, hi=32, lo=8, to_stage=False)
        OUT0 = job("OUT0", a["w_out"][0], KM, 4, mode="T", hi=0, lo=KM, to_stage=False)
        w_odd = a["odd_w_in"][0]
        O1 = job("O1", w_odd, KD, 13)
        O2 = job("O2", w_odd[:, ODD_IN - P:ODD_IN], KD, 1, cols=P, nf=1)
        UQ = job("UQ", a["mla_w_uq"][0], 4, 3, hi=32, lo=8)
        UKV = job("UKV", a["mla_w_ukv"][0], 4, 4, hi=36, lo=12)
        OUT1 = job("OUT1", a["w_out"][1], KM, 4, mode="T", hi=0, lo=KM, to_stage=False)
        jobs = {j["name"]: j for j in plan}

        def sp_slot(sp, j, c, s, n, q, rounds, early):
            if not early:
                sp.wait_ge(w_lo, n - 3)
            col = c * COLS if j["chunks"] > 1 else 0
            sp.dma_start(wraw[:, q, :, 0:j["cols"]],
                         j["w"][:, 2 * s:2 * s + 2, ds(col, j["cols"])]).then_inc(w_loaded[q], 16)

        def act_slot(act, j, n, q, rounds, early):
            act.wait_ge(w_loaded[q], rounds * 16 + 16)
            if not early:
                act.wait_ge(slot_used, n - 3)
            nc.scalar.activation(wsp[:, q, 0, :, 0:j["cols"]], wraw[:, q, :, 0:j["cols"]], ACT.Copy).then_inc(w_hi, 1)

        def dve_slot(dve, j, n, q):
            dve.wait_ge(w_hi, n + 1)
            nc.vector.tensor_tensor(wsp[:, q, 1, :, 0:j["cols"]], wraw[:, q, :, 0:j["cols"]],
                                    wsp[:, q, 0, :, 0:j["cols"]].bitcast(F32), ALU.subtract).then_inc(w_lo, 1)

        def pe_slot(pe, j, s, n, q, free):
            pe.wait_ge(w_lo, n + 1)
            for kk in range(2):
                kt = 2 * s + kk
                for f in range(j["nf"]):
                    if kk == 0 and s == 0 and free[f] is not None:
                        pe.wait_ge(banks_free, free[f])
                    for i, (wp, ap) in enumerate(((0, j["hi"]), (0, j["lo"]), (1, j["hi"]))):
                        if j["mode"] == "F":
                            lhs = wsp[:, q, wp, kk, f * P:f * P + P]
                            rhs = A[:, ap + kt, 0:j["n"]]
                            dst = PS[:, f, 0:j["n"]]
                        else:
                            lhs = A[:, ap + kt, f * P:f * P + P]
                            rhs = wsp[:, q, wp, kk, :]
                            dst = PS[:, f, :]
                        mm = nc.tensor.matmul(dst, lhs, rhs, start=(s == 0 and kk == 0 and i == 0),
                                              stop=(s == j["spc"] - 1 and kk == 1 and i == 2))
            return mm.then_inc(slot_used, 1)

        def chunk_slots(j, c, first):
            for s in range(j["spc"]):
                base = j["slot0"] + s
                if isinstance(c, int):
                    n = base + c * j["spc"]
                    yield s, n, n % RAW, n // RAW, n < RAW
                else:
                    assert j["spc"] % RAW == 0
                    yield s, c * j["spc"] + base, base % RAW, c * (j["spc"] // RAW) + base // RAW, False

        def sp_chunk(sp, j, c):
            for s, n, q, r, early in chunk_slots(j, c, False):
                sp_slot(sp, j, c, s, n, q, r, early)

        def pe_chunk(pe, j, c, hook=None):
            if isinstance(c, int) and c == 0:
                free = [j["bank0"] if j["bank0"] else None] + [None] * 3
            else:
                free = [c * j["nf"] + (j["bank0"] - j["nf"] + 1 + f) for f in range(j["nf"])] + [None] * 3
            for s, n, q, r, early in chunk_slots(j, c, False):
                pe_slot(pe, j, s, n, q, free)
                if hook:
                    hook(s)

        def dve_chunk(dve, j, c, hook=None):
            for s, n, q, r, early in chunk_slots(j, c, False):
                dve_slot(dve, j, n, q)
                if hook:
                    hook(s)

        def act_evac(act, j, c):
            act.wait_ge(slot_used, c * j["spc"] + (j["slot0"] + j["spc"]))
            if not (isinstance(c, int) and c * 1 + j["stored0"] == 0):
                act.wait_ge(stored, c * 16 + j["stored0"] * 16)
            for f in range(j["nf"]):
                n = j["n"] if j["mode"] == "F" else COLS
                nc.scalar.activation(stage[:, f, 0:n], PS[:, f, 0:n], ACT.Copy).then_inc(banks_free, 1)

        def act_chunk(act, j, c, pending, hook=None):
            for s, n, q, r, early in chunk_slots(j, c, False):
                if s == min(3, j["spc"] - 1):
                    pending()
                act_slot(act, j, n, q, r, early)
                if hook:
                    hook(s)

        def pool_store(pool, j, c, dst, n=None):
            pool.wait_ge(banks_free, c * j["nf"] + (j["bank0"] + j["nf"]))
            n = n or (j["n"] if j["mode"] == "F" else COLS)
            pool.dma_start(dst, stage[:, 0:j["nf"], 0:n]).then_inc(stored, 16)

        hrows = S[:, 0:8192].rearrange("p (t d) -> p t d", t=4)
        junk = PS[:, 4:8, :]
        NORMS = [dict(tiles=2, g=2, k=0), dict(tiles=4, g=0, k=1), dict(tiles=4, g=1, k=2), dict(tiles=4, k=3)]

        def act_norm(act, v):
            if v["k"] == 2:
                act.wait_ge(banks_free, OUT0["bank0"] + 16)
            if v["k"] == 3:
                act.wait_ge(banks_free, OUT1["bank0"] + 16)
            for t in range(v["tiles"]):
                if v["k"] < 2:
                    act.wait_ge(rows_in[t], 16 if v["k"] == 0 or t >= 2 else 32)
                if t:
                    act.wait_ge(sq_done, [0, 2, 6, 10][v["k"]] + t)
                elif v["k"] == 1:
                    act.wait_ge(nt_lo, KD)
                nc.scalar.activation(junk, hrows[:, t, :], ACT.Square,
                                     accum_out=small[:, t:t + 1]).then_inc(sq_done, 1)
            act.wait_ge(rms_step, 5 * v["k"] + 1)
            nc.scalar.activation(small[:, 8:8 + v["tiles"]], small[:, 4:4 + v["tiles"]], ACT.Sqrt).then_inc(rms_sqrt, 1)
            if v["k"] == 3:
                return
            if v["k"] == 0:
                act.wait_ge(gains_in, 48)
            for k in range(KD):
                act.wait_ge(nt_pe, KD * v["k"] + k + 1)
                n = v["tiles"] * P
                nc.scalar.activation(A[:, k, 0:n], PS[:, 4 + k % 4, 0:n], ACT.Copy,
                                     scale=gcol[:, v["g"], k:k + 1]).then_inc(nt_hi, 1)

        def dve_norm(dve, v):
            t = v["tiles"]
            ssq, var, root, r0, r1, r = (small[:, 4 * i:4 * i + t] for i in range(6))
            dve.wait_ge(sq_done, [2, 6, 10, 14][v["k"]])
            nc.vector.tensor_scalar(var, ssq, 1.0 / D, EPS, ALU.mult, ALU.add).then_inc(rms_step, 1)
            dve.wait_ge(rms_sqrt, v["k"] + 1)
            nc.vector.reciprocal(r0, root).then_inc(rms_step, 1)
            dve.wait_ge(rms_step, 5 * v["k"] + 2)
            nc.vector.tensor_tensor(r1, r0, r0, ALU.mult).then_inc(rms_step, 1)
            dve.wait_ge(rms_step, 5 * v["k"] + 3)
            nc.vector.tensor_tensor(r1, r1, var, ALU.mult).then_inc(rms_step, 1)
            dve.wait_ge(rms_step, 5 * v["k"] + 4)
            nc.vector.tensor_scalar(r1, r1, -0.5, 1.5, ALU.mult, ALU.add).then_inc(rms_step, 1)
            dve.wait_ge(rms_step, 5 * v["k"] + 5)
            nc.vector.tensor_tensor(r, r0, r1, ALU.mult).then_inc(rows_ok, 1)
            base = [0, 3, 8, 13][v["k"]]
            dve.wait_ge(rows_ok, base + 1)
            if v["k"] == 3:
                return
            if v["k"] == 2:
                dve.wait_ge(h1_out, 16)
            for i in range(t):
                nc.vector.tensor_scalar(hrows[:, i, :], hrows[:, i, :], r[:, i:i + 1], None, ALU.mult).then_inc(rows_ok, 1)
            if v["k"] == 0:
                dve.wait_ge(gains_in, 48)
            for k in range(KD):
                n = t * P
                dve.wait_ge(nt_hi, KD * v["k"] + k + 1)
                nc.vector.scalar_tensor_tensor(A[:, 16 + k, 0:n], PS[:, 4 + k % 4, 0:n], gcol[:, v["g"], k:k + 1],
                                               A[:, k, 0:n].bitcast(F32), ALU.mult, ALU.subtract).then_inc(nt_lo, 1)

        def pe_norm(pe, v):
            base = [0, 3, 8][v["k"]]
            pe.wait_ge(rows_ok, base + 1 + v["tiles"])
            for k in range(KD):
                g = KD * v["k"] + k
                if g >= 4:
                    pe.wait_ge(nt_lo, g - 3)
                for t in range(v["tiles"]):
                    mm = nc.tensor.transpose(PS[:, 4 + k % 4, t * P:(t + 1) * P], hrows[:, t, k * P:(k + 1) * P], ident[:, :])
                mm.then_inc(nt_pe, 1)

        ctx.enter_context(nc.allow_non_contiguous_dma(reason="small columns of gains"))

        offs = [8192]

        def cut(n, *shape, at=None):
            o = offs[0] if at is None else at
            if at is None:
                offs[0] += n
            v = S[:, o:o + n]
            return v

        bc = cut(1024).rearrange("p (i j c) -> p i j c", i=2, j=32)
        cc = cut(1024).rearrange("p (i j c) -> p i j c", i=2, j=32)
        prm = cut(192).rearrange("p (k j) -> p k j", k=6)
        dcol = cut(8)
        low0 = offs[0]
        cnat = cut(2048).rearrange("p (i m q) -> p i m q", i=2, m=8)
        ct = cut(1024).rearrange("p (i j c) -> p i j c", i=2, j=32)
        pt = cut(2816).rearrange("p (k q) -> p k q", k=22)
        pti = pt[:, 20, :].bitcast(I32)
        assert offs[0] <= 16384
        tiles_off = [0]

        def tile512(k=1):
            o = tiles_off[0]
            if o + 512 * k > 8192 and o <= 8192:
                o = max(o, low0)
            tiles_off[0] = o + 512 * k
            assert tiles_off[0] <= 16384
            return S[:, o:o + 512 * k]

        timeS = tile512()
        fS = tile512()
        cosS = [tile512(), tile512()]
        sinS = [tile512(), tile512()]
        ubS = [tile512(2).rearrange("p (i t) -> p i t", i=2) for _ in range(2)]
        t1S, t2S, t5S, vimS, p2S, uS, ystS = [tile512() for _ in range(6)] + [None]
        xS = [tile512(2).rearrange("p (i t) -> p i t", i=2) for _ in range(2)]
        exb = tile512(2).rearrange("p (i j c) -> p i j c", i=2, j=4)
        exc = tile512(2).rearrange("p (i j c) -> p i j c", i=2, j=4)
        bT = tile512(2).rearrange("p (i j c) -> p i j c", i=2, j=4)
        ystS = tile512()
        dg = S[:, tiles_off[0]:tiles_off[0] + P]
        assert tiles_off[0] + P <= 16384

        yS = dram("yS", (1024, T))
        prep_in = sem("prep_in")
        prep = sem("prep")
        prep_sin = sem("prep_sin")
        prep_den = sem("prep_den")
        prepT = sem("prepT")
        prepE = sem("prepE")
        cprime = sem("cprime")
        init = sem("init")
        exb_ok, exc_ok, u_in = sem("exb_ok"), sem("exc_ok"), sem("u_in")
        xt_pe, xt_ev = sem("xt_pe"), sem("xt_ev")
        f_ok, f_chain, tab_ok, bu_ok, eb_ok, vi_ok, vi_chain = [sem(n) for n in ("f_ok", "f_chain", "tab_ok", "bu_ok", "eb_ok", "vi_ok", "vi_chain")]
        r_chain, y_ok, y_ev, y_out = [sem(n) for n in ("r_chain", "y_ok", "y_ev", "y_out")]
        MAGIC = 12582912.0
        TWO_PI = 6.283185307179586
        C1, C2, C3 = 6.28125, 1.93500518798828125e-3, 3.0199159819567529e-7

        def pool_prep_loads(pool):
            for i, n in enumerate(("s5_lam_re", "s5_lam_im")):
                pool.dma_start(pt[0:32, i, :], a[n][0].rearrange("(j e) p -> j (e p)", e=2)).then_inc(prep_in, 16)
            pool.dma_start(pt[0:32, 2, 0:2], a["s5_log_dt"][0].rearrange("(j e) -> j e", e=2)).then_inc(prep_in, 16)
            for i, n in enumerate(("s5_b_re", "s5_b_im")):
                pool.dma_start(bc[:, i, :, :], a[n][0].rearrange("g p c -> (g p) c").rearrange("(j q) c -> q j c", q=P)).then_inc(prep_in, 16)
            for i, n in enumerate(("s5_c_re", "s5_c_im")):
                v = a[n][0].rearrange("g c p -> (g c) p").rearrange("(m r) p -> r m p", r=P)
                for e in range(2):
                    pool.dma_start(cnat[:, i, :, e * 64:e * 64 + 64], v).then_inc(prep_in, 16)
            pool.dma_start(dcol, a["s5_d"][0].rearrange("g c -> (g c)").rearrange("(m r) -> r m", r=P)).then_inc(prep_in, 16)

        def pool_prep(pool):
            k = [0]
            pool.wait_ge(prep_in, 16 * 10)

            def ts(o, i, s1, s2, o1=ALU.mult, o2=ALU.add):
                link(nc.gpsimd.tensor_scalar(o, i, s1, s2, o1, o2))

            def tt(o, i, j_, op=ALU.mult):
                link(nc.gpsimd.tensor_tensor(o, i, j_, op))

            def link(ins):
                k[0] += 1
                ins.then_inc(prep, 1)
                pool.wait_ge(prep, k[0])

            def exp_parts(xx, kk, rr, q, two, twoi, t):
                ts(kk, xx, 1.4426950408889634, MAGIC)
                ts(kk, kk, MAGIC, None, ALU.subtract, ALU.bypass)
                ts(t, kk, -0.693359375, None, ALU.mult, ALU.bypass)
                tt(rr, xx, t, ALU.add)
                ts(t, kk, 2.12194440e-4, None, ALU.mult, ALU.bypass)
                tt(rr, rr, t, ALU.add)
                ts(kk, kk, -127.0, 127.0, ALU.max, ALU.min)
                ts(twoi, kk, 127.0, 8388608.0, ALU.add, ALU.mult)
                ts(q, rr, 1.0 / 8, 1.0)
                for n in range(7, 1, -1):
                    tt(q, q, rr)
                    ts(q, q, 1.0 / n, 1.0)
                tt(q, q, rr)

            R = slice(0, 32)
            t_ = lambda i, w=P: pt[R, i, 0:w]
            exp_parts(t_(2, 2), t_(3, 2), t_(4, 2), t_(5, 2), t_(20, 2), pti[R, 0:2], t_(6, 2))
            tt(t_(5, 2), t_(5, 2), t_(20, 2))
            tt(t_(5, 2), t_(5, 2), t_(20, 2), ALU.add)
            dt = pt[R, 5, 0:2].unsqueeze(2).broadcast_to([32, 2, 64])
            e3 = lambda i: pt[R, i, :].rearrange("r (e p) -> r e p", e=2)
            tt(e3(7), e3(0), dt)
            tt(e3(8), e3(1), dt)
            exp_parts(t_(7), t_(3), t_(4), t_(9), t_(20), pti[R, :], t_(6))
            tt(t_(9), t_(9), t_(20))
            ts(t_(6), t_(20), 1.0, None, ALU.subtract, ALU.bypass)
            tt(t_(9), t_(9), t_(6), ALU.add)
            ts(t_(10), t_(9), 1.0, None, ALU.add, ALU.bypass)
            ts(t_(3), t_(8), 1.0 / TWO_PI, MAGIC)
            ts(t_(3), t_(3), MAGIC, None, ALU.subtract, ALU.bypass)
            for cst in (C1, C2, C3):
                ts(t_(6), t_(3), -cst, None, ALU.mult, ALU.bypass)
                tt(t_(8), t_(8), t_(6), ALU.add)
            ts(t_(8), t_(8), -3.1415925, 3.1415925, ALU.max, ALU.min)
            prep_angle[0] = k[0]
            ts(t_(11), t_(8), 1.0 / TWO_PI, None, ALU.mult, ALU.bypass)
            ts(t_(12), t_(11), 1.0, 192.0)
            ts(t_(12), t_(12), 192.0, None, ALU.subtract, ALU.bypass)
            tt(t_(13), t_(11), t_(12), ALU.subtract)
            tt(t_(14), t_(0), t_(0))
            tt(t_(6), t_(1), t_(1))
            tt(t_(14), t_(14), t_(6), ALU.add)
            prep_den_at[0] = k[0]
            pool.wait_ge(prep_sin, 2)
            tt(t_(17), t_(16), t_(16))
            ts(t_(17), t_(17), -2.0, None, ALU.mult, ALU.bypass)
            tt(t_(15), t_(15), t_(10))
            ts(t_(18), t_(17), 1.0, None, ALU.add, ALU.bypass)
            tt(t_(18), t_(18), t_(9))
            tt(t_(18), t_(18), t_(17), ALU.add)
            pool.wait_ge(prep_den, 1)
            tt(t_(3), t_(18), t_(0))
            tt(t_(4), t_(15), t_(1))
            tt(t_(3), t_(3), t_(4), ALU.add)
            tt(t_(21), t_(3), t_(19))
            tt(t_(3), t_(15), t_(0))
            tt(t_(4), t_(18), t_(1))
            tt(t_(3), t_(3), t_(4), ALU.subtract)
            tt(t_(2), t_(3), t_(19))
            prep_all[0] = k[0]

        prep_angle, prep_den_at, prep_all = [0], [0], [0]
        N_EXP = 8 + 1 + 12 + 1
        prep_angle_n = 2 * N_EXP + 2 + 2 + 4 + 2 + 6 + 1
        prep_den_n = prep_angle_n + 4 + 3
        prep_all_n = prep_den_n + 6 + 8

        def act_prep_sin(act):
            act.wait_ge(prep, prep_angle_n)
            nc.scalar.activation(pt[0:32, 15, :], pt[0:32, 8, :], ACT.Sin).then_inc(prep_sin, 1)
            nc.scalar.activation(pt[0:32, 16, :], pt[0:32, 8, :], ACT.Sin, scale=0.5).then_inc(prep_sin, 1)

        def dve_prep_den(dve):
            dve.wait_ge(prep, prep_den_n)
            nc.vector.reciprocal(pt[0:32, 19, :], pt[0:32, 14, :]).then_inc(prep_den, 1)

        def pe_prep(pe, s):
            if s == 1:
                pe.wait_ge(prep, prep_all_n)
                pe.wait_ge(nt_lo, 2 * KD)
                for i, row in enumerate((10, 11, 12, 13, 21, 2)):
                    mm = nc.tensor.transpose(PS[:, 4, i * 32:i * 32 + 32], pt[0:32, row, :], ident[0:32, 0:32])
                mm.then_inc(prepT, 1)
            if s == 3:
                pe.wait_ge(prepE, 1)
                for i in range(2):
                    for m in range(8):
                        mm = nc.tensor.transpose(PS[:, 4 + 2 * i + m // 4, (m % 4) * P:(m % 4) * P + P], cnat[:, i, m, :], ident[:, :])
                mm.then_inc(prepT, 1)

        def act_prep(act, s):
            if s == 5:
                act.wait_ge(prepT, 1)
                nc.scalar.activation(prm, PS[:, 4, 0:192].rearrange("p (k j) -> p k j", k=6), ACT.Copy).then_inc(prepE, 1)
            if s == 7:
                act.wait_ge(prepT, 2)
                for i in range(2):
                    for h in range(2):
                        for e in range(2):
                            src = PS[e * 64:e * 64 + 64, 4 + 2 * i + h, :].rearrange("p (j k c) -> p j k c", j=16, k=2)[:, :, e, :]
                            nc.scalar.activation(ct[e * 64:e * 64 + 64, i, 16 * h:16 * h + 16, :], src, ACT.Copy).then_inc(prepE, 1)

        def pool_cprime(pool):
            pool.wait_ge(prepE, 9)
            pool.wait_ge(nt_pe, 2 * KD)
            f3 = [prm[:, 4 + i, :].unsqueeze(2).broadcast_to([P, 32, 16]) for i in range(2)]
            u0 = cnat[:, 0].rearrange("p m q -> p (m q)")[:, 0:512].rearrange("p (j c) -> p j c", j=32)
            u1 = cnat[:, 0].rearrange("p m q -> p (m q)")[:, 512:1024].rearrange("p (j c) -> p j c", j=32)
            u2 = cnat[:, 1].rearrange("p m q -> p (m q)")[:, 0:512].rearrange("p (j c) -> p j c", j=32)
            u3 = cnat[:, 1].rearrange("p m q -> p (m q)")[:, 512:1024].rearrange("p (j c) -> p j c", j=32)
            nc.gpsimd.tensor_tensor(u0, ct[:, 0], f3[0], ALU.mult).then_inc(cprime, 1)
            nc.gpsimd.tensor_tensor(u1, ct[:, 1], f3[1], ALU.mult).then_inc(cprime, 1)
            nc.gpsimd.tensor_tensor(u2, ct[:, 0], f3[1], ALU.mult).then_inc(cprime, 1)
            nc.gpsimd.tensor_tensor(u3, ct[:, 1], f3[0], ALU.mult).then_inc(cprime, 1)
            pool.wait_ge(cprime, 4)
            nc.gpsimd.tensor_tensor(cc[:, 0], u0, u1, ALU.subtract).then_inc(cprime, 1)
            nc.gpsimd.tensor_tensor(u2, u2, u3, ALU.add).then_inc(cprime, 1)
            pool.wait_ge(cprime, 6)
            nc.gpsimd.tensor_scalar(cc[:, 1], u2, -1.0, None, ALU.mult).then_inc(cprime, 1)
            pool.wait_ge(cprime, 7)
            nc.gpsimd.iota(timeS, pattern=[[1, T]], base=0, channel_multiplier=0,
                           allow_small_or_imprecise_dtypes=True).then_inc(init, 1)
            nc.gpsimd.memset(exb, 0.0).then_inc(init, 1)
            nc.gpsimd.memset(exc, 0.0).then_inc(init, 1)
            pool.wait_ge(init, 3)

        def pool_frames(pool, m, which, ok):
            src, per = (bc, 5) if which is exb else (cc, 4)
            for e in range(2):
                for i in range(2):
                    s0 = src[e * 64:e * 64 + 64, i, ds(m * 4, 4), :]
                    fr = which[e * 64:e * 64 + 64, i, :, :].rearrange("p j c -> p (j c)")
                    v = bass.AP(tensor=fr.tensor, offset=fr.offset + 16 * e, ap=[fr.ap[0], [160, 4], [1, 16]])
                    nc.gpsimd.tensor_copy(v, s0).then_inc(ok, 1)
                pool.wait_ge(ok, m * per + (2 * e + 2))

        def pool_s5_start(pool, m, first):
            if not first:
                pool.wait_ge(xt_pe, m * 2)
            pool_frames(pool, m, exb, exb_ok)
            if not first:
                pool.wait_ge(y_ok, m * 4 - 1)
            nc.gpsimd.tensor_tensor(dg, ident[:, :], dcol[:, ds(m, 1)].broadcast_to([P, P]), ALU.mult).then_inc(exb_ok, 1)
            pool.dma_start(uS, yE[ds(m * P, P), :]).then_inc(u_in, 16)

        def pool_s5_c(pool, m, first):
            if not first:
                pool.wait_ge(y_ok, m * 4)
            pool_frames(pool, m, exc, exc_ok)
            if not first:
                pool.wait_ge(y_ev, m * 1)
                pool.dma_start(yS[ds((m - 1) * P, P), :], ystS).then_inc(y_out, 16)

        def pool_vi(pool, m, t, first):
            n1 = m * 4 + (t + 1)
            b = ubS[t % 2]
            pool.wait_ge(eb_ok, n1)
            pool.wait_ge(tab_ok, n1)
            if not (first and t == 0):
                pool.wait_ge(r_chain, (m * 4 + t) * 11)
            nc.gpsimd.tensor_tensor(vimS, cosS[t % 2], b[:, 1, :], ALU.mult).then_inc(vi_chain, 1)
            nc.gpsimd.tensor_tensor(p2S, sinS[t % 2], b[:, 0, :], ALU.mult).then_inc(vi_chain, 1)
            pool.wait_ge(vi_chain, n1 * 2)
            nc.gpsimd.tensor_tensor(vimS, vimS, p2S, ALU.subtract).then_inc(vi_ok, 1)

        def dve_f(dve, m, t, first):
            n = m * 4 + t
            if not (first and t == 0):
                dve.wait_ge(tab_ok, n)
            col = lambda k: prm[:, k, ds(n, 1)]
            nc.vector.tensor_scalar(fS, timeS, col(1), MAGIC, ALU.mult, ALU.add).then_inc(f_chain, 1)
            dve.wait_ge(f_chain, n * 4 + 1)
            nc.vector.tensor_scalar(fS, fS, MAGIC, None, ALU.subtract).then_inc(f_chain, 1)
            dve.wait_ge(f_chain, n * 4 + 2)
            nc.vector.scalar_tensor_tensor(fS, timeS, col(2), fS, ALU.mult, ALU.subtract).then_inc(f_chain, 1)
            dve.wait_ge(f_chain, n * 4 + 3)
            nc.vector.scalar_tensor_tensor(fS, timeS, col(3), fS, ALU.mult, ALU.add).then_inc(f_chain, 1)
            dve.wait_ge(f_chain, n * 4 + 4)
            nc.vector.tensor_scalar(fS, fS, -0.4999999, 0.4999999, ALU.max, ALU.min).then_inc(f_ok, 1)

        def act_tab(act, m, t, first):
            n = m * 4 + t
            act.wait_ge(f_ok, n + 1)
            if not (first and t < 2):
                act.wait_ge(r_chain, (n - 1) * 11)
            nc.scalar.activation(sinS[t % 2], fS, ACT.Sin, scale=TWO_PI).then_inc(tab_chain, 1)
            nc.scalar.activation(cosS[t % 2], fS, ACT.Abs).then_inc(tab_chain, 1)
            act.wait_ge(tab_chain, n * 2 + 2)
            nc.scalar.activation(cosS[t % 2], cosS[t % 2], ACT.Sin, scale=-TWO_PI, bias=half_pi).then_inc(tab_ok, 1)

        def act_eb(act, m, t, first):
            n = m * 4 + t
            act.wait_ge(bu_ok, n + 1)
            if not (first and t < 2):
                act.wait_ge(r_chain, (n - 1) * 11)
                act.wait_ge(vi_ok, n - 1)
            nc.scalar.activation(ubS[t % 2], PS[:, 4:6, :], ACT.Copy).then_inc(eb_ok, 1)

        def act_xt(act, m, i):
            act.wait_ge(xt_pe, m * 2 + (i + 1))
            nc.scalar.activation(bT[:, i], PS[:, 7, :].rearrange("p (j c) -> p j c", j=4), ACT.Copy).then_inc(xt_ev, 1)

        def act_yev(act, m1):
            act.wait_ge(y_ok, m1 * 4)
            if not (isinstance(m1, int) and m1 == 1):
                act.wait_ge(y_out, (m1 - 1) * 16)
            nc.scalar.activation(ystS, PS[:, 6, :], ACT.Copy).then_inc(y_ev, 1)

        def dve_r(dve, m, t, first):
            n = m * 4 + t
            co, si, b, x_ = cosS[t % 2], sinS[t % 2], ubS[t % 2], xS[t % 2]
            c0 = n * 11
            mag = prm[:, 0, ds(n, 1)].broadcast_to([P, T])
            dve.wait_ge(eb_ok, n + 1)
            dve.wait_ge(tab_ok, n + 1)
            if not (first and t == 0):
                dve.wait_ge(r_chain, c0)
            nc.vector.tensor_tensor(t1S, co, b[:, 0, :], ALU.mult).then_inc(r_chain, 1)
            nc.vector.tensor_tensor(t2S, si, b[:, 1, :], ALU.mult).then_inc(r_chain, 1)
            dve.wait_ge(r_chain, c0 + 2)
            nc.vector.tensor_tensor(t1S, t1S, t2S, ALU.add).then_inc(r_chain, 1)
            dve.wait_ge(vi_ok, n + 1)
            nc.vector.tensor_tensor_scan(vimS, mag, vimS, 0.0, ALU.mult, ALU.add).then_inc(r_chain, 1)
            dve.wait_ge(r_chain, c0 + 4)
            nc.vector.tensor_tensor_scan(t1S, mag, t1S, 0.0, ALU.mult, ALU.add).then_inc(r_chain, 1)
            if not (first and t < 2):
                dve.wait_ge(y_ok, n - 1)
            nc.vector.tensor_tensor(t2S, si, vimS, ALU.mult).then_inc(r_chain, 1)
            nc.vector.tensor_tensor(t5S, co, vimS, ALU.mult).then_inc(r_chain, 1)
            dve.wait_ge(r_chain, c0 + 7)
            nc.vector.tensor_tensor(x_[:, 0, :], co, t1S, ALU.mult).then_inc(r_chain, 1)
            nc.vector.tensor_tensor(x_[:, 1, :], si, t1S, ALU.mult).then_inc(r_chain, 1)
            dve.wait_ge(r_chain, c0 + 9)
            nc.vector.tensor_tensor(x_[:, 0, :], x_[:, 0, :], t2S, ALU.subtract).then_inc(r_chain, 1)
            nc.vector.tensor_tensor(x_[:, 1, :], x_[:, 1, :], t5S, ALU.add).then_inc(r_chain, 1)

        def pe_xt(pe, m, i, first):
            if i == 0:
                pe.wait_ge(exb_ok, m * 5 + 5)
                if not first:
                    pe.wait_ge(xt_ev, m * 2)
                else:
                    pe.wait_ge(prepE, 9)
            else:
                pe.wait_ge(xt_ev, m * 2 + 1)
            for j_ in range(4):
                mm = nc.tensor.transpose(PS[:, 7, j_ * P:j_ * P + P], exb[:, i, j_, :], ident[:, :])
            mm.then_inc(xt_pe, 1)

        def pe_bu(pe, m, t, first):
            n = m * 4 + t
            if t == 0:
                pe.wait_ge(xt_ev, m * 2 + 2)
                pe.wait_ge(u_in, m * 16 + 16)
            if not (first and t == 0):
                pe.wait_ge(eb_ok, n)
            nc.tensor.matmul(PS[:, 4, :], bT[:, 0, t, :], uS, start=True, stop=True)
            nc.tensor.matmul(PS[:, 5, :], bT[:, 1, t, :], uS, start=True, stop=True).then_inc(bu_ok, 1)

        def pe_y(pe, m, t, first):
            n = m * 4 + t
            if t == 0:
                pe.wait_ge(exc_ok, m * 4 + 4)
                if not first:
                    pe.wait_ge(y_ev, m * 1)
                nc.tensor.matmul(PS[:, 6, :], dg, uS, start=True, stop=False)
            pe.wait_ge(r_chain, n * 11 + 11)
            nc.tensor.matmul(PS[:, 6, :], exc[:, 0, t, :], xS[t % 2][:, 0, :], start=False, stop=False)
            nc.tensor.matmul(PS[:, 6, :], exc[:, 1, t, :], xS[t % 2][:, 1, :], start=False, stop=(t == 3)).then_inc(y_ok, 1)

        tab_chain = sem("tab_chain")
        half_pi_sb = sb("half_pi", [P, 1])
        half_pi = half_pi_sb[:, 0:1]

        def pe_s5(pe, m, first):
            def hook(s):
                if s == 0:
                    if not first:
                        pe_y(pe, m - 1, 3, False)
                    pe_xt(pe, m, 0, first)
                if s == 1:
                    pe_xt(pe, m, 1, first)
                if s in (2, 3):
                    pe_bu(pe, m, s - 2, first)
                if s in (4, 5):
                    pe_y(pe, m, s - 4, first)
                    pe_bu(pe, m, s - 2, first)
                if s == 7:
                    pe_y(pe, m, 2, first)
            return hook

        def act_s5(act, m, first):
            def hook(s):
                if s == 0:
                    act_tab(act, m, 0, first)
                if s == 3:
                    act_xt(act, m, 1)
                    act_tab(act, m, 1, first)
                if s in (4, 5):
                    act_eb(act, m, s - 4, first)
                if s == 5:
                    act_tab(act, m, 2, first)
                if s == 6:
                    act_eb(act, m, 2, first)
                    act_tab(act, m, 3, first)
                if s == 7:
                    act_eb(act, m, 3, first)

            def after_evac():
                act_xt(act, m, 0)
                if not first:
                    act_yev(act, m)
            return hook, after_evac

        def dve_s5(dve, m, first):
            def hook(s):
                if s == 0:
                    dve_f(dve, m, 0, first)
                if s == 2:
                    dve_f(dve, m, 1, first)
                if s == 3:
                    dve_r(dve, m, 0, first)
                if s == 4:
                    dve_f(dve, m, 2, first)
                    dve_r(dve, m, 1, first)
                if s == 5:
                    dve_f(dve, m, 3, first)
                if s == 6:
                    dve_r(dve, m, 2, first)
                if s == 7:
                    dve_r(dve, m, 3, first)
            return hook


        gD = dram("gD", (2560, T))
        selD = a["c_sel"]
        g_in, g_silu, g_out = sem("g_in"), sem("g_silu"), sem("g_out")
        zin, gelu_ok, zhi_ok, zlo_ok, zg_ok = sem("zin"), sem("gelu_ok"), sem("zhi_ok"), sem("zlo_ok"), sem("zg_ok")
        sig_ok, mixs = sem("sig_ok"), sem("mixs")
        fin_, fch = sem("f_in"), sem("fch")
        zS = S[:, 0:4096].rearrange("p (k t) -> p k t", k=8)
        gsS = S[:, 4096:8192].rearrange("p (k t) -> p k t", k=8)
        gb = [S[:, 8192 + 2048 * r:10240 + 2048 * r].rearrange("p (k t) -> p k t", k=4) for r in range(2)]
        sgS = [S[:, 12288 + 512 * r:12800 + 512 * r] for r in range(2)]
        yvS = [S[:, 13312 + 512 * r:13824 + 512 * r] for r in range(2)]
        flS, lnS = S[0:8, 14336:14848], S[0:8, 14848:15360]
        mnS = S[0:8, 15360:15872]
        fb = small[0:8, 24:25]

        def pool_gate_batch(pool, k, src, row):
            if k >= 2:
                pool.wait_ge(g_out, 16 * (k - 1))
            pool.dma_start(gb[k % 2], src.rearrange("(f p) t -> p f t", p=P)).then_inc(g_in, 16)
            pool.wait_ge(g_silu, k + 1)
            pool.dma_start(gD[row:row + 512, :].rearrange("(f p) t -> p f t", p=P), gb[k % 2]).then_inc(g_out, 16)

        def act_gate_batch(act, k):
            act.wait_ge(g_in, 16 * (k + 1))
            nc.scalar.activation(gb[k % 2], gb[k % 2], ACT.Silu).then_inc(g_silu, 1)

        def act_z(act, s):
            if s in (1, 3):
                k = 4 * (s // 2)
                if s == 1:
                    act.wait_ge(zin, 64)
                nc.scalar.activation(zS[:, k:k + 4, :], zS[:, k:k + 4, :], ACT.Gelu_apprx_tanh).then_inc(gelu_ok, 1)
            if s in (4, 5):
                k = 4 * (s - 4)
                nc.scalar.activation(gsS[:, k:k + 4, :], gsS[:, k:k + 4, :], ACT.Silu).then_inc(gelu_ok, 1)
            if s in (6, 7):
                k = 4 * (s - 6)
                if s == 6:
                    act.wait_ge(gelu_ok, 4)
                nc.scalar.activation(A[:, 32 + k:36 + k, :], zS[:, k:k + 4, :], ACT.Copy).then_inc(zhi_ok, 1)

        def dve_z(dve):
            dve.wait_ge(slot_used, GLU["slot0"])
            for k in range(8):
                dve.wait_ge(zhi_ok, 1 + k // 4)
                nc.vector.tensor_tensor(A[:, 8 + k, :], zS[:, k, :], A[:, 32 + k, :].bitcast(F32), ALU.subtract).then_inc(zlo_ok, 1)
            dve.wait_ge(zlo_ok, 8)
            dve.wait_ge(gelu_ok, 4)
            nc.vector.tensor_tensor(S[:, 4096:8192], S[:, 0:4096], S[:, 4096:8192], ALU.mult).then_inc(zg_ok, 1)

        def act_glu(act, c):
            act.wait_ge(slot_used, GLU["slot0"] + 4 * (c + 1))
            for f in range(4):
                k = 4 * c + f
                if k >= 2:
                    act.wait_ge(mixs, 3 * (k - 2) + 1)
                nc.scalar.activation(sgS[k % 2], PS[:, f, :], ACT.Sigmoid).then_inc(banks_free, 1)

        def dve_glu(dve, c):
            for f in range(4):
                k = 4 * c + f
                dve.wait_ge(banks_free, GLU["bank0"] + k + 1)
                if k == 0:
                    dve.wait_ge(zg_ok, 1)
                if k >= 2:
                    dve.wait_ge(mixs, 3 * (k - 1))
                nc.vector.tensor_tensor(yvS[k % 2], sgS[k % 2], gsS[:, k, :], ALU.mult).then_inc(mixs, 1)
                dve.wait_ge(mixs, 3 * k + 1)
                nc.vector.tensor_copy(A[:, k, :], yvS[k % 2]).then_inc(mixs, 1)
                dve.wait_ge(mixs, 3 * k + 2)
                nc.vector.tensor_tensor(A[:, KM + k, :], yvS[k % 2], A[:, k, :].bitcast(F32), ALU.subtract).then_inc(mixs, 1)

        def act_forget(act):
            act.wait_ge(fin_, 32)
            nc.scalar.activation(lnS, flS, ACT.Abs, bias=fb).then_inc(fch, 1)
            act.wait_ge(fch, 1)
            nc.scalar.activation(lnS, lnS, ACT.Exp, scale=-1.0).then_inc(fch, 1)
            act.wait_ge(fch, 2)
            nc.scalar.activation(lnS, lnS, ACT.Ln, bias=one_sb[0:8, 0:1]).then_inc(fch, 1)

        def dve_forget(dve):
            nc.vector.memset(negcum, 0.0).then_inc(fch2, 1)
            dve.wait_ge(fin_, 32)
            nc.vector.tensor_scalar(mnS, flS, fb, 0.0, ALU.add, ALU.min).then_inc(fch2, 1)
            dve.wait_ge(fch, 3)
            dve.wait_ge(fch2, 2)
            nc.vector.tensor_tensor(mnS, mnS, lnS, ALU.subtract).then_inc(fch2, 1)
            dve.wait_ge(fch2, 3)
            nc.vector.tensor_tensor_scan(mnS, one_sb[0:8, 0:1].broadcast_to([8, T]), mnS, 0.0, ALU.mult, ALU.add).then_inc(fch2, 1)
            dve.wait_ge(fch2, 4)
            nc.vector.tensor_scalar(negcum[0:8, :], mnS, -(128.0 ** 0.5), None, ALU.mult).then_inc(cum_ok, 1)

        fch2 = sem("fch2")
        one_sb = sb("one", [P, 1])

        x_in = [sem(f"x_in{t}") for t in range(4)]

        def dve_out(dve, j, c, h0):
            for t in range(4):
                dve.wait_ge(slot_used, j["slot0"] + j["spc"] * (c + 1))
                if c == 0:
                    dve.wait_ge(x_in[t], h0)
                dst = hrows[:, t, c * COLS:(c + 1) * COLS]
                nc.vector.tensor_tensor(dst, PS[:, t, :], dst, ALU.add).then_inc(banks_free, 1)

        S5C = 2

        maskneg = sb("maskneg", [P, P])
        stats = sb("stats", [P, 16])

        def s_tile(o, k=1):
            return S[:, o:o + 512 * k]

        class Att:

            def __init__(self, name, upp, units, tile0, n_heads, base, n_in, in_off, vt, scale, after=None):
                self.name, self.upp, self.units, self.tile0, self.heads = name, upp, units, tile0, n_heads
                self.pairs = n_heads // 2
                self.uph = upp // 2
                self.scale = scale
                self.vt = vt
                self.inp = [[s_tile(in_off + 512 * (n_in * r + i)) for i in range(n_in)] for r in range(2)]
                o = base
                nv = max(1, len(vt))
                self.v = [s_tile(o + 512 * nv * r, nv).rearrange("p (s j d) -> p s j d", s=nv, j=4) for r in range(2)]
                o += 1024 * nv
                self.p = [s_tile(o + 512 * r) for r in range(4)]
                o += 2048
                self.pt = [s_tile(o + 512 * r) for r in range(2)]
                o += 1024
                self.tmp = [s_tile(o + 512 * r) for r in range(2)]
                self.end = o + 1024
                self.b0 = after.b0 + after.pairs if after else 0
                self.tile0 -= 2 * self.b0
                self.sc, self.mx0, self.mx, self.ex = (after.sc, after.mx0, after.mx, after.ex) if after else [
                    sem(f"{name}_{n}") for n in ("scores", "max_step", "max", "exp")]
                self.rc, self.nr, self.tr, self.ev = (after.rc, after.nr, after.tr, after.ev) if after else [
                    sem(f"{name}_{n}") for n in ("reciprocal", "normed", "turned", "turned_out")]
                self.pv, self.vtp, self.vte = (after.pv, after.vtp, after.vte) if after else [
                    sem(f"{name}_{n}") for n in ("values", "v_turned", "v_out")]
                self.fin0, self.fin1, self.fin = (after.fin0, after.fin1, after.fin) if after else [
                    sem(f"{name}_{n}") for n in ("gated", "head_high", "head_low")]
                self.ld = after.ld if after else [sem(f"{name}_ld{r}") for r in range(2)]
                self.ld0 = after.ld0 + after.ld_inc * after.pairs if after else 0
                self.done = 2 * self.b0 + n_heads

        def num(b, k, c):
            return b * k + c

        def known_negative(b, k, c):
            return isinstance(b, int) and b * k + c <= 0

        def wait(eng, s_, b, k, c):
            if not known_negative(b, k, c):
                eng.wait_ge(s_, b * k + c)

        SB = (0, 1, 4, 5)
        TB = (2, 6)
        OB = (3, 7)

        def unit(t, x):
            return t.units[x % t.uph]

        def pe_scores(pe, t, b, x):
            u = unit(t, x)
            r = (x // t.uph) % 2
            bank = PS[:, SB[x % 4], :]
            if x % t.uph == 0:
                pe.wait_ge(t.ld[r], b * t.ld_inc + (t.ld_inc * (1 - t.b0) + t.ld0))
            wait(pe, t.mx if u["bias"] else t.ex, b, t.upp, x - 3)
            u["score"](pe, bank, r, b, x)

        def dve_max(dve, t, b, x):
            u = unit(t, x)
            r = (x // t.uph) % 2
            w = u["w"]
            bank = PS[:, SB[x % 4], 0:w]
            c = x % 4
            dve.wait_ge(t.sc, num(b, t.upp, x + 1))
            wait(dve, t.ex, b, t.upp, x - 3)
            src = bank
            if u["bias"]:
                wait(dve, t.tr, b, t.upp, x - 3)
                nc.vector.scalar_tensor_tensor(t.p[x % 4][:, 0:w], bank, t.scale, u["bias"](r), ALU.mult, ALU.add).then_inc(t.mx0, 1)
                dve.wait_ge(t.mx0, num(b, t.upp * 2, 2 * x + 1))
                nc.vector.tensor_reduce(stats[:, c:c + 1], t.p[x % 4][:, 0:w], AX, ALU.max, negate=True).then_inc(t.mx0, 1)
                dve.wait_ge(t.mx0, num(b, t.upp * 2, 2 * x + 2))
                nc.vector.tensor_scalar(stats[:, 4 + c:5 + c], stats[:, c:c + 1], 1.0, None, ALU.mult).then_inc(t.mx, 1)
            else:
                nc.vector.tensor_reduce(stats[:, c:c + 1], bank, AX, ALU.max, negate=True).then_inc(t.mx0, 1)
                dve.wait_ge(t.mx0, num(b, t.upp, x + 1))
                nc.vector.tensor_scalar(stats[:, 4 + c:5 + c], stats[:, c:c + 1], t.scale, None, ALU.mult).then_inc(t.mx, 1)

        def act_exp(act, t, b, x):
            u = unit(t, x)
            w, c = u["w"], x % 4
            act.wait_ge(t.mx, num(b, t.upp, x + 1))
            wait(act, t.tr, b, t.upp, x - 3)
            wait(act, t.nr, b, t.upp, x - 3)
            if u["bias"]:
                nc.scalar.activation(t.p[x % 4][:, 0:w], t.p[x % 4][:, 0:w], ACT.Exp, bias=stats[:, 4 + c:5 + c],
                                     accum_out=stats[:, 8 + c:9 + c]).then_inc(t.ex, 1)
            else:
                nc.scalar.activation(t.p[x % 4][:, 0:w], PS[:, SB[x % 4], 0:w], ACT.Exp, bias=stats[:, 4 + c:5 + c],
                                     scale=t.scale, accum_out=stats[:, 8 + c:9 + c]).then_inc(t.ex, 1)

        def dve_norm_p(dve, t, b, x):
            u = unit(t, x)
            w, c = u["w"], x % 4
            dve.wait_ge(t.ex, num(b, t.upp, x + 1))
            wait(dve, t.nr, b, t.upp, x)
            nc.vector.reciprocal(stats[:, 12 + c:13 + c], stats[:, 8 + c:9 + c]).then_inc(t.rc, 1)
            dve.wait_ge(t.rc, num(b, t.upp, x + 1))
            if u["gate"]:
                u["gate"](dve, t, b, x, w, c)
            else:
                nc.vector.tensor_scalar(t.p[x % 4][:, 0:w], t.p[x % 4][:, 0:w], stats[:, 12 + c:13 + c], None,
                                        ALU.mult).then_inc(t.nr, 1)

        def pe_turn(pe, t, b, x):
            u = unit(t, x)
            pe.wait_ge(t.nr, num(b, t.upp, x + 1))
            wait(pe, t.ev, b, t.upp, x - 1)
            for j_ in range(u["nb"]):
                mm = nc.tensor.transpose(PS[:, TB[x % 2], j_ * P:j_ * P + P], t.p[x % 4][:, j_ * P:j_ * P + P], ident[:, :])
            mm.then_inc(t.tr, 1)

        def act_turned(act, t, b, x):
            u = unit(t, x)
            n = u["nb"] * P
            act.wait_ge(t.tr, num(b, t.upp, x + 1))
            wait(act, t.pv, b, t.upp, x - 1)
            nc.scalar.activation(t.pt[x % 2][:, 0:n], PS[:, TB[x % 2], 0:n], ACT.Copy).then_inc(t.ev, 1)

        def pe_values(pe, t, b, x):
            u = unit(t, x)
            r = (x // t.uph) % 2
            h0 = x // t.uph
            if x % t.uph == 0:
                if t.vt:
                    pe.wait_ge(t.vte, num(b, 2 * len(t.vt), (h0 + 1) * len(t.vt)))
                wait(pe, t.fin0, b, 2, h0 - 1)
            pe.wait_ge(t.ev, num(b, t.upp, x + 1))
            i = u["i"]
            for j_ in range(u["nb"]):
                mm = nc.tensor.matmul(PS[:, OB[r], i * P:i * P + P], u["v"](r, j_), t.pt[x % 2][:, j_ * P:j_ * P + P],
                                      start=(j_ == 0 and u["first"]), stop=(j_ == u["nb"] - 1 and u["last"]))
            mm.then_inc(t.pv, 1)

        def pe_vt(pe, t, b, h):
            if not t.vt:
                return
            r = h % 2
            pe.wait_ge(t.ld[r], b * t.ld_inc + (t.ld_inc * (1 - t.b0) + t.ld0))
            wait(pe, t.fin0, b, 2, h - 1)
            for k, src in enumerate(t.vt):
                if k:
                    pe.wait_ge(t.vte, num(b, 2 * len(t.vt), h * len(t.vt) + k))
                for j_ in range(4):
                    mm = nc.tensor.transpose(PS[:, OB[r], j_ * P:j_ * P + P], t.inp[r][src][:, j_ * P:j_ * P + P], ident[:, :])
                mm.then_inc(t.vtp, 1)

        def act_vt(act, t, b, h):
            if not t.vt:
                return
            r = h % 2
            for k in range(len(t.vt)):
                act.wait_ge(t.vtp, num(b, 2 * len(t.vt), h * len(t.vt) + k + 1))
                nc.scalar.activation(t.v[r][:, k, :, :], PS[:, OB[r], :].rearrange("p (j d) -> p j d", j=4), ACT.Copy).then_inc(t.vte, 1)

        def dve_finish(dve, t, b, h):
            r = h % 2
            tile = num(b, 2, t.tile0 + h)
            dve.wait_ge(t.pv, num(b, t.upp, t.uph * (h + 1)))
            wait(dve, t.fin, b, 2, h - 1)
            nc.vector.tensor_tensor(t.tmp[r], PS[:, OB[r], :], t.inp[r][-1], ALU.mult).then_inc(t.fin0, 1)
            dve.wait_ge(t.fin0, num(b, 2, h + 1))
            nc.vector.tensor_copy(A[:, ds(tile, 1), :], t.tmp[r].unsqueeze(1)).then_inc(t.fin1, 1)
            dve.wait_ge(t.fin1, num(b, 2, h + 1))
            nc.vector.tensor_tensor(A[:, ds(tile + KM, 1), :], t.tmp[r].unsqueeze(1), A[:, ds(tile, 1), :].bitcast(F32),
                                    ALU.subtract).then_inc(t.fin, 1)

        def run_pairs(eng, t, body):
            body(t.b0, range(0, t.upp))
            with eng.Fori(t.b0 + 1, t.b0 + t.pairs) as b:
                body(b, range(0, t.upp))
            body(t.b0 + t.pairs, range(0, 4), tail=True)

        def pe_att(pe, t):
            def body(b, xs, tail=False):
                first = isinstance(b, int) and b == t.b0
                for x in xs:
                    if not tail:
                        if x % t.uph == 0:
                            pe_vt(pe, t, b, x // t.uph)
                        pe_scores(pe, t, b, x)
                    if x >= 2 or not first:
                        if not (tail and x >= 2):
                            pe_turn(pe, t, b, x - 2)
                    if x >= 3 or not first:
                        if not (tail and x >= 3):
                            pe_values(pe, t, b, x - 3)
            run_pairs(pe, t, body)

        def dve_att(dve, t):
            def body(b, xs, tail=False):
                first = isinstance(b, int) and b == t.b0
                for x in xs:
                    if not tail:
                        dve_max(dve, t, b, x)
                    if x >= 1 or not first:
                        if not (tail and x >= 1):
                            dve_norm_p(dve, t, b, x - 1)
                    if x % t.uph == 3 and (x > 3 or not first) and not (tail and x > 3):
                        dve_finish(dve, t, b, x // t.uph - 1)
            run_pairs(dve, t, body)

        def act_att(act, t):
            def body(b, xs, tail=False):
                first = isinstance(b, int) and b == t.b0
                for x in xs:
                    if not tail:
                        if x % t.uph == 0:
                            act_vt(act, t, b, x // t.uph)
                        act_exp(act, t, b, x)
                    if x >= 2 or not first:
                        if not (tail and x >= 2):
                            act_turned(act, t, b, x - 2)
            run_pairs(act, t, body)

        def pool_att(pool, t, load):
            def one(b, h):
                wait(pool, t.pv, b, t.upp, (h - 1) * t.uph)
                wait(pool, t.fin0, b, 2, h - 1)
                load(pool, num(b, 2, h - 2 * t.b0), h % 2, t.ld[h % 2])
            for h in range(2):
                one(t.b0, h)
            with pool.Fori(t.b0 + 1, t.b0 + t.pairs) as b:
                for h in range(2):
                    one(b, h)

        def causal_mask(bank, w):
            return nc.tensor.matmul(bank[:, w - P:w], ident[:, :], maskneg[:, :], start=False, stop=True)

        def blocks(score, v, bias=None, gate=None, full=None):
            return [dict(i=i, w=full or (i + 1) * P, nb=(full or (i + 1) * P) // P, score=score(i), v=v, bias=bias, gate=gate,
                         first=True, last=True) for i in range(4)]

        INV_SQ = 128.0 ** -0.5

        negcum = S[:, 15872:16384]

        def fox_score(i):
            def score(pe, bank, r, b, x):
                w = (i + 1) * P
                h0 = x // 4
                if x == 0 and isinstance(b, int):
                    pe.wait_ge(cum_ok, 1)
                q, k = FOX.inp[r][0], FOX.inp[r][1]
                nc.tensor.matmul(bank[:, 0:w], q[:, i * P:i * P + P], k[:, 0:w], start=True, stop=False)
                nc.tensor.matmul(bank[:, 0:w], selS[r], negcum[:, 0:w], start=False, stop=False)
                causal_mask(bank, w).then_inc(FOX.sc, 1)
            return score

        cum_ok = sem("cum_ok")
        FOX = Att("fox", 8, blocks(fox_score, lambda r, j_: FOX.v[r][:, 0, j_, :]), 8, 8, 0, 4, 8192, (2,), INV_SQ)
        FOX.ld_inc = 80
        selS = [s_tile(FOX.end + 128 * r)[:, 0:P] for r in range(2)]

        def fox_load(pool, h, r, s_):
            q, k, v, g = FOX.inp[r]
            pool.dma_start(q, yE[ds(h * P + 2048, P), :]).then_inc(s_, 16)
            pool.dma_start(k, yE[ds(h * P + 3072, P), :]).then_inc(s_, 16)
            pool.dma_start(v, yE[ds(h * P + 4096, P), :]).then_inc(s_, 16)
            pool.dma_start(g, gD[ds(h * P, P), :]).then_inc(s_, 16)
            pool.dma_start(selS[r], selD[ds(h, 1), :, :].rearrange("a p n -> (a p) n")).then_inc(s_, 16)

        def mem_att(name, l, y, q_row, g_row, after=None):
            def mem_score(i):
                def score(pe, bank, r, b, x):
                    q, k = t.inp[r][0], t.inp[r][1]
                    nc.tensor.matmul(bank[:, 0:NMEM], q[:, i * P:i * P + P], k[:, 0:NMEM], start=True, stop=True).then_inc(t.sc, 1)
                return score

            t = Att(name, 8, blocks(mem_score, lambda r, j_: t.v[r][:, 0, j_, :], full=NMEM), 16, 4, 8192 - 1024, 3, 4096, (), INV_SQ, after)
            t.ld_inc = 64

            def load(pool, h, r, s_):
                q, k, g = t.inp[r]
                pool.dma_start(q, y[ds(h * P + q_row, P), :]).then_inc(s_, 16)
                pool.dma_start(k[:, 0:NMEM], kmD[l][ds(h * P, P), :]).then_inc(s_, 16)
                pool.dma_start(g, gD[ds(h * P + g_row, P), :]).then_inc(s_, 16)
                pool.dma_start(t.v[r][:, 0, 0:2, :], vmD[l][:, ds(h * P, P)].rearrange("(j p) d -> p j d", p=P)).then_inc(s_, 16)
            return t, load

        MEM0, mem0_load = mem_att("mem0", 0, yE, 6152, 1024)

        h1D = dram("h1D", (T, D))
        biasD = dram("biasD", (8, P, LB))
        quD = dram("quD", (1536, T))
        kvD = dram("kvD", (2048, T))
        kcD = dram("kcD", (2, P, NPAD))
        vcD = dram("vcD", (2, P, P))
        h1_out = sem("h1_out")
        t5c = sb("t5c", [P, 33 * 8 + 8])
        thr = sb("thr", [P, 33])
        pec = sb("pec", [P, 2, 32])
        cols = sb("cols", [P, 16])
        ones = sb("ones", [P, P])
        posi = small[:, 32:36].bitcast(I32)
        const_in, const_ok = sem("const_in"), sem("const_ok")
        OFF = [0, 160, 448, 864]
        accS = S[:, 0:8 * LB].rearrange("p (h n) -> p h n", h=8)
        distS = S[:, 11264:11264 + LB]
        termS = [S[:, 12672 + LB * r:12672 + LB * (r + 1)] for r in range(2)]
        indS = S[:, 15488:15488 + 704].bitcast(mybir.dt.bfloat16)
        poskS = termS[0][:, 0:512]
        poskI = termS[1][:, 0:512].bitcast(I32)
        tabS = termS[1][:, 512:768]
        t5_in, t5_step, t5_ind, t5_acc, t5_term, t5_add, t5_out = [sem(n) for n in
            ("t5_in", "t5_step", "t5_ind", "t5_acc", "t5_term", "t5_add", "t5_out")]
        cm01 = sb("cm01", [P, 4, NPAD])
        cmneg = sb("cmneg", [P, 4, NPAD])
        HV = 5

        def pool_consts(pool):
            pool.dma_start(thr[:, 0:31], a["c_thr"]).then_inc(const_in, 16)
            pool.dma_start(cols[:, 0:1], a["c_inv"]).then_inc(const_in, 16)
            pool.dma_start(cols[:, 1:2], a["c_sgn"]).then_inc(const_in, 16)
            pool.dma_start(posi, a["positions"][0].rearrange("(i p) -> p i", p=P)).then_inc(const_in, 16)
            pool.dma_start(cols[:, 8:12], a["mla_g_cq"][0].rearrange("(k p) -> p k", p=P)).then_inc(const_in, 16)
            pool.dma_start(cols[:, 12:16], a["mla_g_ckv"][0].rearrange("(k p) -> p k", p=P)).then_inc(const_in, 16)
            pool.dma_start(pec[:, :, :], a["nsa_cmp_pe"][0].rearrange("k l d -> d k l")).then_inc(const_in, 16)
            nc.gpsimd.memset(thr[:, 31:33], 1e30).then_inc(const_ok, 1)
            nc.gpsimd.memset(ones[:, :], 1.0).then_inc(const_ok, 1)
            nc.gpsimd.memset(cm01[:, :, :], 1.0).then_inc(const_ok, 1)
            nc.gpsimd.memset(cmneg[:, :, :], 0.0).then_inc(const_ok, 1)
            pool.wait_ge(const_ok, 4)
            for m_, fill in ((cm01, 0.0), (cmneg, NEG)):
                nc.gpsimd.affine_select(out=m_[:, :, :], in_=m_[:, :, :], compare_op=ALU.is_ge, fill=fill, base=-31,
                                        pattern=[[P, 4], [-16, NPAD]], channel_multiplier=1).then_inc(const_ok, 1)
            pool.wait_ge(const_ok, 6)

        def pool_t5_loads(pool):
            pool.wait_ge(nt_pe, 3 * KD)
            pool.dma_start(poskI, a["positions"].broadcast_to([P, T])).then_inc(t5_in, 16)
            pool.dma_start(tabS, a["t5_table"].rearrange("(a b) h -> a (b h)", a=1).broadcast_to([P, 256])).then_inc(t5_in, 16)

        def dve_t5_start(dve):
            dve.wait_ge(t5_in, 32)
            dve.wait_ge(const_in, 7 * 16)
            dve.wait_ge(const_ok, 6)
            nc.vector.tensor_copy(poskS, poskI).then_inc(t5_step, 1)
            nc.vector.tensor_copy(cols[:, 4:8], posi).then_inc(t5_step, 1)
            nc.vector.memset(t5c[:, 248:264], 0.0).then_inc(t5_step, 1)
            nc.vector.tensor_tensor(t5c[:, 0:248], tabS[:, 8:256], tabS[:, 0:248], ALU.subtract).then_inc(t5_step, 1)
            nc.vector.tensor_copy(t5c[:, 264:272], tabS[:, 0:8]).then_inc(t5_step, 1)
            dve.wait_ge(t5_step, 5)
            for i in range(4):
                w = (i + 1) * P
                q = cols[:, 4 + i:5 + i]
                for dst, src in ((distS[:, OFF[i]:OFF[i] + w], poskS[:, 0:w]),
                                 (distS[:, OFF[i] + w:OFF[i] + w + 31], poskS[:, 31:512:16]),
                                 (distS[:, OFF[i] + w + 31:OFF[i] + w + 32], poskS[:, 511:512])):
                    nc.vector.tensor_scalar(dst, src, q, -1.0, ALU.subtract, ALU.mult).then_inc(t5_step, 1)
            dve.wait_ge(t5_step, 17)
            for h in range(8):
                nc.vector.tensor_scalar(accS[:, h, :], distS, 0.0, t5c[:, 264 + h:265 + h], ALU.mult, ALU.add).then_inc(t5_step, 1)
            dve.wait_ge(t5_step, 25)

        def dve_t5_ind(dve, c, k, first):
            if not (first and k == 0):
                dve.wait_ge(t5_term, num(c, 9, 3 * k - 9))
                dve.wait_ge(t5_acc, num(c, 3 * HV, HV * k - 3 * HV))
            nc.vector.tensor_scalar(indS, distS, thr[:, ds(c * 3 + (k - 3), 1)], None, ALU.is_ge).then_inc(t5_ind, 1)

        def dve_t5_acc(dve, c, k, h):
            if h == 0:
                dve.wait_ge(t5_ind, num(c, 3, k - 2))
            if not (isinstance(c, int) and c == 1 and k == 0):
                dve.wait_ge(t5_acc, num(c, 3 * HV, HV * k + h - 4 * HV + 1))
            nc.vector.scalar_tensor_tensor(accS[:, h, :], indS, t5c[:, ds(c * 24 + (8 * k + h - 24), 1)], accS[:, h, :],
                                           ALU.mult, ALU.add).then_inc(t5_acc, 1)

        T5BUF = [termS[0], termS[1], termS[0]]

        def act_t5_term(act, c, k, j_, first):
            act.wait_ge(t5_ind, num(c, 3, k - 2))
            back = (0, 2, 1)[j_]
            if not (first and 3 * k + j_ - back <= 0):
                act.wait_ge(t5_add, num(c, 9, 3 * k + j_ - 9 - back))
            nc.scalar.activation(T5BUF[j_], indS, ACT.Copy, scale=t5c[:, ds(c * 24 + (8 * k + HV + j_ - 24), 1)]).then_inc(t5_term, 1)

        def pool_t5_add(pool, c, k, j_):
            pool.wait_ge(t5_term, num(c, 9, 3 * k + j_ - 8))
            nc.gpsimd.tensor_tensor(accS[:, HV + j_, :], accS[:, HV + j_, :], T5BUF[j_], ALU.add).then_inc(t5_add, 1)

        def dve_t5_hook(dve, c, first):
            todo = [[("i", 0), (0, 0)], [(0, 1), (0, 2)], [(0, 3), (0, 4)], [("i", 1), (1, 0), (1, 1)], [(1, 2), (1, 3), (1, 4)],
                    [("i", 2), (2, 0), (2, 1)], [(2, 2), (2, 3)], [(2, 4)]]

            def hook(s):
                for k, h in todo[s]:
                    if k == "i":
                        dve_t5_ind(dve, c, h, first)
                    else:
                        dve_t5_acc(dve, c, k, h)
            return hook

        def act_t5_hook(act, c, first):
            todo = [[], [(0, 0)], [(0, 1)], [(0, 2)], [(1, 0)], [(1, 1), (1, 2)], [(2, 0)], [(2, 1), (2, 2)]]

            def hook(s):
                for k, j_ in todo[s]:
                    act_t5_term(act, c, k, j_, first)
            return hook

        def dve_t5_end(dve):
            dve.wait_ge(t5_add, 99)
            dve.wait_ge(t5_acc, 33 * HV)
            for i in range(4):
                w = (i + 1) * P
                for o, n, m_ in ((OFF[i] + w - P, P, maskneg[:, :]), (OFF[i] + w, NPAD, cmneg[:, i, :])):
                    v = accS[:, :, o:o + n]
                    nc.vector.tensor_tensor(v, v, m_.unsqueeze(1).broadcast_to([P, 8, n]), ALU.add).then_inc(t5_step, 1)

        XS = [S[:, 2048 * k:2048 * k + 2048].rearrange("p (g n l) -> p g n l", g=2, n=32) for k in range(2)]
        rawS = [S[:, 4096 + 1024 * k:5120 + 1024 * k].rearrange("p (g t) -> p g t", g=2) for k in range(2)]
        w1S = [S[:, 6144 + 2048 * r:8192 + 2048 * r].rearrange("p (l h) -> p l h", l=8) for r in range(2)]
        cS = S[:, 10240:14336].rearrange("p (k t) -> p k t", k=8)
        sqS = [S[:, 14336 + 512 * r:14848 + 512 * r] for r in range(2)]
        rrS = [S[:, 15360 + 512 * r:15872 + 512 * r] for r in range(2)]
        w2S = S[:, 4096:4608].rearrange("p (k h d) -> p k h d", k=2, h=2)
        hcS = S[:, 4608:4864].rearrange("p (k h n) -> p k h n", k=2, h=2)
        vcS = S[:, 4864:5120].rearrange("p (g d) -> p g d", g=2)
        kcS = S[:, 5120:5184].rearrange("p (g n) -> p g n", g=2)
        c_in, cmp_in, w1_in, w1_used, x_ok = sem("c_in"), sem("cmp_in"), [sem(f"w1_in{r}") for r in range(2)], sem("w1_used"), sem("x_ok")
        sq_ok, ss_pe, rr_step, rr_root, cn_step, cn_ok = [sem(n) for n in ("sq_ok", "ss_pe", "rr_step", "rr_root", "cn_step", "cn_ok")]
        cmp_g, w2_in, vc_zero, cmp2_pe, cmp2_ok, cmp_out = [sem(n) for n in ("cmp_g", "w2_in", "vc_zero", "cmp2_pe", "cmp2_ok", "cmp_out")]

        def pool_c(pool):
            pool.wait_ge(t5_out, 16)
            for k in range(2):
                pool.dma_start(cS[:, 4 * k:4 * k + 4, :], yO[512 * k:512 * k + 512, :].rearrange("(f p) t -> p f t", p=P)).then_inc(c_in, 16)
            for k in range(2):
                pool.dma_start(rawS[k], yO[3136 + 256 * k:3392 + 256 * k, :].rearrange("(g p) t -> p g t", p=P)).then_inc(cmp_in, 16)
            w1 = a["nsa_cmp_w1"][0]
            for n in range(8):
                if n >= 2:
                    pool.wait_ge(w1_used, n - 1)
                r0 = (n % 4) * 1024
                pool.dma_start(w1S[n % 2], w1[n // 4, r0:r0 + 1024, :].rearrange("(l d) h -> d l h", d=P)).then_inc(w1_in[n % 2], 16)
                if n == 1:
                    pool.wait_ge(x_ok, 4)
                    nc.gpsimd.memset(vcS, 0.0).then_inc(vc_zero, 1)
                    pool.dma_start(w2S, a["nsa_cmp_w2"][0].rearrange("k (h q) d -> q k h d", q=P)).then_inc(w2_in, 16)
            pool.wait_ge(cmp2_ok, 3)
            pool.dma_start(kcD.rearrange("g p n -> p g n"), kcS).then_inc(cmp_out, 16)
            pool.dma_start(vcD.rearrange("g p d -> p g d"), vcS).then_inc(cmp_out, 16)
            pool.wait_ge(cmp_out, 32)

        def dve_c(dve):
            dve.wait_ge(cmp_in, 32)
            for k in range(2):
                raw, pe_ = rawS[k], pec[:, k, :]
                rv = bass.AP(tensor=raw.tensor, offset=raw.offset, ap=[raw.ap[0], [512, 2], [16, 31], [1, 32]])
                pv = bass.AP(tensor=pe_.tensor, offset=pe_.offset, ap=[pe_.ap[0], [0, 2], [0, 31], [1, 32]])
                nc.vector.tensor_tensor(XS[k][:, :, 0:31, :], rv, pv, ALU.add).then_inc(x_ok, 1)
                nc.vector.memset(XS[k][:, :, 31, :], 0.0).then_inc(x_ok, 1)
            for k in range(2):
                var, r = rrS[k], sqS[k]
                n0 = 6 * k
                dve.wait_ge(ss_pe, 8)
                nc.vector.tensor_scalar(var, PS[:, 6 + k, :], 1.0 / 512, EPS, ALU.mult, ALU.add).then_inc(rr_step, 1)
                dve.wait_ge(rr_root, k + 1)
                nc.vector.reciprocal(r, r).then_inc(rr_step, 1)
                dve.wait_ge(rr_step, n0 + 2)
                nc.vector.tensor_tensor(var, var, r, ALU.mult).then_inc(rr_step, 1)
                dve.wait_ge(rr_step, n0 + 3)
                nc.vector.tensor_tensor(var, var, r, ALU.mult).then_inc(rr_step, 1)
                dve.wait_ge(rr_step, n0 + 4)
                nc.vector.tensor_scalar(var, var, -0.5, 1.5, ALU.mult, ALU.add).then_inc(rr_step, 1)
                dve.wait_ge(rr_step, n0 + 5)
                nc.vector.tensor_tensor(r, r, var, ALU.mult).then_inc(rr_step, 1)
            dve.wait_ge(rr_step, 12)
            dve.wait_ge(slot_used, UQ["slot0"])
            for k in range(8):
                v = cS[:, k, :]
                nc.vector.scalar_tensor_tensor(v, v, cols[:, 8 + k:9 + k], sqS[k // 4], ALU.mult, ALU.mult).then_inc(cn_step, 1)
                dve.wait_ge(cn_step, 2 * k + 1)
                nc.vector.tensor_copy(A[:, 32 + k, :], v).then_inc(cn_step, 1)
                dve.wait_ge(cn_step, 2 * k + 2)
                nc.vector.tensor_tensor(A[:, 8 + k, :], v, A[:, 32 + k, :].bitcast(F32), ALU.subtract).then_inc(cn_ok, 1)

        def dve_c2(dve):
            dve.wait_ge(cmp2_pe, 2)
            nc.vector.tensor_copy(kcS, PS[:, 4, 0:64].rearrange("p (g n) -> p g n", g=2)).then_inc(cmp2_ok, 1)
            dve.wait_ge(vc_zero, 1)
            for g in range(2):
                nc.vector.tensor_copy(vcS[0:NPAD, g, :], PS[0:NPAD, 5, g * P:g * P + P]).then_inc(cmp2_ok, 1)

        def act_c(act):
            act.wait_ge(c_in, 32)
            for k in range(8):
                if k >= 2:
                    act.wait_ge(ss_pe, k - 1)
                nc.scalar.activation(sqS[k % 2], cS[:, k, :], ACT.Square).then_inc(sq_ok, 1)
            for k in range(2):
                act.wait_ge(rr_step, 6 * k + 1)
                nc.scalar.activation(sqS[k], rrS[k], ACT.Sqrt).then_inc(rr_root, 1)

        def act_c2(act):
            for k in range(2):
                act.wait_ge(w1_used, 4 * k + 4)
                if k == 0:
                    act.wait_ge(x_ok, 4)
                for h in range(2):
                    nc.scalar.activation(hcS[:, k, h, :], PS[:, 4 + 2 * k + h, 0:64], ACT.Gelu_apprx_tanh).then_inc(cmp_g, 1)

        def pe_c(pe):
            for k in range(8):
                pe.wait_ge(sq_ok, k + 1)
                nc.tensor.matmul(PS[:, 6 + k // 4, :], ones[:, :], sqS[k % 2], start=(k % 4 == 0), stop=(k % 4 == 3)).then_inc(ss_pe, 1)
            pe.wait_ge(x_ok, 4)
            for k in range(2):
                if k == 1:
                    pe.wait_ge(rr_step, 7)
                for l in range(32):
                    n = 4 * k + l // 8
                    if l % 8 == 0:
                        pe.wait_ge(w1_in[n % 2], 16 * (n // 2 + 1))
                    for h in range(2):
                        mm = nc.tensor.matmul(PS[:, 4 + 2 * k + h, 0:64].rearrange("p (g n) -> p g n", g=2),
                                              w1S[n % 2][:, l % 8, h * P:h * P + P], XS[k][:, :, :, l], start=(l == 0), stop=(l == 31))
                    if l % 8 == 7:
                        mm.then_inc(w1_used, 1)

        def pe_c2(pe):
            pe.wait_ge(cmp_g, 4)
            pe.wait_ge(w2_in, 16)
            for h in range(2):
                mm = nc.tensor.matmul(PS[:, 4, 0:64], w2S[:, 0, h, :], hcS[:, 0, h, :], start=(h == 0), stop=(h == 1))
            mm.then_inc(cmp2_pe, 1)
            for g in range(2):
                for h in range(2):
                    mm = nc.tensor.matmul(PS[0:NPAD, 5, g * P:g * P + P], hcS[:, 1, h, g * NPAD:g * NPAD + NPAD], w2S[:, 1, h, :],
                                          start=(h == 0), stop=(h == 1))
            mm.then_inc(cmp2_pe, 1)

        GATES_O = [(1088, 0), (1600, 512), (4696, 1024), (5208, 1536), (6232, 2048)]

        def mla_score(i):
            def score(pe, bank, r, b, x):
                w = (i + 1) * P
                q, k = MLA.inp[r][0], MLA.inp[r][1]
                nc.tensor.matmul(bank[:, 0:w], q[:, i * P:i * P + P], k[:, 0:w], start=True, stop=False)
                if x % 4 == 0:
                    pe.wait_ge(rope_ok, num(b, 2, x // 4 + 2 - 2 * MLA.b0))
                nc.tensor.matmul(bank[:, 0:w], qrS[r][:, i * P:i * P + P], krS[:, 0:w], start=False, stop=False)
                causal_mask(bank, w).then_inc(MLA.sc, 1)
            return score

        MLA = Att("mla", 8, blocks(mla_score, lambda r, j_: MLA.v[r][:, 0, j_, :]), 0, 8, 0, 4, 5120, (2,), 192.0 ** -0.5, FOX)
        MLA.ld_inc = 64
        cosR, sinR = s_tile(9216), s_tile(9728)
        qrS = [s_tile(10240), s_tile(10752)]
        krS = s_tile(11264)
        qa, qb = [s_tile(11776), s_tile(12288)], [s_tile(12800), s_tile(13312)]
        angS, turnS = s_tile(13824), s_tile(14336)
        posrS, posrI = s_tile(14848), s_tile(15360).bitcast(I32)
        rope_ok, rope_in, rope_t, rope_tab, kr_in = sem("rope_ok"), sem("rope_in"), sem("rope_t"), sem("rope_tab"), sem("kr_in")
        rope_ld, rope_c = [sem(f"rope_ld{r}") for r in range(2)], sem("rope_c")

        def swapped(eng, dst_a, dst_b, src, s_):
            eng.dma_start(dst_a[0:64, :], src(0, 64)).then_inc(s_, 16)
            eng.dma_start(dst_b[0:32, :], src(32, 32)).then_inc(s_, 16)
            eng.dma_start(dst_b[32:64, :], src(0, 32)).then_inc(s_, 16)

        def pool_rope_start(pool):
            pool.dma_start(posrI, a["positions"].broadcast_to([P, T])).then_inc(rope_in, 16)
            swapped(pool, qa[0], qb[0], lambda o, n: yO[1024 + o:1024 + o + n, :], kr_in)
            for v in (krS, qrS[0], qrS[1]):
                nc.gpsimd.memset(v, 0.0).then_inc(rope_c, 1)

        def dve_rope(dve):
            dve.wait_ge(rope_in, 16)
            n = [0]

            def step(ins):
                n[0] += 1
                ins.then_inc(rope_t, 1)
                dve.wait_ge(rope_t, n[0])
            step(nc.vector.tensor_copy(posrS, posrI))
            step(nc.vector.tensor_scalar(angS, posrS, cols[:, 0:1], None, ALU.mult))
            step(nc.vector.tensor_scalar(turnS, angS, 1.0 / TWO_PI, MAGIC, ALU.mult, ALU.add))
            step(nc.vector.tensor_scalar(turnS, turnS, MAGIC, None, ALU.subtract))
            for cst in (C1, C2, C3):
                step(nc.vector.scalar_tensor_tensor(angS, turnS, -cst, angS, ALU.mult, ALU.add))
            step(nc.vector.tensor_scalar(angS, angS, -3.1415925, 3.1415925, ALU.max, ALU.min))
            dve.wait_ge(rope_tab, 3)
            step(nc.vector.tensor_scalar(sinR, sinR, cols[:, 1:2], None, ALU.mult))

        def act_rope(act):
            act.wait_ge(rope_t, 8)
            nc.scalar.activation(sinR, angS, ACT.Sin).then_inc(rope_tab, 1)
            nc.scalar.activation(cosR, angS, ACT.Abs).then_inc(rope_tab, 1)
            act.wait_ge(rope_tab, 2)
            nc.scalar.activation(cosR, cosR, ACT.Sin, scale=-1.0, bias=half_pi).then_inc(rope_tab, 1)

        def pool_rotate(pool, dst, xa, xb, ns):
            nc.gpsimd.tensor_tensor(xa[0:64, :], xa[0:64, :], cosR[0:64, :], ALU.mult).then_inc(rope_c, 1)
            nc.gpsimd.tensor_tensor(xb[0:64, :], xb[0:64, :], sinR[0:64, :], ALU.mult).then_inc(rope_c, 1)
            pool.wait_ge(rope_c, ns)
            nc.gpsimd.tensor_tensor(dst[0:64, :], xa[0:64, :], xb[0:64, :], ALU.add).then_inc(rope_ok, 1)

        def mla_load(pool, h, r, s_):
            static = isinstance(h, int)
            q, k, v, g = MLA.inp[r]
            pool.dma_start(q, quD[ds(h * 192, P), :]).then_inc(s_, 16)
            pool.dma_start(k, kvD[ds(h * 256, P), :]).then_inc(s_, 16)
            pool.dma_start(v, kvD[ds(h * 256 + P, P), :]).then_inc(s_, 16)
            pool.dma_start(g, gD[ds(h * P, P), :]).then_inc(s_, 16)
            pool.wait_ge(rope_ok, max(1, h) if static else h)
            swapped(pool, qa[r], qb[r], lambda o, n: quD[ds(h * 192 + P + o, n), :], rope_ld[r])
            pool.wait_ge(rope_ld[r], 48 * (h // 2 + 1) if static else h * 24 + (48 - 24 * r))
            pool_rotate(pool, qrS[r], qa[r], qb[r], h * 2 + 7)

        gtmS = sb("gtm", [P, 4, 24])
        gateL = S[0:24, 15872:16384]
        rcg = sb("rcg", [P, 4])
        rcg0 = sem("rcg0")
        glog_in, glog_pe, glog_ok, rcg_ok = sem("glog_in"), sem("glog_pe"), sem("glog_ok"), sem("rcg_ok")

        def nsa_score(which, w):
            def score(pe, bank, r, b, x):
                k = NSA.inp[r][1 + which][:, 0:w] if which < 2 else kcB[r]
                i = unit(NSA, x)["i"]
                nc.tensor.matmul(bank[:, 0:w], NSA.inp[r][0][:, i * P:i * P + P], k, start=True, stop=True).then_inc(NSA.sc, 1)
            return score

        def nsa_gate(i, branch):
            def gate(dve, t, b, x, w, c):
                col = num(b, 6, 3 * (x // 12) + branch)
                nc.vector.tensor_tensor(rcg[:, c:c + 1], stats[:, 12 + c:13 + c], gtmS[:, i, ds(col, 1)], ALU.mult).then_inc(rcg_ok, 1)
                dve.wait_ge(rcg_ok, num(b, t.upp, x + 1))
                p = t.p[x % 4][:, 0:w]
                if branch:
                    nc.vector.tensor_scalar(p, p, rcg[:, c:c + 1], None, ALU.mult).then_inc(t.nr, 1)
                else:
                    nc.vector.scalar_tensor_tensor(p, p, rcg[:, c:c + 1], cm01[:, i, :], ALU.mult, ALU.mult).then_inc(t.nr, 1)
            return gate

        def nsa_units():
            out_ = []
            for i in range(4):
                w = (i + 1) * P
                for which in range(3):
                    o = OFF[i] + (w if which == 2 else 0)
                    n = NPAD if which == 2 else w
                    out_.append(dict(i=i, w=n, nb=1 if which == 2 else i + 1, score=nsa_score(which, n),
                                     v=(lambda r, j_, k=which: NSA.v[r][:, k, j_, :] if k < 2 else vcB[r]),
                                     bias=(lambda r, o=o, n=n: biasB[r][:, o:o + n]), gate=nsa_gate(i, (1, 2, 0)[which]),
                                     first=which == 0, last=which == 2))
            return out_

        NSA = Att("nsa", 24, nsa_units(), 8, 8, 0, 6, 6144, (3, 4), INV_SQ)
        NSA.ld_inc = 16 * 9
        biasB = [S[:, 12288 + LB * r:12288 + LB * (r + 1)] for r in range(2)]
        kcB = [S[:, 15104 + 32 * r:15136 + 32 * r] for r in range(2)]
        vcB = [S[:, 15168 + 128 * r:15296 + 128 * r] for r in range(2)]

        def nsa_load(pool, h, r, s_):
            q, ks, kw, vs, vw, g = NSA.inp[r]
            grp = h // 4
            rows = lambda row: yO[ds(grp * P + row, P), :]
            pool.dma_start(q, yO[ds(h * P + 2112, P), :]).then_inc(s_, 16)
            pool.dma_start(ks, rows(3648)).then_inc(s_, 16)
            pool.dma_start(kw, rows(4160)).then_inc(s_, 16)
            pool.dma_start(vs, rows(3904)).then_inc(s_, 16)
            pool.dma_start(vw, rows(4416)).then_inc(s_, 16)
            pool.dma_start(g, gD[ds(h * P + 1024, P), :]).then_inc(s_, 16)
            pool.dma_start(biasB[r], biasD[ds(h, 1), :, :].rearrange("a p n -> (a p) n")).then_inc(s_, 16)
            pool.dma_start(kcB[r], kcD[ds(grp, 1), :, :].rearrange("a p n -> (a p) n")).then_inc(s_, 16)
            pool.dma_start(vcB[r], vcD[ds(grp, 1), :, :].rearrange("a p n -> (a p) n")).then_inc(s_, 16)

        def pe_nsa_gates(pe):
            pe.wait_ge(glog_in, 16)
            for i in range(4):
                mm = nc.tensor.transpose(PS[:, 6, i * 24:i * 24 + 24], gateL[:, i * P:i * P + P], ident[0:24, 0:24])
            mm.then_inc(glog_pe, 1)

        def act_nsa_gates(act):
            act.wait_ge(glog_pe, 1)
            nc.scalar.activation(gtmS[:, :, :], PS[:, 6, 0:96].rearrange("p (i c) -> p i c", i=4), ACT.Sigmoid).then_inc(glog_ok, 1)

        MEM1, mem1_load = mem_att("mem1", 1, yO, 5720, 2048, MEM0)

        gfS = S[:, 8192:10240]
        gf_in, fin_ok, out_sem = sem("gf_in"), sem("fin_ok"), sem("out_sem")

        def dve_final(dve):
            dve_norm(dve, NORMS[3])
            r = small[:, 20:24]
            dve.wait_ge(rows_ok, 14)
            dve.wait_ge(gf_in, 16)
            for t in range(4):
                nc.vector.scalar_tensor_tensor(hrows[:, t, :], hrows[:, t, :], r[:, t:t + 1], gfS, ALU.mult, ALU.mult).then_inc(fin_ok, 1)

        block = ctx.enter_context(nc.Block())

        @block.sync
        def _(sp):
            for j in plan:
                sp_chunk(sp, j, 0)
                if j["spc"] % RAW == 0 and j["chunks"] > 2:
                    with sp.Fori(1, j["chunks"]) as c:
                        sp_chunk(sp, j, c)
                else:
                    for c in range(1, j["chunks"]):
                        sp_chunk(sp, j, c)

        @block.gpsimd
        def _(pool):
            nc.gpsimd.memset(half_pi_sb[:, :], math.pi / 2).then_inc(ident_ok, 1)
            nc.gpsimd.memset(one_sb[:, :], 1.0).then_inc(ident_ok, 1)
            nc.gpsimd.memset(maskneg[:, :], 0.0).then_inc(ident_ok, 1)
            nc.gpsimd.memset(ident[:, :], 0.0).then_inc(ident_ok, 1)
            pool.wait_ge(ident_ok, 4)
            nc.gpsimd.affine_select(out=maskneg[:, :], in_=maskneg[:, :], compare_op=ALU.is_ge, fill=NEG, base=0,
                                    pattern=[[-1, P]], channel_multiplier=1).then_inc(ident_ok, 1)
            nc.gpsimd.affine_select(out=ident[:, :], in_=ident[:, :], compare_op=ALU.not_equal, fill=1.0, base=0,
                                    pattern=[[-1, P]], channel_multiplier=1).then_inc(ident_ok, 1)
            pool.dma_start(hrows[:, 0, :], mem[0:P, :]).then_inc(rows_in[0], 16)
            pool.dma_start(hrows[:, 1, :], mem[P:2 * P, :]).then_inc(rows_in[1], 16)
            for i, g in enumerate((a["norm_g"][0], a["norm_g"][1], a["mem_norm_g"])):
                pool.dma_start(gcol[:, i, :], g.rearrange("(k p) -> p k", p=P)).then_inc(gains_in, 16)
            pool_prep_loads(pool)
            pool_consts(pool)
            pool.wait_ge(nt_pe, KD)
            for t in range(TT):
                pool.dma_start(hrows[:, t, :], x[t * P:(t + 1) * P, :]).then_inc(rows_in[t], 16)
            pool_prep(pool)
            assert (prep_angle_n, prep_den_n, prep_all_n) == (prep_angle[0], prep_den_at[0], prep_all[0])
            for l in range(2):
                pool_store(pool, jobs[f"memk{l}"], 0, kmD[l].rearrange("(f p) t -> p f t", p=P))
                pool_store(pool, jobs[f"memv{l}"], 0, vmD[l].rearrange("(f p) t -> p f t", p=P))

            def store(c):
                pool_store(pool, E1, c, yE[ds(c * COLS, COLS), :].rearrange("(f p) t -> p f t", p=P))

            store(0)
            pool_cprime(pool)
            pool.wait_ge(stored, 16 * (E1["stored0"] + 1))
            pool_s5_start(pool, 0, True)
            store(1)
            pool_s5_c(pool, 0, True)
            for t in range(4):
                pool_vi(pool, 0, t, True)
            with pool.Fori(1, 8) as m:
                pool_s5_start(pool, m, False)
                store(m + (S5C - 1))
                pool_s5_c(pool, m, False)
                for t in range(4):
                    pool_vi(pool, m, t, False)
            store(9)
            pool.wait_ge(y_ev, 8)
            pool.dma_start(yS[7 * P:8 * P, :], ystS).then_inc(y_out, 16)
            pool.wait_ge(y_out, 16 * 8)
            pool.wait_ge(y_ok, 32)
            pool.wait_ge(r_chain, 32 * 11)
            for k in range(2):
                pool.dma_start(zS[:, 4 * k:4 * k + 4, :], yS[512 * k:512 * k + 512, :].rearrange("(f p) t -> p f t", p=P)).then_inc(zin, 16)
                pool.dma_start(gsS[:, 4 * k:4 * k + 4, :], yE[1024 + 512 * k:1536 + 512 * k, :].rearrange("(f p) t -> p f t", p=P)).then_inc(zin, 16)
            with pool.Fori(10, E1["chunks"]) as c:
                store(c)
            pool.wait_ge(stored, 16 * E2["stored0"])
            pool_store(pool, E2, 0, yE[EVEN_IN - P:EVEN_IN, :].rearrange("(f p) t -> p f t", p=P))
            pool.dma_start(flS, yE[5120:5128, :]).then_inc(fin_, 16)
            pool.dma_start(fb, a["fox_b_f"][0].rearrange("(h a) -> h a", a=1)).then_inc(fin_, 16)
            pool_gate_batch(pool, 0, yE[5128:5640, :], 0)
            pool_gate_batch(pool, 1, yE[5640:6152, :], 512)
            pool.wait_ge(stored, 16 * (E2["stored0"] + 1))
            pool_gate_batch(pool, 2, yE[6664:7176, :], 1024)
            pool.wait_ge(g_out, 48)
            pool.wait_ge(mixs, 24)
            pool_att(pool, FOX, fox_load)
            pool.wait_ge(FOX.fin, FOX.done)
            pool_att(pool, MEM0, mem0_load)
            pool.wait_ge(MEM0.fin, MEM0.done)
            for t in range(TT):
                pool.dma_start(hrows[:, t, :], x[t * P:(t + 1) * P, :]).then_inc(x_in[t], 16)
            pool.wait_ge(banks_free, OUT0["bank0"] + 16)
            pool.dma_start(h1D.rearrange("(t p) d -> p t d", p=P), hrows).then_inc(h1_out, 16)
            pool_t5_loads(pool)

            def store_o(c):
                pool_store(pool, O1, c, yO[ds(c * COLS, COLS), :].rearrange("(f p) t -> p f t", p=P))
            with pool.Fori(1, 12) as c:
                store_o(c - 1)
                for k in range(3):
                    for j_ in range(3):
                        pool_t5_add(pool, c, k, j_)
            store_o(11)
            pool.wait_ge(t5_step, 33)
            pool.dma_start(biasD.rearrange("h p n -> p h n"), accS).then_inc(t5_out, 16)
            store_o(12)
            pool.wait_ge(stored, 16 * O2["stored0"])
            pool_store(pool, O2, 0, yO[ODD_IN - P:ODD_IN, :].rearrange("(f p) t -> p f t", p=P))
            pool.wait_ge(stored, 16 * (O2["stored0"] + 1))
            pool_c(pool)
            pool.wait_ge(cn_ok, 8)
            for k, (row, to) in enumerate(GATES_O):
                pool_gate_batch(pool, 3 + k, yO[row:row + 512, :], to)
            pool.wait_ge(g_out, 16 * 8)
            for c in range(3):
                pool_store(pool, UQ, c, quD[c * COLS:(c + 1) * COLS, :].rearrange("(f p) t -> p f t", p=P))
            for c in range(4):
                pool_store(pool, UKV, c, kvD[c * COLS:(c + 1) * COLS, :].rearrange("(f p) t -> p f t", p=P))
            pool.wait_ge(stored, 16 * count["stored"])
            pool_rope_start(pool)
            pool.wait_ge(kr_in, 48)
            pool.wait_ge(rope_t, 9)
            pool.wait_ge(rope_c, 3)
            pool_rotate(pool, krS, qa[0], qb[0], 5)
            pool.wait_ge(rope_ok, 1)
            pool_att(pool, MLA, mla_load)
            pool.wait_ge(MLA.fin, MLA.done)
            pool.dma_start(gateL, yO[4672:4696, :]).then_inc(glog_in, 16)
            pool_att(pool, NSA, nsa_load)
            pool.wait_ge(NSA.fin, NSA.done)
            pool_att(pool, MEM1, mem1_load)
            pool.wait_ge(MEM1.fin, MEM1.done)
            for t in range(TT):
                pool.dma_start(hrows[:, t, :], h1D[t * P:(t + 1) * P, :]).then_inc(x_in[t], 16)
            pool.dma_start(gfS, a["final_norm_g"].rearrange("(a d) -> a d", a=1).broadcast_to([P, D])).then_inc(gf_in, 16)
            for t in range(TT):
                pool.wait_ge(fin_ok, t + 1)
                pool.dma_start(out[t * P:(t + 1) * P, :], hrows[:, t, :]).then_inc(out_sem, 16)
            pool.wait_ge(out_sem, 64)

        @block.scalar
        def _(act):
            act_norm(act, NORMS[0])
            pend = lambda: None
            for n_, j in enumerate(plan[:4]):
                act_chunk(act, j, 0, pend)
                pend = lambda j=j: act_evac(act, j, 0)
                if n_ == 0:
                    act_prep_sin(act)
            pend()
            act_norm(act, NORMS[1])
            act_chunk(act, E1, 0, lambda: None)
            act_chunk(act, E1, 1, lambda: act_evac(act, E1, 0), lambda s: act_prep(act, s))
            act.wait_ge(init, 3)

            def with_s5(c, m, first):
                hook, after = act_s5(act, m, first)

                def pending():
                    act_evac(act, E1, c - 1)
                    after()
                act_chunk(act, E1, c, pending, hook)

            with_s5(2, 0, True)
            with act.Fori(1, 8) as m:
                with_s5(m + S5C, m, False)

            def last():
                act_evac(act, E1, 9)
                act_yev(act, 8)
            act_chunk(act, E1, 10, last)
            with act.Fori(11, E1["chunks"] - 1) as c:
                act_chunk(act, E1, c, lambda: act_evac(act, E1, c - 1))
            act_chunk(act, E1, 13, lambda: act_evac(act, E1, 12), lambda s: act_z(act, s))
            act_chunk(act, E2, 0, lambda: act_evac(act, E1, E1["chunks"] - 1))
            act_chunk(act, GLU, 0, lambda: act_evac(act, E2, 0))
            act_gate_batch(act, 0)
            act_gate_batch(act, 1)
            act_gate_batch(act, 2)
            act_chunk(act, GLU, 1, lambda: act_glu(act, 0))
            act_glu(act, 1)
            act_forget(act)
            act_att(act, FOX)
            act_att(act, MEM0)
            for c in range(4):
                act_chunk(act, OUT0, c, lambda: None)
            act_norm(act, NORMS[2])
            act_chunk(act, O1, 0, lambda: None)
            act_chunk(act, O1, 1, lambda: act_evac(act, O1, 0), act_t5_hook(act, 1, True))
            with act.Fori(2, 12) as c:
                act_chunk(act, O1, c, lambda: act_evac(act, O1, c - 1), act_t5_hook(act, c, False))
            act_chunk(act, O1, 12, lambda: act_evac(act, O1, 11))
            act_chunk(act, O2, 0, lambda: act_evac(act, O1, 12))
            act_evac(act, O2, 0)
            act_c(act)
            act_c2(act)
            act_chunk(act, UQ, 0, lambda: None)
            for k in range(5):
                act_gate_batch(act, 3 + k)
            for c in range(1, 3):
                act_chunk(act, UQ, c, lambda: act_evac(act, UQ, c - 1))
            act_chunk(act, UKV, 0, lambda: act_evac(act, UQ, 2))
            for c in range(1, 4):
                act_chunk(act, UKV, c, lambda: act_evac(act, UKV, c - 1))
            act_evac(act, UKV, 3)
            act_rope(act)
            act_att(act, MLA)
            act_nsa_gates(act)
            act_att(act, NSA)
            act_att(act, MEM1)
            for c in range(4):
                act_chunk(act, OUT1, c, lambda: None)
            act_norm(act, NORMS[3])

        @block.tensor
        def _(pe):
            pe.wait_ge(ident_ok, 6)
            pe_norm(pe, NORMS[0])
            pe.wait_ge(nt_lo, KD)
            for j in plan[:4]:
                pe_chunk(pe, j, 0)
            pe_norm(pe, NORMS[1])
            pe.wait_ge(nt_lo, 2 * KD)
            pe_chunk(pe, E1, 0)
            pe_chunk(pe, E1, 1, lambda s: pe_prep(pe, s))
            pe_chunk(pe, E1, 2, pe_s5(pe, 0, True))
            with pe.Fori(1, 8) as m:
                pe_chunk(pe, E1, m + S5C, pe_s5(pe, m, False))
            pe_chunk(pe, E1, 10, lambda s: pe_y(pe, 7, 3, False) if s == 0 else None)
            with pe.Fori(11, E1["chunks"]) as c:
                pe_chunk(pe, E1, c)
            pe_chunk(pe, E2, 0)
            pe.wait_ge(zlo_ok, 8)
            pe_chunk(pe, GLU, 0)
            pe_chunk(pe, GLU, 1)
            pe.wait_ge(banks_free, GLU["bank0"] + 8)
            pe_att(pe, FOX)
            pe_att(pe, MEM0)
            pe.wait_ge(MEM0.fin, MEM0.done)
            for c in range(4):
                pe_chunk(pe, OUT0, c)
            pe_norm(pe, NORMS[2])
            pe.wait_ge(nt_lo, 3 * KD)
            pe_chunk(pe, O1, 0)
            with pe.Fori(1, 13) as c:
                pe_chunk(pe, O1, c)
            pe_chunk(pe, O2, 0)
            pe.wait_ge(banks_free, UQ["bank0"])
            pe_c(pe)
            pe_c2(pe)
            pe.wait_ge(cn_ok, 8)
            for j in (UQ, UKV):
                for c in range(j["chunks"]):
                    pe_chunk(pe, j, c)
            pe.wait_ge(banks_free, OUT1["bank0"])
            pe.wait_ge(cmp2_ok, 3)
            pe_att(pe, MLA)
            pe.wait_ge(MLA.fin, MLA.done)
            pe_nsa_gates(pe)
            pe.wait_ge(glog_ok, 1)
            pe_att(pe, NSA)
            pe_att(pe, MEM1)
            pe.wait_ge(MEM1.fin, MEM1.done)
            for c in range(4):
                pe_chunk(pe, OUT1, c)

        @block.vector
        def _(dve):
            dve_norm(dve, NORMS[0])
            for n_, j in enumerate(plan[:4]):
                dve_chunk(dve, j, 0)
                if n_ == 0:
                    dve_prep_den(dve)
            dve_norm(dve, NORMS[1])
            dve_chunk(dve, E1, 0)
            dve_chunk(dve, E1, 1)
            dve.wait_ge(init, 3)
            dve_chunk(dve, E1, 2, dve_s5(dve, 0, True))
            with dve.Fori(1, 8) as m:
                dve_chunk(dve, E1, m + S5C, dve_s5(dve, m, False))
            dve_chunk(dve, E1, 10)
            with dve.Fori(11, E1["chunks"]) as c:
                dve_chunk(dve, E1, c)
            dve_chunk(dve, E2, 0)
            dve_z(dve)
            dve_chunk(dve, GLU, 0)
            dve_glu(dve, 0)
            dve_chunk(dve, GLU, 1)
            dve_glu(dve, 1)
            dve_forget(dve)
            dve_att(dve, FOX)
            dve_att(dve, MEM0)
            for c in range(4):
                dve_chunk(dve, OUT0, c)
                dve_out(dve, OUT0, c, 16)
            dve_norm(dve, NORMS[2])
            dve_chunk(dve, O1, 0)
            dve_t5_start(dve)
            dve_chunk(dve, O1, 1, dve_t5_hook(dve, 1, True))
            with dve.Fori(2, 12) as c:
                dve_chunk(dve, O1, c, dve_t5_hook(dve, c, False))
            dve_chunk(dve, O1, 12, lambda s: dve_t5_end(dve) if s == 1 else None)
            dve_chunk(dve, O2, 0)
            dve_c(dve)
            dve_c2(dve)
            for j in (UQ, UKV):
                for c in range(j["chunks"]):
                    dve_chunk(dve, j, c)
            dve_rope(dve)
            dve_att(dve, MLA)
            for r in range(4):
                nc.vector.memset(NSA.p[r], 0.0).then_inc(rcg0, 1)
            dve.wait_ge(rcg0, 4)
            dve_att(dve, NSA)
            dve_att(dve, MEM1)
            for c in range(4):
                dve_chunk(dve, OUT1, c)
                dve_out(dve, OUT1, c, 32)
            dve_final(dve)


_INS = ["x", "mem", "positions", "norm_g", "mem_norm_g", "final_norm_g", "t5_table", "w_out", "mem_w_kv", "even_w_in",
        "s5_lam_re", "s5_lam_im", "s5_log_dt", "s5_b_re", "s5_b_im", "s5_c_re", "s5_c_im", "s5_d", "s5_w_glu", "fox_b_f",
        "odd_w_in", "mla_g_cq", "mla_g_ckv", "mla_w_uq", "mla_w_ukv", "nsa_cmp_pe", "nsa_cmp_w1", "nsa_cmp_w2"]


def kernel(**inputs):
    import concourse.bacc as _bacc
    from concourse.bass_utils import run_bass_kernel_spmd as _run

    nc = _bacc.Bacc("TRN2", target_bir_lowering=False, num_devices=1)
    arrays, aps = {}, {}
    for name, v in [(n, inputs[n]) for n in _INS] + list(const_inputs().items()):
        v = np.ascontiguousarray(v)
        arrays[f"in_{name}_dram"] = v
        aps[name] = nc.dram_tensor(f"in_{name}_dram", v.shape, mybir.dt.from_np(v.dtype), kind="ExternalInput").ap()
    aps["out"] = nc.dram_tensor("out_0_dram", (1, T, D), F32, kind="ExternalOutput").ap()
    build(nc, aps)
    r = _run(nc, [arrays], core_ids=[0])
    return r.results[0]["out_0_dram"]
```

```python
import numpy as np
import math
from contextlib import ExitStack

import concourse.bass as bass
from concourse import mybir

F32 = mybir.dt.float32
F32R = mybir.dt.float32r
I32 = mybir.dt.int32
ACT = mybir.ActivationFunctionType
ALU = mybir.AluOpType
AX = mybir.AxisListType.X
ds = bass.ds

P = 128
D = 2048
T = 512
NMEM = 256
NPAD = 32
LB = 1408
TT = T // P
EVEN_IN = 7176
ODD_IN = 6744
KD = D // P
MIX = 2560
KM = MIX // P
EPS = 1e-6
NEG = -1e30
RAW = 4
COLS = 512


def const_inputs():
    half = 32
    inv_freq = (np.float32(10000.0) ** (-np.arange(half, dtype=np.float32) / np.float32(half))).astype(np.float32)
    inv = np.tile(inv_freq, 4).reshape(P, 1)
    sgn = np.tile(np.repeat(np.array([-1.0, 1.0], np.float32), 32), 2).reshape(P, 1)
    n = np.arange(3000)
    ratio = np.log(np.maximum(n, 1).astype(np.float32) / np.float32(16)) / np.float32(math.log(64))
    large = np.minimum(16 + (ratio * np.float32(16)).astype(np.int32), 31)
    bucket = np.where(n < 16, n, large)
    first = [float(np.argmax(bucket >= b)) for b in range(1, 32)]
    thr = np.tile(np.array(first, np.float32), (P, 1))
    sel = np.zeros((8, P, P), np.float32)
    for h in range(8):
        sel[h, h, :] = 1.0
    return {"c_sel": sel, "c_inv": inv.astype(np.float32), "c_sgn": sgn, "c_thr": thr}


def build(nc, a):
    x, mem = a["x"][0], a["mem"][0]
    out = a["out"][0]
    with ExitStack() as ctx:
        def sb(name, shape, dt=F32):
            return ctx.enter_context(nc.sbuf_tensor(name, shape, dt))

        def sem(name):
            return ctx.enter_context(nc.semaphore(name))

        def dram(name, shape, dt=F32):
            return nc.dram_tensor(name, shape, dt, kind="Internal").ap()

        yE = dram("yE", (EVEN_IN, T))
        yO = dram("yO", (ODD_IN, T))
        kmD = [dram(f"kmD{l}", (512, NMEM)) for l in range(2)]
        vmD = [dram(f"vmD{l}", (NMEM, 512)) for l in range(2)]

        wraw = sb("wraw", [P, RAW, 2, COLS])
        wsp = sb("wsp", [P, RAW, 2, 2, COLS], F32R)
        A = sb("A", [P, 40, T], F32R)
        stage = sb("stage", [P, 4, COLS])
        S = sb("S", [P, 16384])
        ident = sb("ident", [P, P])
        gcol = sb("gcol", [P, 3, KD])
        small = sb("small", [P, 64])
        PS = ctx.enter_context(nc.psum_tensor("PS", [P, 8, 512], F32))

        w_loaded = [sem(f"w_loaded{i}") for i in range(RAW)]
        w_hi = sem("w_hi")
        w_lo = sem("w_lo")
        slot_used = sem("slot_used")
        banks_free = sem("banks_free")
        stored = sem("stored")
        ident_ok = sem("ident_ok")
        gains_in = sem("gains_in")
        rows_in = [sem(f"rows_in{t}") for t in range(4)]
        sq_done = sem("sq_done")
        rms_step = sem("rms_step")
        rms_sqrt = sem("rms_sqrt")
        rows_ok = sem("rows_ok")
        nt_pe = sem("nt_pe")
        nt_hi = sem("nt_hi")
        nt_lo = sem("nt_lo")

        mwk = a["mem_w_kv"]
        plan = []
        count = {"slot": 0, "chunk": 0, "bank": 0, "staged": 0, "stored": 0}

        def job(name, w, k_tiles, chunks, cols=COLS, nf=4, mode="F", n=T, hi=0, lo=16, to_stage=True, parts=None):
            j = dict(name=name, w=w.rearrange("(k p) n -> p k n", p=P), spc=k_tiles // 2, chunks=chunks, cols=cols,
                     nf=nf, mode=mode, n=n, hi=hi, lo=lo, stage=to_stage, parts=parts or [(0, chunks, 0)], **{k + "0": v for k, v in count.items()})
            count["slot"] += k_tiles // 2 * chunks
            count["chunk"] += chunks
            count["bank"] += nf * chunks
            if to_stage:
                count["staged"] += nf * chunks
                count["stored"] += chunks
            plan.append(j)
            return j

        for l in range(2):
            job(f"memk{l}", mwk[l][:, 0:512], KD, 1, mode="F", n=NMEM)
            job(f"memv{l}", mwk[l][:, 512:1024], KD, 1, mode="T", nf=2)
        w_even = a["even_w_in"][0]
        E1 = job("E1", w_even, KD, 14, parts=[(0, 10, 0), (10, 14, 8)])
        E2 = job("E2", w_even[:, 5120:5128], KD, 1, cols=8, nf=1)
        GLU = job("GLU", a["s5_w_glu"][0], 8, 2, hi=32, lo=8, to_stage=False)
        OUT0 = job("OUT0", a["w_out"][0], KM, 4, mode="T", hi=0, lo=KM, to_stage=False)
        w_odd = a["odd_w_in"][0]
        O1 = job("O1", w_odd, KD, 13, parts=[(0, 2, 0), (2, 7, 1088), (7, 8, 2136), (8, 10, -3008), (10, 12, -424), (12, 13, 88)])
        O2 = job("O2", w_odd, KD, 1, cols=88, nf=1)
        UQ = job("UQ", a["mla_w_uq"][0], 4, 3, hi=32, lo=8)
        UKV = job("UKV", a["mla_w_ukv"][0], 4, 4, hi=36, lo=12)
        OUT1 = job("OUT1", a["w_out"][1], KM, 4, mode="T", hi=0, lo=KM, to_stage=False)
        jobs = {j["name"]: j for j in plan}

        def sp_slot(sp, j, c, s, n, q, rounds, early, part0):
            if not early:
                sp.wait_ge(w_lo, n - 3)
            col = c * COLS + [sh for c0, c1, sh in j["parts"] if c0 <= (part0 if part0 is not None else c) < c1][0]
            if j is O2:
                sp.dma_start(wraw[:, q, :, 0:64], j["w"][:, 2 * s:2 * s + 2, 1024:1088]).then_inc(w_loaded[q], 16)
                sp.dma_start(wraw[:, q, :, 64:88], j["w"][:, 2 * s:2 * s + 2, 4672:4696]).then_inc(w_loaded[q], 16)
                return
            sp.dma_start(wraw[:, q, :, 0:j["cols"]],
                         j["w"][:, 2 * s:2 * s + 2, ds(col, j["cols"])]).then_inc(w_loaded[q], 16)

        def act_slot(act, j, n, q, rounds, early):
            twice = 0
            if isinstance(n, int) and n >= O2["slot0"]:
                twice = 16 * min((n - O2["slot0"]) // RAW + 1, 2)
            act.wait_ge(w_loaded[q], rounds * 16 + (16 + twice))
            if not early:
                act.wait_ge(slot_used, n - 3)
            nc.scalar.activation(wsp[:, q, 0, :, 0:j["cols"]], wraw[:, q, :, 0:j["cols"]], ACT.Copy).then_inc(w_hi, 1)

        def dve_slot(dve, j, n, q):
            dve.wait_ge(w_hi, n + 1)
            nc.vector.tensor_tensor(wsp[:, q, 1, :, 0:j["cols"]], wraw[:, q, :, 0:j["cols"]],
                                    wsp[:, q, 0, :, 0:j["cols"]].bitcast(F32), ALU.subtract).then_inc(w_lo, 1)

        def pe_slot(pe, j, s, n, q, free):
            pe.wait_ge(w_lo, n + 1)
            for kk in range(2):
                kt = 2 * s + kk
                for f in range(j["nf"]):
                    if kk == 0 and s == 0 and free[f] is not None:
                        pe.wait_ge(banks_free, free[f])
                    for i, (wp, ap) in enumerate(((0, j["hi"]), (0, j["lo"]), (1, j["hi"]))):
                        if j["mode"] == "F":
                            lhs = wsp[:, q, wp, kk, f * P:f * P + min(P, j["cols"])]
                            rhs = A[:, ap + kt, 0:j["n"]]
                            dst = PS[0:min(P, j["cols"]), f, 0:j["n"]]
                        else:
                            lhs = A[:, ap + kt, f * P:f * P + P]
                            rhs = wsp[:, q, wp, kk, :]
                            dst = PS[:, f, :]
                        mm = nc.tensor.matmul(dst, lhs, rhs, start=(s == 0 and kk == 0 and i == 0),
                                              stop=(s == j["spc"] - 1 and kk == 1 and i == 2))
            return mm.then_inc(slot_used, 1)

        def chunk_slots(j, c, first):
            for s in range(j["spc"]):
                base = j["slot0"] + s
                if isinstance(c, int):
                    n = base + c * j["spc"]
                    yield s, n, n % RAW, n // RAW, n < RAW
                else:
                    assert j["spc"] % RAW == 0
                    yield s, c * j["spc"] + base, base % RAW, c * (j["spc"] // RAW) + base // RAW, False

        def sp_chunk(sp, j, c, part0=None):
            for s, n, q, r, early in chunk_slots(j, c, False):
                sp_slot(sp, j, c, s, n, q, r, early, part0)

        def pe_chunk(pe, j, c, hook=None):
            if isinstance(c, int) and c == 0:
                free = [j["bank0"] if j["bank0"] else None] + [None] * 3
            else:
                free = [c * j["nf"] + (j["bank0"] - j["nf"] + 1 + f) for f in range(j["nf"])] + [None] * 3
            for s, n, q, r, early in chunk_slots(j, c, False):
                pe_slot(pe, j, s, n, q, free)
                if hook:
                    hook(s)

        def dve_chunk(dve, j, c, hook=None):
            for s, n, q, r, early in chunk_slots(j, c, False):
                dve_slot(dve, j, n, q)
                if hook:
                    hook(s)

        def act_evac(act, j, c, func=ACT.Copy):
            act.wait_ge(slot_used, c * j["spc"] + (j["slot0"] + j["spc"]))
            if not (isinstance(c, int) and c * 1 + j["stored0"] == 0):
                act.wait_ge(stored, c * 16 + j["stored0"] * 16)
            for f in range(j["nf"]):
                n = j["n"] if j["mode"] == "F" else COLS
                rows = min(P, j["cols"])
                nc.scalar.activation(stage[0:rows, f, 0:n], PS[0:rows, f, 0:n], func).then_inc(banks_free, 1)

        def act_chunk(act, j, c, pending, hook=None):
            for s, n, q, r, early in chunk_slots(j, c, False):
                if s == min(3, j["spc"] - 1):
                    pending()
                act_slot(act, j, n, q, r, early)
                if hook:
                    hook(s)

        def pool_store(pool, j, c, dst, n=None):
            pool.wait_ge(banks_free, c * j["nf"] + (j["bank0"] + j["nf"]))
            n = n or (j["n"] if j["mode"] == "F" else COLS)
            src = stage[:, 0:j["nf"], 0:n] if j["cols"] >= P else stage[0:j["cols"], 0, 0:n]
            pool.dma_start(dst, src).then_inc(stored, 16)

        hrows = S[:, 0:8192].rearrange("p (t d) -> p t d", t=4)
        junk = PS[:, 4:8, :]
        NORMS = [dict(tiles=2, g=2, k=0), dict(tiles=4, g=0, k=1), dict(tiles=4, g=1, k=2), dict(tiles=4, k=3)]

        def act_norm(act, v):
            if v["k"] == 2:
                act.wait_ge(banks_free, OUT0["bank0"] + 16)
            if v["k"] == 3:
                act.wait_ge(banks_free, OUT1["bank0"] + 16)
            for t in range(v["tiles"]):
                if v["k"] < 2:
                    act.wait_ge(rows_in[t], 16 if v["k"] == 0 or t >= 2 else 32)
                if t:
                    act.wait_ge(sq_done, [0, 2, 6, 10][v["k"]] + t)
                elif v["k"] == 1:
                    act.wait_ge(nt_lo, KD)
                nc.scalar.activation(junk, hrows[:, t, :], ACT.Square,
                                     accum_out=small[:, t:t + 1]).then_inc(sq_done, 1)
            act.wait_ge(rms_step, 5 * v["k"] + 1)
            nc.scalar.activation(small[:, 8:8 + v["tiles"]], small[:, 4:4 + v["tiles"]], ACT.Sqrt).then_inc(rms_sqrt, 1)
            if v["k"] == 3:
                return
            if v["k"] == 0:
                act.wait_ge(gains_in, 48)
            for k in range(KD):
                act.wait_ge(nt_pe, KD * v["k"] + k + 1)
                n = v["tiles"] * P
                nc.scalar.activation(A[:, k, 0:n], PS[:, 4 + k % 4, 0:n], ACT.Copy,
                                     scale=gcol[:, v["g"], k:k + 1]).then_inc(nt_hi, 1)

        def dve_norm(dve, v):
            t = v["tiles"]
            ssq, var, root, r0, r1, r = (small[:, 4 * i:4 * i + t] for i in range(6))
            dve.wait_ge(sq_done, [2, 6, 10, 14][v["k"]])
            nc.vector.tensor_scalar(var, ssq, 1.0 / D, EPS, ALU.mult, ALU.add).then_inc(rms_step, 1)
            dve.wait_ge(rms_sqrt, v["k"] + 1)
            nc.vector.reciprocal(r0, root).then_inc(rms_step, 1)
            dve.wait_ge(rms_step, 5 * v["k"] + 2)
            nc.vector.tensor_tensor(r1, r0, r0, ALU.mult).then_inc(rms_step, 1)
            dve.wait_ge(rms_step, 5 * v["k"] + 3)
            nc.vector.tensor_tensor(r1, r1, var, ALU.mult).then_inc(rms_step, 1)
            dve.wait_ge(rms_step, 5 * v["k"] + 4)
            nc.vector.tensor_scalar(r1, r1, -0.5, 1.5, ALU.mult, ALU.add).then_inc(rms_step, 1)
            dve.wait_ge(rms_step, 5 * v["k"] + 5)
            nc.vector.tensor_tensor(r, r0, r1, ALU.mult).then_inc(rows_ok, 1)
            base = [0, 3, 8, 13][v["k"]]
            dve.wait_ge(rows_ok, base + 1)
            if v["k"] == 3:
                return
            if v["k"] == 2:
                dve.wait_ge(h1_out, 16)
            for i in range(t):
                nc.vector.tensor_scalar(hrows[:, i, :], hrows[:, i, :], r[:, i:i + 1], None, ALU.mult).then_inc(rows_ok, 1)
            if v["k"] == 0:
                dve.wait_ge(gains_in, 48)
            for k in range(KD):
                n = t * P
                dve.wait_ge(nt_hi, KD * v["k"] + k + 1)
                nc.vector.scalar_tensor_tensor(A[:, 16 + k, 0:n], PS[:, 4 + k % 4, 0:n], gcol[:, v["g"], k:k + 1],
                                               A[:, k, 0:n].bitcast(F32), ALU.mult, ALU.subtract).then_inc(nt_lo, 1)

        def pe_norm(pe, v):
            base = [0, 3, 8][v["k"]]
            pe.wait_ge(rows_ok, base + 1 + v["tiles"])
            for k in range(KD):
                g = KD * v["k"] + k
                if g >= 4:
                    pe.wait_ge(nt_lo, g - 3)
                for t in range(v["tiles"]):
                    mm = nc.tensor.transpose(PS[:, 4 + k % 4, t * P:(t + 1) * P], hrows[:, t, k * P:(k + 1) * P], ident[:, :])
                mm.then_inc(nt_pe, 1)

        ctx.enter_context(nc.allow_non_contiguous_dma(reason="small columns of gains"))

        offs = [8192]

        def cut(n, *shape, at=None):
            o = offs[0] if at is None else at
            if at is None:
                offs[0] += n
            v = S[:, o:o + n]
            return v

        bc = cut(1024).rearrange("p (i j c) -> p i j c", i=2, j=32)
        cc = cut(1024).rearrange("p (i j c) -> p i j c", i=2, j=32)
        prm = cut(192).rearrange("p (k j) -> p k j", k=6)
        dcol = cut(8)
        low0 = offs[0]
        cnat = cut(2048).rearrange("p (i m q) -> p i m q", i=2, m=8)
        ct = cut(1024).rearrange("p (i j c) -> p i j c", i=2, j=32)
        pt = cut(2816).rearrange("p (k q) -> p k q", k=22)
        pti = pt[:, 20, :].bitcast(I32)
        assert offs[0] <= 16384
        tiles_off = [0]

        def tile512(k=1):
            o = tiles_off[0]
            if o + 512 * k > 8192 and o <= 8192:
                o = max(o, low0)
            tiles_off[0] = o + 512 * k
            assert tiles_off[0] <= 16384
            return S[:, o:o + 512 * k]

        timeS = tile512()
        fS = tile512()
        cosS = [tile512(), tile512()]
        sinS = [tile512(), tile512()]
        ubS = [tile512(2).rearrange("p (i t) -> p i t", i=2) for _ in range(2)]
        t1S, t2S, t5S, vimS, p2S, uS, ystS = [tile512() for _ in range(6)] + [None]
        xS = [tile512(2).rearrange("p (i t) -> p i t", i=2) for _ in range(2)]
        exb = tile512(2).rearrange("p (i j c) -> p i j c", i=2, j=4)
        exc = tile512(2).rearrange("p (i j c) -> p i j c", i=2, j=4)
        bT = tile512(2).rearrange("p (i j c) -> p i j c", i=2, j=4)
        ystS = tile512()
        dg = S[:, tiles_off[0]:tiles_off[0] + P]
        assert tiles_off[0] + P <= 16384

        yS = dram("yS", (1024, T))
        prep_in = sem("prep_in")
        prep = sem("prep")
        prep_sin = sem("prep_sin")
        prep_den = sem("prep_den")
        prepT = sem("prepT")
        prepE = sem("prepE")
        cprime = sem("cprime")
        init = sem("init")
        exb_ok, exc_ok, dg_ok, u_in = sem("exb_ok"), sem("exc_ok"), sem("dg_ok"), sem("u_in")
        xt_pe, xt_ev = sem("xt_pe"), sem("xt_ev")
        f_ok, f_chain, tab_ok, bu_ok, eb_ok, vi_ok, vi_chain = [sem(n) for n in ("f_ok", "f_chain", "tab_ok", "bu_ok", "eb_ok", "vi_ok", "vi_chain")]
        r_chain, y_ok, y_ev, y_out = [sem(n) for n in ("r_chain", "y_ok", "y_ev", "y_out")]
        MAGIC = 12582912.0
        TWO_PI = 6.283185307179586
        C1, C2, C3 = 6.28125, 1.93500518798828125e-3, 3.0199159819567529e-7

        def pool_prep_loads(pool):
            for i, n in enumerate(("s5_lam_re", "s5_lam_im")):
                pool.dma_start(pt[0:32, i, :], a[n][0].rearrange("(j e) p -> j (e p)", e=2)).then_inc(prep_in, 16)
            pool.dma_start(pt[0:32, 2, 0:2], a["s5_log_dt"][0].rearrange("(j e) -> j e", e=2)).then_inc(prep_in, 16)
            for i, n in enumerate(("s5_b_re", "s5_b_im")):
                pool.dma_start(bc[:, i, :, :], a[n][0].rearrange("g p c -> (g p) c").rearrange("(j q) c -> q j c", q=P)).then_inc(prep_in, 16)
            for i, n in enumerate(("s5_c_re", "s5_c_im")):
                v = a[n][0].rearrange("g c p -> (g c) p").rearrange("(m r) p -> r m p", r=P)
                for e in range(2):
                    pool.dma_start(cnat[:, i, :, e * 64:e * 64 + 64], v).then_inc(prep_in, 16)
            pool.dma_start(dcol, a["s5_d"][0].rearrange("g c -> (g c)").rearrange("(m r) -> r m", r=P)).then_inc(prep_in, 16)

        def pool_prep(pool):
            k = [0]
            pool.wait_ge(prep_in, 16 * 10)

            def ts(o, i, s1, s2, o1=ALU.mult, o2=ALU.add):
                link(nc.gpsimd.tensor_scalar(o, i, s1, s2, o1, o2))

            def tt(o, i, j_, op=ALU.mult):
                link(nc.gpsimd.tensor_tensor(o, i, j_, op))

            def link(ins):
                k[0] += 1
                ins.then_inc(prep, 1)
                pool.wait_ge(prep, k[0])

            def exp_parts(xx, kk, rr, q, two, twoi, t):
                ts(kk, xx, 1.4426950408889634, MAGIC)
                ts(kk, kk, MAGIC, None, ALU.subtract, ALU.bypass)
                ts(t, kk, -0.693359375, None, ALU.mult, ALU.bypass)
                tt(rr, xx, t, ALU.add)
                ts(t, kk, 2.12194440e-4, None, ALU.mult, ALU.bypass)
                tt(rr, rr, t, ALU.add)
                ts(kk, kk, -127.0, 127.0, ALU.max, ALU.min)
                ts(twoi, kk, 127.0, 8388608.0, ALU.add, ALU.mult)
                ts(q, rr, 1.0 / 8, 1.0)
                for n in range(7, 1, -1):
                    tt(q, q, rr)
                    ts(q, q, 1.0 / n, 1.0)
                tt(q, q, rr)

            R = slice(0, 32)
            t_ = lambda i, w=P: pt[R, i, 0:w]
            exp_parts(t_(2, 2), t_(3, 2), t_(4, 2), t_(5, 2), t_(20, 2), pti[R, 0:2], t_(6, 2))
            tt(t_(5, 2), t_(5, 2), t_(20, 2))
            tt(t_(5, 2), t_(5, 2), t_(20, 2), ALU.add)
            dt = pt[R, 5, 0:2].unsqueeze(2).broadcast_to([32, 2, 64])
            e3 = lambda i: pt[R, i, :].rearrange("r (e p) -> r e p", e=2)
            tt(e3(7), e3(0), dt)
            tt(e3(8), e3(1), dt)
            exp_parts(t_(7), t_(3), t_(4), t_(9), t_(20), pti[R, :], t_(6))
            tt(t_(9), t_(9), t_(20))
            ts(t_(6), t_(20), 1.0, None, ALU.subtract, ALU.bypass)
            tt(t_(9), t_(9), t_(6), ALU.add)
            ts(t_(10), t_(9), 1.0, None, ALU.add, ALU.bypass)
            ts(t_(3), t_(8), 1.0 / TWO_PI, MAGIC)
            ts(t_(3), t_(3), MAGIC, None, ALU.subtract, ALU.bypass)
            for cst in (C1, C2, C3):
                ts(t_(6), t_(3), -cst, None, ALU.mult, ALU.bypass)
                tt(t_(8), t_(8), t_(6), ALU.add)
            ts(t_(8), t_(8), -3.1415925, 3.1415925, ALU.max, ALU.min)
            prep_angle[0] = k[0]
            ts(t_(11), t_(8), 1.0 / TWO_PI, None, ALU.mult, ALU.bypass)
            ts(t_(12), t_(11), 1.0, 192.0)
            ts(t_(12), t_(12), 192.0, None, ALU.subtract, ALU.bypass)
            tt(t_(13), t_(11), t_(12), ALU.subtract)
            tt(t_(14), t_(0), t_(0))
            tt(t_(6), t_(1), t_(1))
            tt(t_(14), t_(14), t_(6), ALU.add)
            prep_den_at[0] = k[0]
            pool.wait_ge(prep_sin, 2)
            tt(t_(17), t_(16), t_(16))
            ts(t_(17), t_(17), -2.0, None, ALU.mult, ALU.bypass)
            tt(t_(15), t_(15), t_(10))
            ts(t_(18), t_(17), 1.0, None, ALU.add, ALU.bypass)
            tt(t_(18), t_(18), t_(9))
            tt(t_(18), t_(18), t_(17), ALU.add)
            pool.wait_ge(prep_den, 1)
            tt(t_(3), t_(18), t_(0))
            tt(t_(4), t_(15), t_(1))
            tt(t_(3), t_(3), t_(4), ALU.add)
            tt(t_(21), t_(3), t_(19))
            tt(t_(3), t_(15), t_(0))
            tt(t_(4), t_(18), t_(1))
            tt(t_(3), t_(3), t_(4), ALU.subtract)
            tt(t_(2), t_(3), t_(19))
            prep_all[0] = k[0]

        prep_angle, prep_den_at, prep_all = [0], [0], [0]
        N_EXP = 8 + 1 + 12 + 1
        prep_angle_n = 2 * N_EXP + 2 + 2 + 4 + 2 + 6 + 1
        prep_den_n = prep_angle_n + 4 + 3
        prep_all_n = prep_den_n + 6 + 8

        def act_prep_sin(act):
            act.wait_ge(prep, prep_angle_n)
            nc.scalar.activation(pt[0:32, 15, :], pt[0:32, 8, :], ACT.Sin).then_inc(prep_sin, 1)
            nc.scalar.activation(pt[0:32, 16, :], pt[0:32, 8, :], ACT.Sin, scale=0.5).then_inc(prep_sin, 1)

        def dve_prep_den(dve):
            dve.wait_ge(prep, prep_den_n)
            nc.vector.reciprocal(pt[0:32, 19, :], pt[0:32, 14, :]).then_inc(prep_den, 1)

        def pe_prep(pe, s):
            if s == 1:
                pe.wait_ge(prep, prep_all_n)
                pe.wait_ge(nt_lo, 2 * KD)
                for i, row in enumerate((10, 11, 12, 13, 21, 2)):
                    mm = nc.tensor.transpose(PS[:, 4, i * 32:i * 32 + 32], pt[0:32, row, :], ident[0:32, 0:32])
                mm.then_inc(prepT, 1)
            if s == 3:
                pe.wait_ge(prepE, 1)
                for i in range(2):
                    for m in range(8):
                        mm = nc.tensor.transpose(PS[:, 4 + 2 * i + m // 4, (m % 4) * P:(m % 4) * P + P], cnat[:, i, m, :], ident[:, :])
                mm.then_inc(prepT, 1)

        def act_prep(act, s):
            if s == 5:
                act.wait_ge(prepT, 1)
                nc.scalar.activation(prm, PS[:, 4, 0:192].rearrange("p (k j) -> p k j", k=6), ACT.Copy).then_inc(prepE, 1)
            if s == 7:
                act.wait_ge(prepT, 2)
                for i in range(2):
                    for h in range(2):
                        for e in range(2):
                            src = PS[e * 64:e * 64 + 64, 4 + 2 * i + h, :].rearrange("p (j k c) -> p j k c", j=16, k=2)[:, :, e, :]
                            nc.scalar.activation(ct[e * 64:e * 64 + 64, i, 16 * h:16 * h + 16, :], src, ACT.Copy).then_inc(prepE, 1)

        def pool_cprime(pool):
            pool.wait_ge(prepE, 9)
            pool.wait_ge(nt_pe, 2 * KD)
            f3 = [prm[:, 4 + i, :].unsqueeze(2).broadcast_to([P, 32, 16]) for i in range(2)]
            u0 = cnat[:, 0].rearrange("p m q -> p (m q)")[:, 0:512].rearrange("p (j c) -> p j c", j=32)
            u1 = cnat[:, 0].rearrange("p m q -> p (m q)")[:, 512:1024].rearrange("p (j c) -> p j c", j=32)
            u2 = cnat[:, 1].rearrange("p m q -> p (m q)")[:, 0:512].rearrange("p (j c) -> p j c", j=32)
            u3 = cnat[:, 1].rearrange("p m q -> p (m q)")[:, 512:1024].rearrange("p (j c) -> p j c", j=32)
            nc.gpsimd.tensor_tensor(u0, ct[:, 0], f3[0], ALU.mult).then_inc(cprime, 1)
            nc.gpsimd.tensor_tensor(u1, ct[:, 1], f3[1], ALU.mult).then_inc(cprime, 1)
            nc.gpsimd.tensor_tensor(u2, ct[:, 0], f3[1], ALU.mult).then_inc(cprime, 1)
            nc.gpsimd.tensor_tensor(u3, ct[:, 1], f3[0], ALU.mult).then_inc(cprime, 1)
            pool.wait_ge(cprime, 4)
            nc.gpsimd.tensor_tensor(cc[:, 0], u0, u1, ALU.subtract).then_inc(cprime, 1)
            nc.gpsimd.tensor_tensor(u2, u2, u3, ALU.add).then_inc(cprime, 1)
            pool.wait_ge(cprime, 6)
            nc.gpsimd.tensor_scalar(cc[:, 1], u2, -1.0, None, ALU.mult).then_inc(cprime, 1)
            pool.wait_ge(cprime, 7)
            nc.gpsimd.iota(timeS, pattern=[[1, T]], base=0, channel_multiplier=0,
                           allow_small_or_imprecise_dtypes=True).then_inc(init, 1)
            nc.gpsimd.memset(exb, 0.0).then_inc(init, 1)
            nc.gpsimd.memset(exc, 0.0).then_inc(init, 1)
            pool.wait_ge(init, 3)

        def pool_frames(pool, m, which, ok):
            src, per = (bc, 4) if which is exb else (cc, 4)
            for e in range(2):
                for i in range(2):
                    s0 = src[e * 64:e * 64 + 64, i, ds(m * 4, 4), :]
                    fr = which[e * 64:e * 64 + 64, i, :, :].rearrange("p j c -> p (j c)")
                    v = bass.AP(tensor=fr.tensor, offset=fr.offset + 16 * e, ap=[fr.ap[0], [160, 4], [1, 16]])
                    nc.gpsimd.tensor_copy(v, s0).then_inc(ok, 1)
                pool.wait_ge(ok, m * per + (2 * e + 2))

        def pool_s5_b(pool, m, first):
            if not first:
                pool.wait_ge(xt_pe, m * 2)
            pool_frames(pool, m, exb, exb_ok)

        def pool_s5_u(pool, m, first):
            if not first:
                pool.wait_ge(bu_ok, m * 4)
                pool.wait_ge(y_ok, m * 4 - 3)
            pool.dma_start(uS, yE[ds(m * P, P), :]).then_inc(u_in, 16)
            nc.gpsimd.tensor_tensor(dg, ident[:, :], dcol[:, ds(m, 1)].broadcast_to([P, P]), ALU.mult).then_inc(dg_ok, 1)

        def pool_s5_c(pool, m, first):
            if not first:
                pool.wait_ge(y_ok, m * 4)
            pool_frames(pool, m, exc, exc_ok)

        def pool_y_out(pool, m):
            pool.wait_ge(y_ev, m + 1)
            pool.dma_start(yS[ds(m * P, P), :], ystS).then_inc(y_out, 16)

        def pool_vi(pool, m, t, first):
            n1 = m * 4 + (t + 1)
            b = ubS[t % 2]
            pool.wait_ge(eb_ok, n1)
            pool.wait_ge(tab_ok, n1)
            if not (first and t == 0):
                pool.wait_ge(r_chain, (m * 4 + t) * 11)
            nc.gpsimd.tensor_tensor(vimS, cosS[t % 2], b[:, 1, :], ALU.mult).then_inc(vi_chain, 1)
            nc.gpsimd.tensor_tensor(p2S, sinS[t % 2], b[:, 0, :], ALU.mult).then_inc(vi_chain, 1)
            pool.wait_ge(vi_chain, n1 * 2)
            nc.gpsimd.tensor_tensor(vimS, vimS, p2S, ALU.subtract).then_inc(vi_ok, 1)

        def dve_f(dve, m, t, first):
            n = m * 4 + t
            if not (first and t == 0):
                dve.wait_ge(tab_ok, n)
            col = lambda k: prm[:, k, ds(n, 1)]
            nc.vector.tensor_scalar(fS, timeS, col(1), MAGIC, ALU.mult, ALU.add).then_inc(f_chain, 1)
            dve.wait_ge(f_chain, n * 4 + 1)
            nc.vector.tensor_scalar(fS, fS, MAGIC, None, ALU.subtract).then_inc(f_chain, 1)
            dve.wait_ge(f_chain, n * 4 + 2)
            nc.vector.scalar_tensor_tensor(fS, timeS, col(2), fS, ALU.mult, ALU.subtract).then_inc(f_chain, 1)
            dve.wait_ge(f_chain, n * 4 + 3)
            nc.vector.scalar_tensor_tensor(fS, timeS, col(3), fS, ALU.mult, ALU.add).then_inc(f_chain, 1)
            dve.wait_ge(f_chain, n * 4 + 4)
            nc.vector.tensor_scalar(fS, fS, -0.4999999, 0.4999999, ALU.max, ALU.min).then_inc(f_ok, 1)

        def act_tab(act, m, t, first):
            n = m * 4 + t
            act.wait_ge(f_ok, n + 1)
            if not (first and t < 2):
                act.wait_ge(r_chain, (n - 1) * 11)
            nc.scalar.activation(sinS[t % 2], fS, ACT.Sin, scale=TWO_PI).then_inc(tab_chain, 1)
            nc.scalar.activation(cosS[t % 2], fS, ACT.Abs).then_inc(tab_chain, 1)
            act.wait_ge(tab_chain, n * 2 + 2)
            nc.scalar.activation(cosS[t % 2], cosS[t % 2], ACT.Sin, scale=-TWO_PI, bias=half_pi).then_inc(tab_ok, 1)

        def act_eb(act, m, t, first):
            n = m * 4 + t
            act.wait_ge(bu_ok, n + 1)
            if not (first and t < 2):
                act.wait_ge(r_chain, (n - 1) * 11)
                act.wait_ge(vi_ok, n - 1)
            nc.scalar.activation(ubS[t % 2], PS[:, 4:6, :], ACT.Copy).then_inc(eb_ok, 1)

        def act_xt(act, m, i):
            act.wait_ge(xt_pe, m * 2 + (i + 1))
            if not (isinstance(m, int) and m == 0):
                act.wait_ge(bu_ok, m * 4)
            nc.scalar.activation(bT[:, i], PS[:, 7, :].rearrange("p (j c) -> p j c", j=4), ACT.Copy).then_inc(xt_ev, 1)

        def act_yev(act, m1):
            act.wait_ge(y_ok, m1 * 4)
            if not (isinstance(m1, int) and m1 == 1):
                act.wait_ge(y_out, (m1 - 1) * 16)
            nc.scalar.activation(ystS, PS[:, 6, :], ACT.Copy).then_inc(y_ev, 1)

        def dve_r(dve, m, t, first):
            n = m * 4 + t
            co, si, b, x_ = cosS[t % 2], sinS[t % 2], ubS[t % 2], xS[t % 2]
            c0 = n * 11
            mag = prm[:, 0, ds(n, 1)].broadcast_to([P, T])
            dve.wait_ge(eb_ok, n + 1)
            dve.wait_ge(tab_ok, n + 1)
            if not (first and t == 0):
                dve.wait_ge(r_chain, c0)
            nc.vector.tensor_tensor(t1S, co, b[:, 0, :], ALU.mult).then_inc(r_chain, 1)
            nc.vector.tensor_tensor(t2S, si, b[:, 1, :], ALU.mult).then_inc(r_chain, 1)
            dve.wait_ge(r_chain, c0 + 2)
            nc.vector.tensor_tensor(t1S, t1S, t2S, ALU.add).then_inc(r_chain, 1)
            dve.wait_ge(vi_ok, n + 1)
            nc.vector.tensor_tensor_scan(vimS, mag, vimS, 0.0, ALU.mult, ALU.add).then_inc(r_chain, 1)
            dve.wait_ge(r_chain, c0 + 4)
            nc.vector.tensor_tensor_scan(t1S, mag, t1S, 0.0, ALU.mult, ALU.add).then_inc(r_chain, 1)
            if not (first and t < 2):
                dve.wait_ge(y_ok, n - 1)
            nc.vector.tensor_tensor(t2S, si, vimS, ALU.mult).then_inc(r_chain, 1)
            nc.vector.tensor_tensor(t5S, co, vimS, ALU.mult).then_inc(r_chain, 1)
            dve.wait_ge(r_chain, c0 + 7)
            nc.vector.tensor_tensor(x_[:, 0, :], co, t1S, ALU.mult).then_inc(r_chain, 1)
            nc.vector.tensor_tensor(x_[:, 1, :], si, t1S, ALU.mult).then_inc(r_chain, 1)
            dve.wait_ge(r_chain, c0 + 9)
            nc.vector.tensor_tensor(x_[:, 0, :], x_[:, 0, :], t2S, ALU.subtract).then_inc(r_chain, 1)
            nc.vector.tensor_tensor(x_[:, 1, :], x_[:, 1, :], t5S, ALU.add).then_inc(r_chain, 1)

        def pe_xt(pe, m, i, first):
            if i == 0:
                pe.wait_ge(exb_ok, m * 4 + 4)
                if not first:
                    pe.wait_ge(xt_ev, m * 2)
                else:
                    pe.wait_ge(prepE, 9)
            else:
                pe.wait_ge(xt_ev, m * 2 + 1)
            for j_ in range(4):
                mm = nc.tensor.transpose(PS[:, 7, j_ * P:j_ * P + P], exb[:, i, j_, :], ident[:, :])
            mm.then_inc(xt_pe, 1)

        def pe_bu(pe, m, t, first):
            n = m * 4 + t
            if t == 0:
                pe.wait_ge(xt_ev, m * 2 + 2)
                pe.wait_ge(u_in, m * 16 + 16)
            if not (first and t == 0):
                pe.wait_ge(eb_ok, n)
            nc.tensor.matmul(PS[:, 4, :], bT[:, 0, t, :], uS, start=True, stop=True)
            nc.tensor.matmul(PS[:, 5, :], bT[:, 1, t, :], uS, start=True, stop=True).then_inc(bu_ok, 1)

        def pe_y(pe, m, t, first):
            n = m * 4 + t
            if t == 0:
                pe.wait_ge(exc_ok, m * 4 + 4)
                pe.wait_ge(dg_ok, m + 1)
                if not first:
                    pe.wait_ge(y_ev, m * 1)
                nc.tensor.matmul(PS[:, 6, :], dg, uS, start=True, stop=False)
            pe.wait_ge(r_chain, n * 11 + 11)
            nc.tensor.matmul(PS[:, 6, :], exc[:, 0, t, :], xS[t % 2][:, 0, :], start=False, stop=False)
            nc.tensor.matmul(PS[:, 6, :], exc[:, 1, t, :], xS[t % 2][:, 1, :], start=False, stop=(t == 3)).then_inc(y_ok, 1)

        tab_chain = sem("tab_chain")
        half_pi_sb = sb("half_pi", [P, 1])
        half_pi = half_pi_sb[:, 0:1]

        def s5_hooks(m, table):
            def hook(s):
                for step, back, *args in table.get(s, ()):
                    if isinstance(m, int) and (m + back < 0 or m + back > 7):
                        continue
                    step(m + back if back else m, *args, isinstance(m, int) and m + back == 0)
            return hook

        def pe_s5(pe, m):
            xt = lambda g, i, first: pe_xt(pe, g, i, first)
            bu = lambda g, t, first: pe_bu(pe, g, t, first)
            y = lambda g, t, first: pe_y(pe, g, t, first)
            if isinstance(m, int) and m == 0:
                return s5_hooks(m, {0: [(xt, 0, 0)], 1: [(xt, 0, 1)], 2: [(bu, 0, 0)], 3: [(bu, 0, 1)], 4: [(bu, 0, 2)],
                                    5: [(y, 0, 0), (xt, 1, 0)], 6: [(bu, 0, 3)], 7: [(y, 0, 1), (xt, 1, 1)]})
            return s5_hooks(m, {0: [(bu, 0, 0)], 1: [(y, -1, 2)], 2: [(bu, 0, 1)], 3: [(y, -1, 3)], 4: [(bu, 0, 2)],
                                5: [(y, 0, 0), (xt, 1, 0)], 6: [(bu, 0, 3)], 7: [(y, 0, 1), (xt, 1, 1)]})

        def act_s5(act, m):
            tab = lambda g, t, first: act_tab(act, g, t, first)
            eb = lambda g, t, first: act_eb(act, g, t, first)
            xt = lambda g, i, first: act_xt(act, g, i)
            yev = lambda g, first: act_yev(act, g + 1)
            start = isinstance(m, int) and m == 0
            return s5_hooks(m, {0: [(eb, -1, 2)], 1: [(tab, -1, 3)] + ([] if start else [(xt, 0, 0)]),
                                2: [(eb, -1, 3)] + ([] if start else [(xt, 0, 1)]),
                                3: [(tab, 0, 0)] + ([(xt, 0, 0), (xt, 0, 1)] if start else []),
                                4: [(eb, 0, 0)], 5: [(tab, 0, 1)], 6: [(eb, 0, 1), (yev, -1)], 7: [(tab, 0, 2)]})

        def dve_s5(dve, m):
            f = lambda g, t, first: dve_f(dve, g, t, first)
            r = lambda g, t, first: dve_r(dve, g, t, first)
            return s5_hooks(m, {0: [(f, -1, 3)], 1: [(r, -1, 2)], 2: [(f, 0, 0)], 3: [(r, -1, 3)], 4: [(f, 0, 1)], 5: [(r, 0, 0)],
                                6: [(f, 0, 2)], 7: [(r, 0, 1)]})

        def pool_s5(pool, m, store):
            static = isinstance(m, int)
            if not (static and m == 0):
                pool_vi(pool, m - 1, 2, False)
                if not (static and m == 8):
                    pool_s5_u(pool, m, False)
                pool_vi(pool, m - 1, 3, False)
            if not (static and m >= 7):
                pool_s5_b(pool, m + 1, False)
            store(m + (S5C - 1))
            if not (static and m == 8):
                pool_vi(pool, m, 0, static and m == 0)
                pool_s5_c(pool, m, static and m == 0)
                pool_vi(pool, m, 1, False)
            if not (static and m == 0):
                pool_y_out(pool, m - 1)

        selD = a["c_sel"]
        zin, gelu_ok, zhi_ok, zlo_ok, zg_ok = sem("zin"), sem("gelu_ok"), sem("zhi_ok"), sem("zlo_ok"), sem("zg_ok")
        sig_ok, mixs = sem("sig_ok"), sem("mixs")
        fin_, fch = sem("f_in"), sem("fch")
        zS = S[:, 0:4096].rearrange("p (k t) -> p k t", k=8)
        gsS = S[:, 4096:8192].rearrange("p (k t) -> p k t", k=8)
        sgS = [S[:, 12288 + 512 * r:12800 + 512 * r] for r in range(2)]
        yvS = [S[:, 13312 + 512 * r:13824 + 512 * r] for r in range(2)]
        flS, lnS = S[0:8, 14336:14848], S[0:8, 14848:15360]
        mnS = S[0:8, 15360:15872]
        fb = small[0:8, 24:25]

        def act_z(act, s):
            if s in (1, 3):
                k = 4 * (s // 2)
                if s == 1:
                    act.wait_ge(zin, 64)
                nc.scalar.activation(zS[:, k:k + 4, :], zS[:, k:k + 4, :], ACT.Gelu_apprx_tanh).then_inc(gelu_ok, 1)
            if s in (4, 5):
                k = 4 * (s - 4)
                nc.scalar.activation(gsS[:, k:k + 4, :], gsS[:, k:k + 4, :], ACT.Silu).then_inc(gelu_ok, 1)
            if s in (6, 7):
                k = 4 * (s - 6)
                if s == 6:
                    act.wait_ge(gelu_ok, 4)
                nc.scalar.activation(A[:, 32 + k:36 + k, :], zS[:, k:k + 4, :], ACT.Copy).then_inc(zhi_ok, 1)

        def dve_z(dve):
            dve.wait_ge(slot_used, GLU["slot0"])
            for k in range(8):
                dve.wait_ge(zhi_ok, 1 + k // 4)
                nc.vector.tensor_tensor(A[:, 8 + k, :], zS[:, k, :], A[:, 32 + k, :].bitcast(F32), ALU.subtract).then_inc(zlo_ok, 1)
            dve.wait_ge(zlo_ok, 8)
            dve.wait_ge(gelu_ok, 4)
            nc.vector.tensor_tensor(S[:, 4096:8192], S[:, 0:4096], S[:, 4096:8192], ALU.mult).then_inc(zg_ok, 1)

        def act_glu(act, c):
            act.wait_ge(slot_used, GLU["slot0"] + 4 * (c + 1))
            for f in range(4):
                k = 4 * c + f
                if k >= 2:
                    act.wait_ge(mixs, 3 * (k - 2) + 1)
                nc.scalar.activation(sgS[k % 2], PS[:, f, :], ACT.Sigmoid).then_inc(banks_free, 1)

        def dve_glu(dve, c):
            for f in range(4):
                k = 4 * c + f
                dve.wait_ge(banks_free, GLU["bank0"] + k + 1)
                if k == 0:
                    dve.wait_ge(zg_ok, 1)
                if k >= 2:
                    dve.wait_ge(mixs, 3 * (k - 1))
                nc.vector.tensor_tensor(yvS[k % 2], sgS[k % 2], gsS[:, k, :], ALU.mult).then_inc(mixs, 1)
                dve.wait_ge(mixs, 3 * k + 1)
                nc.vector.tensor_copy(A[:, k, :], yvS[k % 2]).then_inc(mixs, 1)
                dve.wait_ge(mixs, 3 * k + 2)
                nc.vector.tensor_tensor(A[:, KM + k, :], yvS[k % 2], A[:, k, :].bitcast(F32), ALU.subtract).then_inc(mixs, 1)

        def act_forget(act):
            act.wait_ge(fin_, 32)
            nc.scalar.activation(lnS, flS, ACT.Abs, bias=fb).then_inc(fch, 1)
            act.wait_ge(fch, 1)
            nc.scalar.activation(lnS, lnS, ACT.Exp, scale=-1.0).then_inc(fch, 1)
            act.wait_ge(fch, 2)
            nc.scalar.activation(lnS, lnS, ACT.Ln, bias=one_sb[0:8, 0:1]).then_inc(fch, 1)

        def dve_forget(dve):
            nc.vector.memset(negcum, 0.0).then_inc(fch2, 1)
            dve.wait_ge(fin_, 32)
            nc.vector.tensor_scalar(mnS, flS, fb, 0.0, ALU.add, ALU.min).then_inc(fch2, 1)
            dve.wait_ge(fch, 3)
            dve.wait_ge(fch2, 2)
            nc.vector.tensor_tensor(mnS, mnS, lnS, ALU.subtract).then_inc(fch2, 1)
            dve.wait_ge(fch2, 3)
            nc.vector.tensor_tensor_scan(mnS, one_sb[0:8, 0:1].broadcast_to([8, T]), mnS, 0.0, ALU.mult, ALU.add).then_inc(fch2, 1)
            dve.wait_ge(fch2, 4)
            nc.vector.tensor_scalar(negcum[0:8, :], mnS, -(128.0 ** 0.5), None, ALU.mult).then_inc(cum_ok, 1)

        fch2 = sem("fch2")
        one_sb = sb("one", [P, 1])


        def dve_out(dve, j, c, h0):
            for t in range(4):
                dve.wait_ge(slot_used, j["slot0"] + j["spc"] * (c + 1))
                if c == 0:
                    dve.wait_ge(rows_in[t], h0 + (32 if t < 2 else 16))
                dst = hrows[:, t, c * COLS:(c + 1) * COLS]
                nc.vector.tensor_tensor(dst, PS[:, t, :], dst, ALU.add).then_inc(banks_free, 1)

        S5C = 2

        maskneg = sb("maskneg", [P, P])
        stats = sb("stats", [P, 16])

        def s_tile(o, k=1):
            return S[:, o:o + 512 * k]

        gate_ld = [sem(f"gate_ld{r}") for r in range(2)]
        gates_before = [0]

        class Att:

            def __init__(self, name, upp, units, tile0, n_heads, base, n_in, in_off, vt, scale, after=None):
                self.name, self.upp, self.units, self.tile0, self.heads = name, upp, units, tile0, n_heads
                self.pairs = n_heads // 2
                self.uph = upp // 2
                self.scale = scale
                self.vt = vt
                self.inp = [[s_tile(in_off + 512 * (n_in * r + i)) for i in range(n_in)] for r in range(2)]
                o = base
                nv = max(1, len(vt))
                self.v = [s_tile(o + 512 * nv * r, nv).rearrange("p (s j d) -> p s j d", s=nv, j=4) for r in range(2)]
                o += 1024 * nv
                self.p = [s_tile(o + 512 * r) for r in range(4)]
                o += 2048
                self.pt = [s_tile(o + 512 * r) for r in range(2)]
                o += 1024
                self.tmp = [s_tile(o + 512 * r) for r in range(2)]
                self.end = o + 1024
                self.b0 = after.b0 + after.pairs if after else 0
                self.tile0 -= 2 * self.b0
                self.sc, self.mx0, self.mx, self.ex = (after.sc, after.mx0, after.mx, after.ex) if after else [
                    sem(f"{name}_{n}") for n in ("scores", "max_step", "max", "exp")]
                self.rc, self.nr, self.tr, self.ev = (after.rc, after.nr, after.tr, after.ev) if after else [
                    sem(f"{name}_{n}") for n in ("reciprocal", "normed", "turned", "turned_out")]
                self.pv, self.vtp, self.vte = (after.pv, after.vtp, after.vte) if after else [
                    sem(f"{name}_{n}") for n in ("values", "v_turned", "v_out")]
                self.fin0, self.fin1, self.fin = (after.fin0, after.fin1, after.fin) if after else [
                    sem(f"{name}_{n}") for n in ("gated", "head_high", "head_low")]
                self.gl0 = gates_before[0] - 16 * self.b0
                gates_before[0] += 16 * self.pairs
                self.ld = after.ld if after else [sem(f"{name}_ld{r}") for r in range(2)]
                self.ld0 = after.ld0 + after.ld_inc * after.pairs if after else 0
                self.done = 2 * self.b0 + n_heads + 2

        def num(b, k, c):
            return b * k + c

        def known_negative(b, k, c):
            return isinstance(b, int) and b * k + c <= 0

        def wait(eng, s_, b, k, c):
            if not known_negative(b, k, c):
                eng.wait_ge(s_, b * k + c)

        SB = (0, 1, 4, 5)
        TB = (2, 6)
        OB = (3, 7)

        def unit(t, x):
            return t.units[x % t.uph]

        def pe_scores(pe, t, b, x):
            u = unit(t, x)
            r = (x // t.uph) % 2
            bank = PS[:, SB[x % 4], :]
            if x % t.uph == 0:
                pe.wait_ge(t.ld[r], b * t.ld_inc + (t.ld_inc * (1 - t.b0) + t.ld0))
            wait(pe, t.ex, b, t.upp, x - 3)
            u["score"](pe, bank, r, b, x)

        def dve_max_1(dve, t, b, x):
            u = unit(t, x)
            w, c = u["w"], x % 4
            bank = PS[:, SB[x % 4], 0:w]
            dve.wait_ge(t.sc, num(b, t.upp, x + 1))
            wait(dve, t.ex, b, t.upp, x - 3)
            if u["bias"]:
                nc.vector.scalar_tensor_tensor(bank, bank, t.scale, u["bias"]((x // t.uph) % 2), ALU.mult, ALU.add).then_inc(t.mx0, 1)
            else:
                nc.vector.tensor_reduce(stats[:, c:c + 1], bank, AX, ALU.max, negate=True).then_inc(t.mx0, 1)

        def dve_max_2(dve, t, b, x):
            u = unit(t, x)
            w, c = u["w"], x % 4
            dve.wait_ge(t.mx0, num(b, t.upp, x + 1))
            if u["bias"]:
                nc.vector.tensor_reduce(stats[:, 4 + c:5 + c], PS[:, SB[x % 4], 0:w], AX, ALU.max, negate=True).then_inc(t.mx, 1)
            else:
                nc.vector.tensor_scalar(stats[:, 4 + c:5 + c], stats[:, c:c + 1], t.scale, None, ALU.mult).then_inc(t.mx, 1)

        def act_exp(act, t, b, x):
            u = unit(t, x)
            w, c = u["w"], x % 4
            act.wait_ge(t.mx, num(b, t.upp, x + 1))
            wait(act, t.tr, b, t.upp, x - 3)
            wait(act, t.nr, b, t.upp, x - 3)
            nc.scalar.activation(t.p[x % 4][:, 0:w], PS[:, SB[x % 4], 0:w], ACT.Exp, bias=stats[:, 4 + c:5 + c],
                                 scale=1.0 if u["bias"] else t.scale, accum_out=stats[:, 8 + c:9 + c]).then_inc(t.ex, 1)

        def dve_recip(dve, t, b, x):
            c = x % 4
            dve.wait_ge(t.ex, num(b, t.upp, x + 1))
            wait(dve, t.nr, b, t.upp, x - 3)
            nc.vector.reciprocal(stats[:, 12 + c:13 + c], stats[:, 8 + c:9 + c]).then_inc(t.rc, 1)

        def dve_norm_p(dve, t, b, x):
            u = unit(t, x)
            w, c = u["w"], x % 4
            dve.wait_ge(t.rc, num(b, t.upp, x + 1))
            if u["gate"]:
                u["gate"](dve, t, b, x, w, c)
            else:
                nc.vector.tensor_scalar(t.p[x % 4][:, 0:w], t.p[x % 4][:, 0:w], stats[:, 12 + c:13 + c], None,
                                        ALU.mult).then_inc(t.nr, 1)

        def pe_turn(pe, t, b, x):
            u = unit(t, x)
            pe.wait_ge(t.nr, num(b, t.upp, x + 1))
            wait(pe, t.ev, b, t.upp, x - 1)
            for j_ in range(u["nb"]):
                mm = nc.tensor.transpose(PS[:, TB[x % 2], j_ * P:j_ * P + P], t.p[x % 4][:, j_ * P:j_ * P + P], ident[:, :])
            mm.then_inc(t.tr, 1)

        def act_turned(act, t, b, x):
            u = unit(t, x)
            n = u["nb"] * P
            act.wait_ge(t.tr, num(b, t.upp, x + 1))
            wait(act, t.pv, b, t.upp, x - 1)
            nc.scalar.activation(t.pt[x % 2][:, 0:n], PS[:, TB[x % 2], 0:n], ACT.Copy).then_inc(t.ev, 1)

        def pe_values(pe, t, b, x):
            u = unit(t, x)
            r = (x // t.uph) % 2
            h0 = x // t.uph
            if x % t.uph == 0:
                if t.vt:
                    pe.wait_ge(t.vte, num(b, 2 * len(t.vt), (h0 + 1) * len(t.vt)))
                wait(pe, t.fin0, b, 2, h0 - 1)
            pe.wait_ge(t.ev, num(b, t.upp, x + 1))
            i = u["i"]
            for j_ in range(u["nb"]):
                mm = nc.tensor.matmul(PS[:, OB[r], i * P:i * P + P], u["v"](r, j_), t.pt[x % 2][:, j_ * P:j_ * P + P],
                                      start=(j_ == 0 and u["first"]), stop=(j_ == u["nb"] - 1 and u["last"]))
            mm.then_inc(t.pv, 1)

        def vt_at(t, x):
            steps = {0: (), 1: (2,), 2: (0, 2)}[len(t.vt)]
            return (x // t.uph, steps.index(x % t.uph)) if x % t.uph in steps else None

        def pe_vt(pe, t, b, x):
            if vt_at(t, x) is None:
                return
            h, k = vt_at(t, x)
            r = h % 2
            if k == 0:
                wait(pe, t.fin0, b, 2, h - 1)
            else:
                pe.wait_ge(t.vte, num(b, 2 * len(t.vt), h * len(t.vt) + k))
            for j_ in range(4):
                mm = nc.tensor.transpose(PS[:, OB[r], j_ * P:j_ * P + P], t.inp[r][t.vt[k]][:, j_ * P:j_ * P + P], ident[:, :])
            mm.then_inc(t.vtp, 1)

        def act_vt(act, t, b, x):
            if vt_at(t, x) is None:
                return
            h, k = vt_at(t, x)
            r = h % 2
            act.wait_ge(t.vtp, num(b, 2 * len(t.vt), h * len(t.vt) + k + 1))
            nc.scalar.activation(t.v[r][:, k, :, :], PS[:, OB[r], :].rearrange("p (j d) -> p j d", j=4), ACT.Copy).then_inc(t.vte, 1)

        def dve_finish(dve, t, b, h):
            r = h % 2
            tile = num(b, 2, t.tile0 + h)
            dve.wait_ge(t.pv, num(b, t.upp, t.uph * (h + 1)))
            wait(dve, t.fin, b, 2, h + 1)
            dve.wait_ge(gate_ld[r], b * 16 + (16 + 16 * (h // 2) + t.gl0))
            nc.vector.tensor_tensor(t.tmp[r], PS[:, OB[r], :], t.inp[r][-1], ALU.mult).then_inc(t.fin0, 1)
            dve.wait_ge(t.fin0, num(b, 2, h + 1))
            nc.vector.tensor_copy(A[:, ds(tile, 1), :], t.tmp[r].unsqueeze(1)).then_inc(t.fin1, 1)
            dve.wait_ge(t.fin1, num(b, 2, h + 1))
            nc.vector.tensor_tensor(A[:, ds(tile + KM, 1), :], t.tmp[r].unsqueeze(1), A[:, ds(tile, 1), :].bitcast(F32),
                                    ALU.subtract).then_inc(t.fin, 1)

        LT, LV = 3, 4

        def run_pairs(eng, t, body):
            body(t.b0, range(0, t.upp))
            with eng.Fori(t.b0 + 1, t.b0 + t.pairs) as b:
                body(b, range(0, t.upp))
            body(t.b0 + t.pairs, range(0, LV + 1), tail=True)

        def pe_att(pe, t):
            def body(b, xs, tail=False):
                first = isinstance(b, int) and b == t.b0
                for x in xs:
                    if not tail:
                        pe_scores(pe, t, b, x)
                        pe_vt(pe, t, b, x)
                    if (x >= LT or not first) and not (tail and x >= LT):
                        pe_turn(pe, t, b, x - LT)
                    if (x >= LV or not first) and not (tail and x >= LV):
                        pe_values(pe, t, b, x - LV)
            run_pairs(pe, t, body)

        def dve_att_start(dve, t):
            for c in (0, 4):
                nc.vector.memset(stats[:, c:c + 1], 0.0).then_inc(t.fin, 1)
            dve.wait_ge(t.fin, 2)

        def dve_att(dve, t):
            if t.b0 == 0:
                dve_att_start(dve, t)
            def body(b, xs, tail=False):
                first = isinstance(b, int) and b == t.b0
                for x in xs:
                    last = (x >= 1 or not first) and not (tail and x >= 1)
                    if (x - LV) % t.uph == 0 and ((x - LV) // t.uph > 0 or not first):
                        dve_finish(dve, t, b, (x - LV) // t.uph - 1)
                    if not tail:
                        dve_max_1(dve, t, b, x)
                    if last:
                        dve_recip(dve, t, b, x - 1)
                    if not tail:
                        dve_max_2(dve, t, b, x)
                    if last:
                        dve_norm_p(dve, t, b, x - 1)
            run_pairs(dve, t, body)

        def act_att(act, t):
            def body(b, xs, tail=False):
                first = isinstance(b, int) and b == t.b0
                for x in xs:
                    if not tail:
                        act_vt(act, t, b, x)
                    if (x >= LT or not first) and not (tail and x >= LT):
                        act_turned(act, t, b, x - LT)
                    if not tail:
                        act_exp(act, t, b, x)
            run_pairs(act, t, body)

        def pool_att(pool, t, load):
            def one(b, h):
                wait(pool, t.sc, b, t.upp, (h - 1) * t.uph)
                if t.vt and not t.units[0]["bias"]:
                    wait(pool, t.vtp, b, 2 * len(t.vt), (h - 1) * len(t.vt))
                else:
                    wait(pool, t.pv, b, t.upp, (h - 1) * t.uph)
                gate = load(pool, num(b, 2, h - 2 * t.b0), h % 2, t.ld[h % 2])
                wait(pool, t.fin0, b, 2, h - 1)
                pool.dma_start(t.inp[h % 2][-1], gate).then_inc(gate_ld[h % 2], 16)
            for h in range(2):
                one(t.b0, h)
            with pool.Fori(t.b0 + 1, t.b0 + t.pairs) as b:
                for h in range(2):
                    one(b, h)

        def causal_mask(bank, w):
            return nc.tensor.matmul(bank[:, w - P:w], ident[:, :], maskneg[:, :], start=False, stop=True)

        ORDER = (3, 0, 2, 1)

        def blocks(score, v, bias=None, gate=None, full=None):
            return [dict(i=i, w=full or (i + 1) * P, nb=(full or (i + 1) * P) // P, score=score(i), v=v, bias=bias, gate=gate,
                         first=True, last=True) for i in ORDER]

        INV_SQ = 128.0 ** -0.5

        negcum = S[:, 15872:16384]

        def fox_score(i):
            def score(pe, bank, r, b, x):
                w = (i + 1) * P
                h0 = x // 4
                if x == 0 and isinstance(b, int):
                    pe.wait_ge(cum_ok, 1)
                q, k = FOX.inp[r][0], FOX.inp[r][1]
                nc.tensor.matmul(bank[:, 0:w], q[:, i * P:i * P + P], k[:, 0:w], start=True, stop=False)
                nc.tensor.matmul(bank[:, 0:w], selS[r], negcum[:, 0:w], start=False, stop=False)
                causal_mask(bank, w).then_inc(FOX.sc, 1)
            return score

        cum_ok = sem("cum_ok")
        FOX = Att("fox", 8, blocks(fox_score, lambda r, j_: FOX.v[r][:, 0, j_, :]), 8, 8, 0, 4, 8192, (2,), INV_SQ)
        FOX.ld_inc = 32
        selS = [s_tile(FOX.end + 128 * r)[:, 0:P] for r in range(2)]

        def fox_load(pool, h, r, s_):
            qkv = S[:, 8192 + 2048 * r:8192 + 2048 * r + 1536].rearrange("p (s t) -> p s t", s=3)
            pool.dma_start(qkv, yE[2048:5120, :].rearrange("(s r) t -> r s t", s=3)[ds(h * P, P), :, :]).then_inc(s_, 16)
            pool.dma_start(selS[r], selD[ds(h, 1), :, :].rearrange("a p n -> (a p) n")).then_inc(s_, 16)
            return yE[ds(h * P + 5120, P), :]

        def mem_att(name, l, y, q_row, g_row, after=None):
            def mem_score(i):
                def score(pe, bank, r, b, x):
                    q, k = t.inp[r][0], t.inp[r][1]
                    nc.tensor.matmul(bank[:, 0:NMEM], q[:, i * P:i * P + P], k[:, 0:NMEM], start=True, stop=True).then_inc(t.sc, 1)
                return score

            t = Att(name, 8, blocks(mem_score, lambda r, j_: t.v[r][:, 0, j_, :], full=NMEM), 16, 4, 8192 - 1024, 3, 4096, (), INV_SQ, after)
            t.ld_inc = 48

            def load(pool, h, r, s_):
                q, k, _ = t.inp[r]
                pool.dma_start(q, y[ds(h * P + q_row, P), :]).then_inc(s_, 16)
                pool.dma_start(k[:, 0:NMEM], kmD[l][ds(h * P, P), :]).then_inc(s_, 16)
                pool.dma_start(t.v[r][:, 0, 0:2, :], vmD[l][:, ds(h * P, P)].rearrange("(j p) d -> p j d", p=P)).then_inc(s_, 16)
                return y[ds(h * P + g_row, P), :]
            return t, load

        MEM0, mem0_load = mem_att("mem0", 0, yE, 6144, 6656)

        h1D = dram("h1D", (T, D))
        biasD = dram("biasD", (8, P, LB))
        quD = dram("quD", (1536, T))
        kvD = dram("kvD", (2048, T))
        cmpD = dram("cmpD", (2, P, NPAD + P))
        h1_out = sem("h1_out")
        t5c = sb("t5c", [P, 33 * 8 + 8])
        thr = sb("thr", [P, 33])
        pec = sb("pec", [P, 2, 32])
        cols = sb("cols", [P, 16])
        ones = sb("ones", [P, P])
        posi = small[:, 32:36].bitcast(I32)
        const_in, const_ok = sem("const_in"), sem("const_ok")
        OFF = [0, 160, 448, 864]
        accS = S[:, 0:8 * LB].rearrange("p (h n) -> p h n", h=8)
        distS = S[:, 11264:11264 + LB]
        termS = [S[:, 12672 + LB * r:12672 + LB * (r + 1)] for r in range(2)]
        indS = S[:, 15488:15488 + 704].bitcast(mybir.dt.bfloat16)
        poskS = termS[0][:, 0:512]
        poskI = termS[1][:, 0:512].bitcast(I32)
        tabS = termS[1][:, 512:768]
        t5_in, t5_step, t5_ind, t5_acc, t5_term, t5_add, t5_out = [sem(n) for n in
            ("t5_in", "t5_step", "t5_ind", "t5_acc", "t5_term", "t5_add", "t5_out")]
        cm01 = sb("cm01", [P, 4, NPAD])
        cmneg = sb("cmneg", [P, 4, NPAD])
        HV = 5

        def pool_consts(pool):
            pool.dma_start(thr[:, 0:31], a["c_thr"]).then_inc(const_in, 16)
            pool.dma_start(cols[:, 0:1], a["c_inv"]).then_inc(const_in, 16)
            pool.dma_start(cols[:, 1:2], a["c_sgn"]).then_inc(const_in, 16)
            pool.dma_start(posi, a["positions"][0].rearrange("(i p) -> p i", p=P)).then_inc(const_in, 16)
            pool.dma_start(cols[:, 8:12], a["mla_g_cq"][0].rearrange("(k p) -> p k", p=P)).then_inc(const_in, 16)
            pool.dma_start(cols[:, 12:16], a["mla_g_ckv"][0].rearrange("(k p) -> p k", p=P)).then_inc(const_in, 16)
            pool.dma_start(pec[:, :, :], a["nsa_cmp_pe"][0].rearrange("k l d -> d k l")).then_inc(const_in, 16)
            nc.gpsimd.memset(thr[:, 31:33], 1e30).then_inc(const_ok, 1)
            nc.gpsimd.memset(ones[:, :], 1.0).then_inc(const_ok, 1)
            nc.gpsimd.memset(cm01[:, :, :], 1.0).then_inc(const_ok, 1)
            nc.gpsimd.memset(cmneg[:, :, :], 0.0).then_inc(const_ok, 1)
            pool.wait_ge(const_ok, 4)
            for m_, fill in ((cm01, 0.0), (cmneg, NEG)):
                nc.gpsimd.affine_select(out=m_[:, :, :], in_=m_[:, :, :], compare_op=ALU.is_ge, fill=fill, base=-31,
                                        pattern=[[P, 4], [-16, NPAD]], channel_multiplier=1).then_inc(const_ok, 1)
            pool.wait_ge(const_ok, 6)

        def pool_t5_loads(pool):
            pool.wait_ge(nt_pe, 3 * KD)
            pool.dma_start(poskI, a["positions"].broadcast_to([P, T])).then_inc(t5_in, 16)
            pool.dma_start(tabS, a["t5_table"].rearrange("(a b) h -> a (b h)", a=1).broadcast_to([P, 256])).then_inc(t5_in, 16)

        def dve_t5_start(dve):
            dve.wait_ge(t5_in, 32)
            dve.wait_ge(const_in, 7 * 16)
            dve.wait_ge(const_ok, 6)
            nc.vector.tensor_copy(poskS, poskI).then_inc(t5_step, 1)
            nc.vector.tensor_copy(cols[:, 4:8], posi).then_inc(t5_step, 1)
            nc.vector.memset(t5c[:, 248:264], 0.0).then_inc(t5_step, 1)
            nc.vector.tensor_tensor(t5c[:, 0:248], tabS[:, 8:256], tabS[:, 0:248], ALU.subtract).then_inc(t5_step, 1)
            nc.vector.tensor_copy(t5c[:, 264:272], tabS[:, 0:8]).then_inc(t5_step, 1)
            dve.wait_ge(t5_step, 5)
            for i in range(4):
                w = (i + 1) * P
                q = cols[:, 4 + i:5 + i]
                for dst, src in ((distS[:, OFF[i]:OFF[i] + w], poskS[:, 0:w]),
                                 (distS[:, OFF[i] + w:OFF[i] + w + 31], poskS[:, 31:512:16]),
                                 (distS[:, OFF[i] + w + 31:OFF[i] + w + 32], poskS[:, 511:512])):
                    nc.vector.tensor_scalar(dst, src, q, -1.0, ALU.subtract, ALU.mult).then_inc(t5_step, 1)
            dve.wait_ge(t5_step, 17)
            for h in range(8):
                nc.vector.tensor_scalar(accS[:, h, :], distS, 0.0, t5c[:, 264 + h:265 + h], ALU.mult, ALU.add).then_inc(t5_step, 1)
            dve.wait_ge(t5_step, 25)

        def dve_t5_ind(dve, c, k, first):
            if not (first and k == 0):
                dve.wait_ge(t5_term, num(c, 9, 3 * k - 9))
                dve.wait_ge(t5_acc, num(c, 3 * HV, HV * k - 3 * HV))
            nc.vector.tensor_scalar(indS, distS, thr[:, ds(c * 3 + (k - 3), 1)], None, ALU.is_ge).then_inc(t5_ind, 1)

        def dve_t5_acc(dve, c, k, h):
            if h == 0:
                dve.wait_ge(t5_ind, num(c, 3, k - 2))
            if not (isinstance(c, int) and c == 1 and k == 0):
                dve.wait_ge(t5_acc, num(c, 3 * HV, HV * k + h - 4 * HV + 1))
            nc.vector.scalar_tensor_tensor(accS[:, h, :], indS, t5c[:, ds(c * 24 + (8 * k + h - 24), 1)], accS[:, h, :],
                                           ALU.mult, ALU.add).then_inc(t5_acc, 1)

        T5BUF = [termS[0], termS[1], termS[0]]

        def act_t5_term(act, c, k, j_, first):
            act.wait_ge(t5_ind, num(c, 3, k - 2))
            back = (0, 2, 1)[j_]
            if not (first and 3 * k + j_ - back <= 0):
                act.wait_ge(t5_add, num(c, 9, 3 * k + j_ - 9 - back))
            nc.scalar.activation(T5BUF[j_], indS, ACT.Copy, scale=t5c[:, ds(c * 24 + (8 * k + HV + j_ - 24), 1)]).then_inc(t5_term, 1)

        def pool_t5_add(pool, c, k, j_):
            pool.wait_ge(t5_term, num(c, 9, 3 * k + j_ - 8))
            nc.gpsimd.tensor_tensor(accS[:, HV + j_, :], accS[:, HV + j_, :], T5BUF[j_], ALU.add).then_inc(t5_add, 1)

        def dve_t5_hook(dve, c, first):
            todo = [[("i", 0), (0, 0)], [(0, 1), (0, 2)], [(0, 3), (0, 4)], [("i", 1), (1, 0), (1, 1)], [(1, 2), (1, 3), (1, 4)],
                    [("i", 2), (2, 0), (2, 1)], [(2, 2), (2, 3)], [(2, 4)]]

            def hook(s):
                for k, h in todo[s]:
                    if k == "i":
                        dve_t5_ind(dve, c, h, first)
                    else:
                        dve_t5_acc(dve, c, k, h)
            return hook

        def act_t5_hook(act, c, first):
            todo = [[], [(0, 0)], [(0, 1)], [(0, 2)], [(1, 0)], [(1, 1), (1, 2)], [(2, 0)], [(2, 1), (2, 2)]]

            def hook(s):
                for k, j_ in todo[s]:
                    act_t5_term(act, c, k, j_, first)
            return hook

        def dve_t5_end(dve, i):
            if i == 0:
                dve.wait_ge(t5_add, 99)
                dve.wait_ge(t5_acc, 33 * HV)
            w = (i + 1) * P
            for o, n, m_ in ((OFF[i] + w - P, P, maskneg[:, :]), (OFF[i] + w, NPAD, cmneg[:, i, :])):
                v = accS[:, :, o:o + n]
                nc.vector.tensor_tensor(v, v, m_.unsqueeze(1).broadcast_to([P, 8, n]), ALU.add).then_inc(t5_step, 1)

        XS = [S[:, 2048 * k:2048 * k + 2048].rearrange("p (g n l) -> p g n l", g=2, n=32) for k in range(2)]
        rawS = [S[:, 4096 + 1024 * k:5120 + 1024 * k].rearrange("p (g t) -> p g t", g=2) for k in range(2)]
        w1S = [S[:, 6144 + 2048 * r:8192 + 2048 * r].rearrange("p (l h) -> p l h", l=8) for r in range(2)]
        cS = S[:, 11264:15360].rearrange("p (k t) -> p k t", k=8)
        sqS = [S[:, 15360 + 512 * r:15872 + 512 * r] for r in range(2)]
        rrS = [PS[:, 6 + r, :] for r in range(2)]
        w2S = S[:, 4096:4608].rearrange("p (k h d) -> p k h d", k=2, h=2)
        hcS = S[:, 4608:4864].rearrange("p (k h n) -> p k h n", k=2, h=2)
        vcS = S[:, 4864:5120].rearrange("p (g d) -> p g d", g=2)
        kcS = S[:, 15872:15936].rearrange("p (g n) -> p g n", g=2)
        c_in, cmp_in, w1_in, w1_used, x_ok = sem("c_in"), sem("cmp_in"), [sem(f"w1_in{r}") for r in range(2)], sem("w1_used"), sem("x_ok")
        sq_ok, ss_pe, rr_step, rr_root, cn_step, cn_ok = [sem(n) for n in ("sq_ok", "ss_pe", "rr_step", "rr_root", "cn_step", "cn_ok")]
        cmp_g, w2_in, vc_zero, cmp2_pe, cmp2_ok, cmp_out = [sem(n) for n in ("cmp_g", "w2_in", "vc_zero", "cmp2_pe", "cmp2_ok", "cmp_out")]

        def pool_c(pool):
            pool.wait_ge(t5_acc, 33 * HV)
            pool.wait_ge(t5_add, 99)
            pool.wait_ge(stored, 16 * (O1["stored0"] + 2))
            for k in range(2):
                pool.dma_start(cS[:, 4 * k:4 * k + 4, :], yO[512 * k:512 * k + 512, :].rearrange("(f p) t -> p f t", p=P)).then_inc(c_in, 16)

        def pool_cmp(pool):
            pool.wait_ge(t5_out, 16)
            for k in range(2):
                pool.dma_start(rawS[k], yO[2048 + 256 * k:2304 + 256 * k, :].rearrange("(g p) t -> p g t", p=P)).then_inc(cmp_in, 16)

        def pool_w1(pool, n):
            if n >= 2:
                pool.wait_ge(w1_used, n - 1)
            r0 = (n % 4) * 1024
            pool.dma_start(w1S[n % 2], a["nsa_cmp_w1"][0][n // 4, r0:r0 + 1024, :].rearrange("(l d) h -> d l h", d=P)).then_inc(w1_in[n % 2], 16)

        def pool_w2(pool):
            pool.wait_ge(x_ok, 4)
            nc.gpsimd.memset(vcS, 0.0).then_inc(vc_zero, 1)
            pool.dma_start(w2S, a["nsa_cmp_w2"][0].rearrange("k (h q) d -> q k h d", q=P)).then_inc(w2_in, 16)

        def pool_cmp_out(pool):
            pool.wait_ge(cmp2_ok, 3)
            pool.dma_start(cmpD[:, :, 0:NPAD].rearrange("g p n -> p g n"), kcS).then_inc(cmp_out, 16)
            pool.dma_start(cmpD[:, :, NPAD:].rearrange("g p d -> p g d"), vcS).then_inc(cmp_out, 16)
            pool.wait_ge(cmp_out, 32)

        def dve_x(dve):
            dve.wait_ge(cmp_in, 32)
            for k in range(2):
                raw, pe_ = rawS[k], pec[:, k, :]
                rv = bass.AP(tensor=raw.tensor, offset=raw.offset, ap=[raw.ap[0], [512, 2], [16, 31], [1, 32]])
                pv = bass.AP(tensor=pe_.tensor, offset=pe_.offset, ap=[pe_.ap[0], [0, 2], [0, 31], [1, 32]])
                nc.vector.tensor_tensor(XS[k][:, :, 0:31, :], rv, pv, ALU.add).then_inc(x_ok, 1)
                nc.vector.memset(XS[k][:, :, 31, :], 0.0).then_inc(x_ok, 1)

        def dve_c(dve):
            for k in range(2):
                var, r = rrS[k], sqS[k]
                n0 = 6 * k
                dve.wait_ge(ss_pe, 8)
                nc.vector.tensor_scalar(var, var, 1.0 / 512, EPS, ALU.mult, ALU.add).then_inc(rr_step, 1)
                dve.wait_ge(rr_root, k + 1)
                nc.vector.reciprocal(r, r).then_inc(rr_step, 1)
                dve.wait_ge(rr_step, n0 + 2)
                nc.vector.tensor_tensor(var, var, r, ALU.mult).then_inc(rr_step, 1)
                dve.wait_ge(rr_step, n0 + 3)
                nc.vector.tensor_tensor(var, var, r, ALU.mult).then_inc(rr_step, 1)
                dve.wait_ge(rr_step, n0 + 4)
                nc.vector.tensor_scalar(var, var, -0.5, 1.5, ALU.mult, ALU.add).then_inc(rr_step, 1)
                dve.wait_ge(rr_step, n0 + 5)
                nc.vector.tensor_tensor(r, r, var, ALU.mult).then_inc(rr_step, 1)
            dve.wait_ge(rr_step, 12)

        def dve_cn(dve, half):
            for k in range(4 * half, 4 * half + 4):
                v = cS[:, k, :]
                nc.vector.scalar_tensor_tensor(v, v, cols[:, 8 + k:9 + k], sqS[k // 4], ALU.mult, ALU.mult).then_inc(cn_step, 1)
                dve.wait_ge(cn_step, 2 * k + 1)
                nc.vector.tensor_copy(A[:, 32 + k, :], v).then_inc(cn_step, 1)

        def dve_cn_low(dve, half):
            dve.wait_ge(slot_used, UQ["slot0"])
            dve.wait_ge(cn_step, 8 * half + 8)
            for k in range(4 * half, 4 * half + 4):
                nc.vector.tensor_tensor(A[:, 8 + k, :], cS[:, k, :], A[:, 32 + k, :].bitcast(F32), ALU.subtract).then_inc(cn_ok, 1)

        def dve_c2(dve):
            dve.wait_ge(cmp2_pe, 2)
            nc.vector.tensor_copy(kcS, PS[:, 4, 0:64].rearrange("p (g n) -> p g n", g=2)).then_inc(cmp2_ok, 1)
            dve.wait_ge(vc_zero, 1)
            for g in range(2):
                nc.vector.tensor_copy(vcS[0:NPAD, g, :], PS[0:NPAD, 5, g * P:g * P + P]).then_inc(cmp2_ok, 1)

        def act_c(act, s):
            if 2 <= s < 6:
                if s == 2:
                    act.wait_ge(c_in, 32)
                for k in (2 * s - 4, 2 * s - 3):
                    if k >= 2:
                        act.wait_ge(ss_pe, k - 1)
                    nc.scalar.activation(sqS[k % 2], cS[:, k, :], ACT.Square).then_inc(sq_ok, 1)

        def act_c_root(act):
            for k in range(2):
                act.wait_ge(rr_step, 6 * k + 1)
                nc.scalar.activation(sqS[k], rrS[k], ACT.Sqrt).then_inc(rr_root, 1)

        def act_c2(act):
            for k in range(2):
                act.wait_ge(w1_used, 4 * k + 4)
                if k == 0:
                    act.wait_ge(x_ok, 4)
                for h in range(2):
                    nc.scalar.activation(hcS[:, k, h, :], PS[:, 4 + 2 * k + h, 0:64], ACT.Gelu_apprx_tanh).then_inc(cmp_g, 1)

        def pe_c(pe, s):
            if 2 <= s < 6:
                for k in (2 * s - 4, 2 * s - 3):
                    pe.wait_ge(sq_ok, k + 1)
                    nc.tensor.matmul(PS[:, 6 + k // 4, :], ones[:, :], sqS[k % 2], start=(k % 4 == 0), stop=(k % 4 == 3)).then_inc(ss_pe, 1)

        W1_AT = (3, 5, 6, 8, 9, 11, 12, 13)

        def pe_w1(pe, at):
            for n, g in enumerate(W1_AT):
                if g != at:
                    continue
                if n == 0:
                    pe.wait_ge(x_ok, 4)
                if n == 4:
                    pe.wait_ge(rr_step, 12)
                pe.wait_ge(w1_in[n % 2], 16 * (n // 2 + 1))
                k = n // 4
                for l in range(8 * (n % 4), 8 * (n % 4) + 8):
                    for h in range(2):
                        mm = nc.tensor.matmul(PS[:, 4 + 2 * k + h, 0:64].rearrange("p (g n) -> p g n", g=2),
                                              w1S[n % 2][:, l % 8, h * P:h * P + P], XS[k][:, :, :, l], start=(l == 0), stop=(l == 31))
                mm.then_inc(w1_used, 1)

        def pe_c2(pe):
            pe.wait_ge(cmp_g, 4)
            pe.wait_ge(w2_in, 16)
            for h in range(2):
                mm = nc.tensor.matmul(PS[:, 4, 0:64], w2S[:, 0, h, :], hcS[:, 0, h, :], start=(h == 0), stop=(h == 1))
            mm.then_inc(cmp2_pe, 1)
            for g in range(2):
                for h in range(2):
                    mm = nc.tensor.matmul(PS[0:NPAD, 5, g * P:g * P + P], hcS[:, 1, h, g * NPAD:g * NPAD + NPAD], w2S[:, 1, h, :],
                                          start=(h == 0), stop=(h == 1))
            mm.then_inc(cmp2_pe, 1)

        def mla_score(i):
            def score(pe, bank, r, b, x):
                w = (i + 1) * P
                q, k = MLA.inp[r][0], MLA.inp[r][1]
                nc.tensor.matmul(bank[:, 0:w], q[:, i * P:i * P + P], k[:, 0:w], start=True, stop=False)
                if x % 4 == 0:
                    pe.wait_ge(rope_ok, num(b, 2, x // 4 + 3 - 2 * MLA.b0))
                half = slice(64 * r, 64 * r + 64)
                nc.tensor.matmul(bank[:, 0:w], qrS[half, i * P:i * P + P], krS[half, 0:w], start=False, stop=False)
                causal_mask(bank, w).then_inc(MLA.sc, 1)
            return score

        MLA = Att("mla", 8, blocks(mla_score, lambda r, j_: MLA.v[r][:, 0, j_, :]), 0, 8, 0, 4, 5120, (2,), 192.0 ** -0.5, FOX)
        MLA.ld_inc = 32
        qrS, krS = s_tile(10240), s_tile(11264)
        qa, qb = s_tile(11776), s_tile(12800)
        angS, turnS = s_tile(13824), s_tile(14336)
        posrS, posrI = s_tile(14848), s_tile(15360).bitcast(I32)
        sinR, cosR = turnS, posrS
        rope_ok, rope_in, rope_t, rope_tab, kr_in = sem("rope_ok"), sem("rope_in"), sem("rope_t"), sem("rope_tab"), sem("kr_in")
        rope_ld, rope_c = sem("rope_ld"), sem("rope_c")

        def pool_rotary(pool, src, s_):
            for e in range(2):
                pool.dma_start(qa[64 * e:64 * e + 64, :], src(e, 0, 64)).then_inc(s_, 16)
                pool.dma_start(qb[64 * e:64 * e + 32, :], src(e, 32, 32)).then_inc(s_, 16)
                pool.dma_start(qb[64 * e + 32:64 * e + 64, :], src(e, 0, 32)).then_inc(s_, 16)

        def pool_rope_start(pool):
            pool.wait_ge(cn_ok, 8)
            pool.dma_start(posrI, a["positions"].broadcast_to([P, T])).then_inc(rope_in, 16)
            pool_rotary(pool, lambda e, o, n: yO[6656 + o:6656 + o + n, :], kr_in)

        def dve_rope(dve):
            dve.wait_ge(rope_in, 16)
            n = [0]

            def step(ins):
                n[0] += 1
                ins.then_inc(rope_t, 1)
                dve.wait_ge(rope_t, n[0])
            step(nc.vector.tensor_copy(posrS, posrI))
            step(nc.vector.tensor_scalar(angS, posrS, cols[:, 0:1], None, ALU.mult))
            step(nc.vector.tensor_scalar(turnS, angS, 1.0 / TWO_PI, MAGIC, ALU.mult, ALU.add))
            step(nc.vector.tensor_scalar(turnS, turnS, MAGIC, None, ALU.subtract))
            for cst in (C1, C2, C3):
                step(nc.vector.scalar_tensor_tensor(angS, turnS, -cst, angS, ALU.mult, ALU.add))
            step(nc.vector.tensor_scalar(angS, angS, -3.1415925, 3.1415925, ALU.max, ALU.min))

        def dve_rope_sign(dve):
            dve.wait_ge(rope_tab, 3)
            nc.vector.tensor_scalar(sinR, sinR, cols[:, 1:2], None, ALU.mult).then_inc(rope_t, 1)

        def act_rope(act):
            act.wait_ge(rope_t, 8)
            nc.scalar.activation(sinR, angS, ACT.Sin).then_inc(rope_tab, 1)
            nc.scalar.activation(cosR, angS, ACT.Abs).then_inc(rope_tab, 1)
            act.wait_ge(rope_tab, 2)
            nc.scalar.activation(cosR, cosR, ACT.Sin, scale=-1.0, bias=half_pi).then_inc(rope_tab, 1)

        def pool_turn(pool, n):
            nc.gpsimd.tensor_tensor(qa, qa, cosR, ALU.mult).then_inc(rope_c, 1)
            nc.gpsimd.tensor_tensor(qb, qb, sinR, ALU.mult).then_inc(rope_c, 1)
            pool.wait_ge(rope_c, n * 2 + 2)

        def pool_sum(pool, dst, e):
            half = slice(64 * e, 64 * e + 64)
            nc.gpsimd.tensor_tensor(dst[half, :], qa[half, :], qb[half, :], ALU.add).then_inc(rope_ok, 1)

        def mla_load(pool, h, r, s_):
            static = isinstance(h, int)
            kv = S[:, 5120 + 2048 * r + 512:5120 + 2048 * r + 1536].rearrange("p (s t) -> p s t", s=2)
            pool.dma_start(MLA.inp[r][0], quD[ds(h * 192, P), :]).then_inc(s_, 16)
            pool.dma_start(kv, kvD[ds(h * 256, 2 * P), :].rearrange("(s p) t -> p s t", s=2)).then_inc(s_, 16)
            if r == 0:
                if not static:
                    pool.wait_ge(rope_ok, h + 2)
                pool_rotary(pool, lambda e, o, n: quD[ds(h * 192 + (192 * e + P + o), n), :], rope_ld)
                pool.wait_ge(rope_ld, 96 if static else h * 48 + 96)
                pool_turn(pool, 1 if static else h // 2 + 1)
            pool_sum(pool, qrS, r)
            return yO[ds(h * P + 4096, P), :]

        gtmS = sb("gtm", [P, 4, 24])
        gateL = S[0:24, 15872:16384]
        glog_in, glog_pe, glog_ok, p_zero = sem("glog_in"), sem("glog_pe"), sem("glog_ok"), sem("p_zero")

        def nsa_score(which, w):
            def score(pe, bank, r, b, x):
                k = NSA.inp[r][1 + 2 * which][:, 0:w] if which < 2 else kcB[r]
                i = unit(NSA, x)["i"]
                nc.tensor.matmul(bank[:, 0:w], NSA.inp[r][0][:, i * P:i * P + P], k, start=True, stop=True).then_inc(NSA.sc, 1)
            return score

        def nsa_gate(i, branch):
            def gate(dve, t, b, x, w, c):
                p = t.p[x % 4][:, 0:w]
                nc.vector.tensor_scalar(p, p, stats[:, 12 + c:13 + c], gtmS[:, i, ds(num(b, 6, 3 * (x // 12) + branch), 1)],
                                        ALU.mult, ALU.mult).then_inc(t.nr, 1)
            return gate

        def nsa_units():
            out_ = []
            for i in ORDER:
                w = (i + 1) * P
                for which in (0, 2, 1):
                    o = OFF[i] + (w if which == 2 else 0)
                    n = NPAD if which == 2 else w
                    out_.append(dict(i=i, w=n, nb=1 if which == 2 else i + 1, score=nsa_score(which, n),
                                     v=(lambda r, j_, k=which: NSA.v[r][:, k, j_, :] if k < 2 else vcB[r]),
                                     bias=(lambda r, o=o, n=n: biasB[r][:, o:o + n]), gate=nsa_gate(i, (1, 2, 0)[which]),
                                     first=which == 0, last=which == 1))
            return out_

        NSA = Att("nsa", 24, nsa_units(), 8, 8, 0, 6, 6144, (2, 4), INV_SQ)
        NSA.ld_inc = 16 * 4
        biasB = [S[:, 12288 + LB * r:12288 + LB * (r + 1)] for r in range(2)]
        kcB = [S[:, 15104 + 160 * r:15136 + 160 * r] for r in range(2)]
        vcB = [S[:, 15136 + 160 * r:15264 + 160 * r] for r in range(2)]

        def nsa_load(pool, h, r, s_):
            grp = h // 4
            kv = S[:, 6144 + 3072 * r + 512:6144 + 3072 * r + 2560].rearrange("p (s t) -> p s t", s=4)
            pool.dma_start(NSA.inp[r][0], yO[ds(h * P + 1024, P), :]).then_inc(s_, 16)
            pool.dma_start(kv, yO[2560:3584, :].rearrange("(s r) t -> r s t", s=4)[ds(grp * P, P), :, :]).then_inc(s_, 16)
            pool.dma_start(biasB[r], biasD[ds(h, 1), :, :].rearrange("a p n -> (a p) n")).then_inc(s_, 16)
            pool.dma_start(S[:, 15104 + 160 * r:15264 + 160 * r], cmpD[ds(grp, 1), :, :].rearrange("a p n -> (a p) n")).then_inc(s_, 16)
            return yO[ds(h * P + 5120, P), :]

        def pe_nsa_gates(pe):
            pe.wait_ge(glog_in, 16)
            for i in range(4):
                mm = nc.tensor.transpose(PS[:, 6, i * 24:i * 24 + 24], gateL[:, i * P:i * P + P], ident[0:24, 0:24])
            mm.then_inc(glog_pe, 1)

        def act_nsa_gates(act):
            act.wait_ge(glog_pe, 1)
            nc.scalar.activation(gtmS[:, :, :], PS[:, 6, 0:96].rearrange("p (i c) -> p i c", i=4), ACT.Sigmoid).then_inc(glog_ok, 1)

        MEM1, mem1_load = mem_att("mem1", 1, yO, 3584, 6144, MEM0)

        gfS = S[:, 8192:10240]
        gf_in, fin_ok, out_sem = sem("gf_in"), sem("fin_ok"), sem("out_sem")

        def dve_final(dve):
            dve_norm(dve, NORMS[3])
            r = small[:, 20:24]
            dve.wait_ge(rows_ok, 14)
            dve.wait_ge(gf_in, 16)
            for t in range(4):
                nc.vector.scalar_tensor_tensor(hrows[:, t, :], hrows[:, t, :], r[:, t:t + 1], gfS, ALU.mult, ALU.mult).then_inc(fin_ok, 1)

        block = ctx.enter_context(nc.Block())

        @block.sync
        def _(sp):
            for j in plan:
                for c0, c1, _ in j["parts"]:
                    if j["spc"] % RAW == 0 and c1 - c0 > 2:
                        sp_chunk(sp, j, c0)
                        with sp.Fori(c0 + 1, c1) as c:
                            sp_chunk(sp, j, c, c0)
                    else:
                        for c in range(c0, c1):
                            sp_chunk(sp, j, c)

        @block.gpsimd
        def _(pool):
            nc.gpsimd.memset(half_pi_sb[:, :], math.pi / 2).then_inc(ident_ok, 1)
            nc.gpsimd.memset(one_sb[:, :], 1.0).then_inc(ident_ok, 1)
            nc.gpsimd.memset(maskneg[:, :], 0.0).then_inc(ident_ok, 1)
            nc.gpsimd.memset(ident[:, :], 0.0).then_inc(ident_ok, 1)
            pool.wait_ge(ident_ok, 4)
            nc.gpsimd.affine_select(out=maskneg[:, :], in_=maskneg[:, :], compare_op=ALU.is_ge, fill=NEG, base=0,
                                    pattern=[[-1, P]], channel_multiplier=1).then_inc(ident_ok, 1)
            nc.gpsimd.affine_select(out=ident[:, :], in_=ident[:, :], compare_op=ALU.not_equal, fill=1.0, base=0,
                                    pattern=[[-1, P]], channel_multiplier=1).then_inc(ident_ok, 1)
            pool.dma_start(hrows[:, 0, :], mem[0:P, :]).then_inc(rows_in[0], 16)
            pool.dma_start(hrows[:, 1, :], mem[P:2 * P, :]).then_inc(rows_in[1], 16)
            for i, g in enumerate((a["norm_g"][0], a["norm_g"][1], a["mem_norm_g"])):
                pool.dma_start(gcol[:, i, :], g.rearrange("(k p) -> p k", p=P)).then_inc(gains_in, 16)
            pool_prep_loads(pool)
            pool_consts(pool)
            pool.wait_ge(nt_pe, KD)
            for t in range(TT):
                pool.dma_start(hrows[:, t, :], x[t * P:(t + 1) * P, :]).then_inc(rows_in[t], 16)
            pool_prep(pool)
            assert (prep_angle_n, prep_den_n, prep_all_n) == (prep_angle[0], prep_den_at[0], prep_all[0])
            for l in range(2):
                pool_store(pool, jobs[f"memk{l}"], 0, kmD[l].rearrange("(f p) t -> p f t", p=P))
                pool_store(pool, jobs[f"memv{l}"], 0, vmD[l].rearrange("(f p) t -> p f t", p=P))

            def store(c):
                pool_store(pool, E1, c, yE[ds(c * COLS, COLS), :].rearrange("(f p) t -> p f t", p=P))

            store(0)
            pool_cprime(pool)
            pool.wait_ge(stored, 16 * (E1["stored0"] + 1))
            pool_s5_b(pool, 0, True)
            pool_s5_u(pool, 0, True)
            pool_s5(pool, 0, store)
            with pool.Fori(1, 7) as m:
                pool_s5(pool, m, store)
            pool_s5(pool, 7, store)
            pool_s5(pool, 8, store)
            pool.wait_ge(y_out, 16 * 8)
            pool.wait_ge(y_ok, 32)
            pool.wait_ge(r_chain, 32 * 11)
            for k in range(2):
                pool.dma_start(zS[:, 4 * k:4 * k + 4, :], yS[512 * k:512 * k + 512, :].rearrange("(f p) t -> p f t", p=P)).then_inc(zin, 16)
                pool.dma_start(gsS[:, 4 * k:4 * k + 4, :], yE[1024 + 512 * k:1536 + 512 * k, :].rearrange("(f p) t -> p f t", p=P)).then_inc(zin, 16)
            with pool.Fori(10, E1["chunks"]) as c:
                store(c)
            pool.wait_ge(stored, 16 * E2["stored0"])
            pool.dma_start(fb, a["fox_b_f"][0].rearrange("(h a) -> h a", a=1)).then_inc(fin_, 16)
            pool_store(pool, E2, 0, yE[7168:7176, :])
            pool.wait_ge(stored, 16 * (E2["stored0"] + 1))
            pool.dma_start(flS, yE[7168:7176, :]).then_inc(fin_, 16)
            pool.wait_ge(mixs, 24)
            pool_att(pool, FOX, fox_load)
            pool.wait_ge(FOX.fin, FOX.done)
            pool_att(pool, MEM0, mem0_load)
            pool.wait_ge(MEM0.fin, MEM0.done)
            for t in range(TT):
                pool.dma_start(hrows[:, t, :], x[t * P:(t + 1) * P, :]).then_inc(rows_in[t], 16)
            pool.wait_ge(banks_free, OUT0["bank0"] + 16)
            pool.dma_start(h1D.rearrange("(t p) d -> p t d", p=P), hrows).then_inc(h1_out, 16)
            pool_t5_loads(pool)

            def store_o(c):
                pool_store(pool, O1, c, yO[ds(c * COLS, COLS), :].rearrange("(f p) t -> p f t", p=P))
            with pool.Fori(1, 12) as c:
                store_o(c - 1)
                for k in range(3):
                    for j_ in range(3):
                        pool_t5_add(pool, c, k, j_)
            pool_c(pool)
            store_o(11)
            pool.wait_ge(t5_step, 33)
            pool.dma_start(biasD.rearrange("h p n -> p h n"), accS).then_inc(t5_out, 16)
            store_o(12)
            pool.wait_ge(stored, 16 * O2["stored0"])
            pool_store(pool, O2, 0, yO[6656:6744, :])
            pool.wait_ge(stored, 16 * (O2["stored0"] + 1))

            def store_uq(c):
                pool_store(pool, UQ, c, quD[c * COLS:(c + 1) * COLS, :].rearrange("(f p) t -> p f t", p=P))

            def store_ukv(c):
                pool_store(pool, UKV, c, kvD[c * COLS:(c + 1) * COLS, :].rearrange("(f p) t -> p f t", p=P))
            pool_cmp(pool)
            pool_w1(pool, 0)
            pool_w1(pool, 1)
            pool_w2(pool)
            store_uq(0)
            pool_w1(pool, 2)
            pool_rope_start(pool)
            store_uq(1)
            pool_w1(pool, 3)
            store_uq(2)
            pool_w1(pool, 4)
            pool_w1(pool, 5)
            store_ukv(0)
            pool_w1(pool, 6)
            store_ukv(1)
            pool_w1(pool, 7)
            pool.wait_ge(kr_in, 96)
            pool.wait_ge(rope_t, 9)
            pool_turn(pool, 0)
            pool_sum(pool, krS, 0)
            pool_sum(pool, krS, 1)
            store_ukv(2)
            store_ukv(3)
            pool.wait_ge(rope_ok, 2)
            pool.wait_ge(w1_used, 8)
            pool.wait_ge(stored, 16 * count["stored"])
            pool_cmp_out(pool)
            pool_att(pool, MLA, mla_load)
            pool.wait_ge(MLA.fin, MLA.done)
            pool.dma_start(gateL, yO[6720:6744, :]).then_inc(glog_in, 16)
            pool_att(pool, NSA, nsa_load)
            pool.wait_ge(NSA.fin, NSA.done)
            pool_att(pool, MEM1, mem1_load)
            pool.wait_ge(MEM1.fin, MEM1.done)
            for t in range(TT):
                pool.dma_start(hrows[:, t, :], h1D[t * P:(t + 1) * P, :]).then_inc(rows_in[t], 16)
            pool.dma_start(gfS, a["final_norm_g"].rearrange("(a d) -> a d", a=1).broadcast_to([P, D])).then_inc(gf_in, 16)
            for t in range(TT):
                pool.wait_ge(fin_ok, t + 1)
                pool.dma_start(out[t * P:(t + 1) * P, :], hrows[:, t, :]).then_inc(out_sem, 16)
            pool.wait_ge(out_sem, 64)

        @block.scalar
        def _(act):
            act_norm(act, NORMS[0])
            pend = lambda: None
            for n_, j in enumerate(plan[:4]):
                act_chunk(act, j, 0, pend)
                pend = lambda j=j: act_evac(act, j, 0)
                if n_ == 0:
                    act_prep_sin(act)
            pend()
            act_norm(act, NORMS[1])
            act_chunk(act, E1, 0, lambda: None)
            act_chunk(act, E1, 1, lambda: act_evac(act, E1, 0), lambda s: act_prep(act, s))
            act.wait_ge(init, 3)

            act_chunk(act, E1, 2, lambda: act_evac(act, E1, 1), act_s5(act, 0))
            with act.Fori(1, 7) as m:
                act_chunk(act, E1, m + S5C, lambda: act_evac(act, E1, m + (S5C - 1)), act_s5(act, m))
            for m in (7, 8):
                act_chunk(act, E1, m + S5C, lambda: act_evac(act, E1, m + (S5C - 1)), act_s5(act, m))
            act_chunk(act, E1, 11, lambda: act_evac(act, E1, 10, ACT.Silu))
            act_chunk(act, E1, 12, lambda: act_evac(act, E1, 11, ACT.Silu))
            act_chunk(act, E1, 13, lambda: act_evac(act, E1, 12), lambda s: act_z(act, s))
            act_chunk(act, E2, 0, lambda: act_evac(act, E1, 13, ACT.Silu))
            act_chunk(act, GLU, 0, lambda: act_evac(act, E2, 0))
            act_chunk(act, GLU, 1, lambda: act_glu(act, 0))
            act_glu(act, 1)
            act_forget(act)
            act_att(act, FOX)
            act_att(act, MEM0)
            for c in range(4):
                act_chunk(act, OUT0, c, lambda: None)
            act_norm(act, NORMS[2])
            act_chunk(act, O1, 0, lambda: None)
            act_chunk(act, O1, 1, lambda: act_evac(act, O1, 0), act_t5_hook(act, 1, True))
            with act.Fori(2, 9) as c:
                act_chunk(act, O1, c, lambda: act_evac(act, O1, c - 1), act_t5_hook(act, c, False))
            with act.Fori(9, 12) as c:
                act_chunk(act, O1, c, lambda: act_evac(act, O1, c - 1, ACT.Silu), act_t5_hook(act, c, False))
            act_chunk(act, O1, 12, lambda: act_evac(act, O1, 11, ACT.Silu), lambda s: act_c(act, s))
            act_c_root(act)
            act_chunk(act, O2, 0, lambda: act_evac(act, O1, 12, ACT.Silu))
            act_chunk(act, UQ, 0, lambda: act_evac(act, O2, 0))
            for c in range(1, 3):
                act_chunk(act, UQ, c, lambda: act_evac(act, UQ, c - 1))
            act_chunk(act, UKV, 0, lambda: act_evac(act, UQ, 2))
            act_rope(act)
            for c in range(1, 4):
                act_chunk(act, UKV, c, lambda: act_evac(act, UKV, c - 1))
            act_evac(act, UKV, 3)
            act_c2(act)
            act_att(act, MLA)
            act_nsa_gates(act)
            act_att(act, NSA)
            act_att(act, MEM1)
            for c in range(4):
                act_chunk(act, OUT1, c, lambda: None)
            act_norm(act, NORMS[3])

        @block.tensor
        def _(pe):
            pe.wait_ge(ident_ok, 6)
            pe_norm(pe, NORMS[0])
            pe.wait_ge(nt_lo, KD)
            for j in plan[:4]:
                pe_chunk(pe, j, 0)
            pe_norm(pe, NORMS[1])
            pe.wait_ge(nt_lo, 2 * KD)
            pe_chunk(pe, E1, 0)
            pe_chunk(pe, E1, 1, lambda s: pe_prep(pe, s))
            pe_chunk(pe, E1, 2, pe_s5(pe, 0))
            with pe.Fori(1, 7) as m:
                pe_chunk(pe, E1, m + S5C, pe_s5(pe, m))
            for m in (7, 8):
                pe_chunk(pe, E1, m + S5C, pe_s5(pe, m))
            with pe.Fori(11, E1["chunks"]) as c:
                pe_chunk(pe, E1, c)
            pe_chunk(pe, E2, 0)
            pe.wait_ge(zlo_ok, 8)
            pe_chunk(pe, GLU, 0)
            pe_chunk(pe, GLU, 1)
            pe.wait_ge(banks_free, GLU["bank0"] + 8)
            pe_att(pe, FOX)
            pe_att(pe, MEM0)
            pe.wait_ge(MEM0.fin, MEM0.done)
            for c in range(4):
                pe_chunk(pe, OUT0, c)
            pe_norm(pe, NORMS[2])
            pe.wait_ge(nt_lo, 3 * KD)
            pe_chunk(pe, O1, 0)
            with pe.Fori(1, 12) as c:
                pe_chunk(pe, O1, c)
            pe_chunk(pe, O1, 12, lambda s: pe_c(pe, s))
            pe_chunk(pe, O2, 0)
            pe.wait_ge(cn_ok, 4)
            for c in range(3):
                pe_chunk(pe, UQ, c, lambda s: pe_w1(pe, 2 * c + s))
            pe.wait_ge(cn_ok, 8)
            for c in range(4):
                pe_chunk(pe, UKV, c, lambda s: pe_w1(pe, 6 + 2 * c + s))
            pe_c2(pe)
            pe.wait_ge(banks_free, OUT1["bank0"])
            pe.wait_ge(cmp2_ok, 3)
            pe_att(pe, MLA)
            pe.wait_ge(MLA.fin, MLA.done)
            pe_nsa_gates(pe)
            pe.wait_ge(glog_ok, 1)
            pe_att(pe, NSA)
            pe_att(pe, MEM1)
            pe.wait_ge(MEM1.fin, MEM1.done)
            for c in range(4):
                pe_chunk(pe, OUT1, c)

        @block.vector
        def _(dve):
            dve_norm(dve, NORMS[0])
            for n_, j in enumerate(plan[:4]):
                dve_chunk(dve, j, 0)
                if n_ == 0:
                    dve_prep_den(dve)
            dve_norm(dve, NORMS[1])
            dve_chunk(dve, E1, 0)
            dve_chunk(dve, E1, 1)
            dve.wait_ge(init, 3)
            dve_chunk(dve, E1, 2, dve_s5(dve, 0))
            with dve.Fori(1, 7) as m:
                dve_chunk(dve, E1, m + S5C, dve_s5(dve, m))
            for m in (7, 8):
                dve_chunk(dve, E1, m + S5C, dve_s5(dve, m))
            with dve.Fori(11, E1["chunks"]) as c:
                dve_chunk(dve, E1, c)
            dve_chunk(dve, E2, 0)
            dve_z(dve)
            dve_chunk(dve, GLU, 0)
            dve_glu(dve, 0)
            dve_chunk(dve, GLU, 1)
            dve_glu(dve, 1)
            dve_forget(dve)
            dve_att(dve, FOX)
            dve_att(dve, MEM0)
            for c in range(4):
                dve_chunk(dve, OUT0, c)
                dve_out(dve, OUT0, c, 16)
            dve_norm(dve, NORMS[2])
            dve_chunk(dve, O1, 0)
            dve_t5_start(dve)
            dve_chunk(dve, O1, 1, dve_t5_hook(dve, 1, True))
            with dve.Fori(2, 12) as c:
                dve_chunk(dve, O1, c, dve_t5_hook(dve, c, False))
            dve_chunk(dve, O1, 12, lambda s: dve_t5_end(dve, s) if s < 4 else None)
            dve_c(dve)
            dve_chunk(dve, O2, 0, lambda s: dve_cn(dve, 0) if s == 2 else dve_cn(dve, 1) if s == 6 else None)
            dve_cn_low(dve, 0)
            dve_chunk(dve, UQ, 0)
            dve_cn_low(dve, 1)
            dve_chunk(dve, UQ, 1)
            dve_x(dve)
            dve_chunk(dve, UQ, 2)
            dve_rope(dve)
            for c in range(4):
                dve_chunk(dve, UKV, c)
                if c == 1:
                    dve_rope_sign(dve)
            dve_c2(dve)
            dve_att(dve, MLA)
            for r in range(4):
                nc.vector.memset(NSA.p[r], 0.0).then_inc(p_zero, 1)
            dve.wait_ge(glog_ok, 1)
            nc.vector.tensor_tensor(gtmS[:, 0, 0:24:3], gtmS[:, 0, 0:24:3], cm01[:, 0, 0:1].broadcast_to([P, 8]), ALU.mult).then_inc(p_zero, 1)
            dve.wait_ge(p_zero, 5)
            dve_att(dve, NSA)
            dve_att(dve, MEM1)
            for c in range(4):
                dve_chunk(dve, OUT1, c)
                dve_out(dve, OUT1, c, 32)
            dve_final(dve)


_INS = ["x", "mem", "positions", "norm_g", "mem_norm_g", "final_norm_g", "t5_table", "w_out", "mem_w_kv", "even_w_in",
        "s5_lam_re", "s5_lam_im", "s5_log_dt", "s5_b_re", "s5_b_im", "s5_c_re", "s5_c_im", "s5_d", "s5_w_glu", "fox_b_f",
        "odd_w_in", "mla_g_cq", "mla_g_ckv", "mla_w_uq", "mla_w_ukv", "nsa_cmp_pe", "nsa_cmp_w1", "nsa_cmp_w2"]


def kernel(**inputs):
    import concourse.bacc as _bacc
    from concourse.bass_utils import run_bass_kernel_spmd as _run

    nc = _bacc.Bacc("TRN2", target_bir_lowering=False, num_devices=1)
    arrays, aps = {}, {}
    for name, v in [(n, inputs[n]) for n in _INS] + list(const_inputs().items()):
        v = np.ascontiguousarray(v)
        arrays[f"in_{name}_dram"] = v
        aps[name] = nc.dram_tensor(f"in_{name}_dram", v.shape, mybir.dt.from_np(v.dtype), kind="ExternalInput").ap()
    aps["out"] = nc.dram_tensor("out_0_dram", (1, T, D), F32, kind="ExternalOutput").ap()
    build(nc, aps)
    r = _run(nc, [arrays], core_ids=[0])
    return r.results[0]["out_0_dram"]
```
